# Optimizing a Trainium2 kernel written in Bass

```python
import jax, jax.numpy as jnp
from jax import lax
import numpy as np

D_MODEL = 1024
BATCH = 1
SEQ = 256
DEPTH = 1

D_PLE = 256
HEAD_DIM = 64
ROPE_DIM = HEAD_DIM // 4
ROPE_THETA = 500000.0
N_HEADS_A = 8
N_HEADS_B = 8
WIDTH_A = N_HEADS_A * HEAD_DIM
WIDTH_B = N_HEADS_B * HEAD_DIM
N_IDX_HEADS = 8
IDX_DIM = 64
TOPK_MAX = 256
Q_BLOCK = 128
EPS = 1e-6
NEG = -1e30

SPLITS = (WIDTH_A, HEAD_DIM, HEAD_DIM, WIDTH_A,
          N_IDX_HEADS * IDX_DIM, IDX_DIM, N_IDX_HEADS,
          WIDTH_B, WIDTH_B, WIDTH_B, N_HEADS_B, WIDTH_B)
D_IN = sum(SPLITS)


def _offsets():
    offs, acc = [], 0
    for w in SPLITS[:-1]:
        acc += w
        offs.append(acc)
    return offs

def rmsnorm(x, g):
    xf = x.astype(jnp.float32)
    y = xf * lax.rsqrt(jnp.mean(xf * xf, axis=-1, keepdims=True) + EPS) * g.astype(jnp.float32)
    return y.astype(x.dtype)

def partial_rope(x, pos):
    half = ROPE_DIM // 2
    freqs = ROPE_THETA ** (-jnp.arange(half, dtype=jnp.float32) / half)
    ang = pos.astype(jnp.float32)[:, None] * freqs[None, :]
    cos = jnp.cos(ang)[None, :, None, :]
    sin = jnp.sin(ang)[None, :, None, :]
    x1 = x[..., :half].astype(jnp.float32)
    x2 = x[..., half:ROPE_DIM].astype(jnp.float32)
    rot = jnp.concatenate([x1 * cos - x2 * sin, x2 * cos + x1 * sin], axis=-1).astype(x.dtype)
    return jnp.concatenate([rot, x[..., ROPE_DIM:]], axis=-1)

def to_blocks(t):
    B, S = t.shape[:2]
    t = t.reshape((B, S // Q_BLOCK, Q_BLOCK) + t.shape[2:])
    return jnp.moveaxis(t, 1, 0)

def from_blocks(t):
    t = jnp.moveaxis(t, 0, 1)
    return t.reshape((t.shape[0], t.shape[1] * t.shape[2]) + t.shape[3:])

def dsa_branch(qa, ka, va, qi, ki, wi):
    B, S = ka.shape[:2]
    topk = min(TOPK_MAX, S // 4)
    nb = S // Q_BLOCK
    key_pos = jnp.arange(S)
    scale = HEAD_DIM ** -0.5

    def block(args):
        blk, q_blk, qi_blk, wi_blk = args
        q_pos = blk * Q_BLOCK + jnp.arange(Q_BLOCK)
        causal = key_pos[None, :] <= q_pos[:, None]
        dots = jnp.einsum('bqhd,bsd->bqhs', qi_blk, ki)
        score = jnp.einsum('bqhs,bqh->bqs', jax.nn.relu(dots).astype(jnp.float32),
                           wi_blk.astype(jnp.float32))
        score = jnp.where(causal[None], score, -jnp.inf)
        _, sel = lax.top_k(score, topk)
        k_sel = jax.vmap(lambda k, i: k[i])(ka, sel)
        v_sel = jax.vmap(lambda v, i: v[i])(va, sel)
        logits = jnp.einsum('bqhd,bqkd->bhqk', q_blk, k_sel).astype(jnp.float32) * scale
        valid = sel <= q_pos[None, :, None]
        logits = jnp.where(valid[:, None], logits, NEG)
        probs = jax.nn.softmax(logits, axis=-1).astype(v_sel.dtype)
        return jnp.einsum('bhqk,bqkd->bqhd', probs, v_sel)

    out = lax.map(block, (jnp.arange(nb), to_blocks(qa), to_blocks(qi), to_blocks(wi)))
    return from_blocks(out)

def fox_branch(qb, kb, vb, log_f):
    B, S = qb.shape[:2]
    nb = S // Q_BLOCK
    key_pos = jnp.arange(S)
    scale = HEAD_DIM ** -0.5
    c = jnp.cumsum(log_f, axis=1)
    c_k = jnp.transpose(c, (0, 2, 1))

    def block(args):
        blk, q_blk, cq_blk = args
        q_pos = blk * Q_BLOCK + jnp.arange(Q_BLOCK)
        causal = key_pos[None, :] <= q_pos[:, None]
        logits = jnp.einsum('bqhd,bshd->bhqs', q_blk, kb).astype(jnp.float32) * scale
        logits = logits + jnp.transpose(cq_blk, (0, 2, 1))[..., None] - c_k[:, :, None, :]
        logits = jnp.where(causal[None, None], logits, NEG)
        probs = jax.nn.softmax(logits, axis=-1).astype(vb.dtype)
        return jnp.einsum('bhqs,bshd->bqhd', probs, vb)

    out = lax.map(block, (jnp.arange(nb), to_blocks(qb), to_blocks(c)))
    return from_blocks(out)

def first_inputs(seed: int = 0) -> dict:
    key = jax.random.key(seed)
    ks = jax.random.split(key, 14)
    f32 = jnp.float32
    nrm = lambda k, shape, fan_in: jax.random.normal(k, shape, f32) * (fan_in ** -0.5)
    x = jax.random.normal(ks[0], (BATCH, SEQ, D_MODEL), f32)
    p = jax.random.normal(ks[1], (DEPTH, BATCH, SEQ, D_PLE), f32)
    w_in = nrm(ks[2], (DEPTH, D_MODEL, D_IN), D_MODEL)
    b_forget = jax.random.uniform(ks[3], (DEPTH, N_HEADS_B), f32, 1.0, 5.0)
    w_branch_a = nrm(ks[4], (DEPTH, WIDTH_A, D_MODEL), WIDTH_A)
    w_branch_b = nrm(ks[5], (DEPTH, WIDTH_B, D_MODEL), WIDTH_B)
    w_merge = nrm(ks[6], (DEPTH, D_MODEL, 2 * D_MODEL), D_MODEL)
    w_out = nrm(ks[7], (DEPTH, D_MODEL, D_MODEL), D_MODEL)
    g_pre = 1.0 + 0.02 * jax.random.normal(ks[8], (DEPTH, D_MODEL), f32)
    g_post = 1.0 + 0.02 * jax.random.normal(ks[9], (DEPTH, D_MODEL), f32)
    w_ple = nrm(ks[10], (DEPTH, D_PLE, D_MODEL), D_PLE)
    w_ple_gate = nrm(ks[11], (DEPTH, D_MODEL, D_MODEL), D_MODEL)
    g_ple = 1.0 + 0.02 * jax.random.normal(ks[12], (DEPTH, D_MODEL), f32)
    return {"x": x, "p": p, "w_in": w_in, "b_forget": b_forget,
            "w_branch_a": w_branch_a, "w_branch_b": w_branch_b, "w_merge": w_merge,
            "w_out": w_out, "g_pre": g_pre, "g_post": g_post, "w_ple": w_ple,
            "w_ple_gate": w_ple_gate, "g_ple": g_ple}

def first_block(x, p, w_in, b_forget, w_branch_a, w_branch_b, w_merge, w_out,
              g_pre, g_post, w_ple, w_ple_gate, g_ple):
    B, S, _ = x.shape
    pos = jnp.arange(S)
    offs = _offsets()
    idx_scale = (N_IDX_HEADS ** -0.5) * (IDX_DIM ** -0.5)
    for i in range(DEPTH):
        h = rmsnorm(x, g_pre[i])
        proj = h @ w_in[i]
        (qa, ka, va, gate_a, qi, ki, wi, qb, kb, vb, fb, gate_b) = jnp.split(proj, offs, axis=-1)

        qa = partial_rope(qa.reshape(B, S, N_HEADS_A, HEAD_DIM), pos)
        ka = partial_rope(ka.reshape(B, S, 1, HEAD_DIM), pos).reshape(B, S, HEAD_DIM)
        qi = partial_rope(qi.reshape(B, S, N_IDX_HEADS, IDX_DIM), pos)
        ki = partial_rope(ki.reshape(B, S, 1, IDX_DIM), pos).reshape(B, S, IDX_DIM)
        wi = wi * idx_scale
        att_a = dsa_branch(qa, ka, va, qi, ki, wi).reshape(B, S, WIDTH_A)
        y_a = (att_a * jax.nn.silu(gate_a)) @ w_branch_a[i]

        log_f = jax.nn.log_sigmoid(fb.astype(jnp.float32) + b_forget[i].astype(jnp.float32))
        att_b = fox_branch(qb.reshape(B, S, N_HEADS_B, HEAD_DIM),
                           kb.reshape(B, S, N_HEADS_B, HEAD_DIM),
                           vb.reshape(B, S, N_HEADS_B, HEAD_DIM), log_f).reshape(B, S, WIDTH_B)
        y_b = (att_b * jax.nn.silu(gate_b)) @ w_branch_b[i]

        m_a, m_b = jnp.split(jax.nn.sigmoid(h @ w_merge[i]), 2, axis=-1)
        out = (m_a * y_a + m_b * y_b) @ w_out[i]
        x = x + rmsnorm(out, g_post[i])

        e = p[i] @ w_ple[i]
        gate = jax.nn.sigmoid(x @ w_ple_gate[i])
        x = x + rmsnorm(gate * e, g_ple[i])
    return x


DEPTH_2 = 2

N_MIXERS = 2
MEM_LEN = 256
MEM_HEADS = 4
MEM_WIDTH = MEM_HEADS * HEAD_DIM
TOK_WIDTH = D_MODEL - MEM_WIDTH
MOBA_HEADS = TOK_WIDTH // HEAD_DIM
MOBA_BLOCK = 256
MOBA_TOPK = 3
Q_CHUNK = 128
POOL_WINDOWS = (2, 4, 8, 16)
POOL_GROUPS = len(POOL_WINDOWS)
POOL_GROUP_WIDTH = TOK_WIDTH // POOL_GROUPS
D_FF = 4 * D_MODEL
ROPE_THETA_2 = 10000.0
NEG_2 = -1e30
N_POOL_LAYERS = (DEPTH_2 + 1) // 2
N_MOBA_LAYERS = DEPTH_2 // 2


def rms_norm(x, g):
    xf = x.astype(jnp.float32)
    y = xf * lax.rsqrt(jnp.mean(xf * xf, axis=-1, keepdims=True) + EPS)
    return (y * g.astype(jnp.float32)).astype(x.dtype)

def rope_tables(seq_len):
    pos = jnp.arange(seq_len, dtype=jnp.float32)
    inv = ROPE_THETA_2 ** (-jnp.arange(0, HEAD_DIM, 2, dtype=jnp.float32) / HEAD_DIM)
    ang = pos[:, None] * inv[None, :]
    return jnp.cos(ang), jnp.sin(ang)

def apply_rope(x, cos, sin):
    x1, x2 = jnp.split(x, 2, axis=-1)
    c = cos.astype(x.dtype)
    s = sin.astype(x.dtype)
    return jnp.concatenate([x1 * c - x2 * s, x2 * c + x1 * s], axis=-1)

def causal_window_mean(u, w):
    S = u.shape[1]
    c = jnp.cumsum(u.astype(jnp.float32), axis=1)
    c = jnp.pad(c, ((0, 0), (1, 0), (0, 0)))
    hi = c[:, 1:]
    lo = jnp.pad(c[:, :S + 1 - w], ((0, 0), (w - 1, 0), (0, 0)))
    cnt = jnp.minimum(jnp.arange(S) + 1, w).astype(jnp.float32)[None, :, None]
    return (hi - lo) / cnt

def pool_mixer(u, w_group, scale):
    B, S, _ = u.shape
    ug = u.reshape(B, S, POOL_GROUPS, POOL_GROUP_WIDTH)
    pooled = jnp.stack([causal_window_mean(ug[:, :, g], w) for g, w in enumerate(POOL_WINDOWS)], axis=2)
    d = (pooled - ug.astype(jnp.float32)).astype(u.dtype)
    y = jnp.einsum('bsgc,gcd->bsgd', d, w_group)
    return y.reshape(B, S, TOK_WIDTH) * scale

def moba_mixer(qkv, q_gain, k_gain, cos, sin):
    B, S, _ = qkv.shape
    q, k, v = jnp.split(qkv, 3, axis=-1)

    def heads(t):
        return t.reshape(B, S, MOBA_HEADS, HEAD_DIM).transpose(0, 2, 1, 3)

    q = apply_rope(rms_norm(heads(q), q_gain), cos, sin)
    k = apply_rope(rms_norm(heads(k), k_gain), cos, sin)
    v = heads(v)
    H = MOBA_HEADS
    nb = -(-S // MOBA_BLOCK)
    pad = nb * MOBA_BLOCK - S
    kb = jnp.pad(k, ((0, 0), (0, 0), (0, pad), (0, 0))).reshape(B, H, nb, MOBA_BLOCK, HEAD_DIM)
    vb = jnp.pad(v, ((0, 0), (0, 0), (0, pad), (0, 0))).reshape(B, H, nb, MOBA_BLOCK, HEAD_DIM)
    k_mean = jnp.mean(kb.astype(jnp.float32), axis=3)
    topk = min(MOBA_TOPK, nb)
    n_chunks = S // Q_CHUNK
    scale = HEAD_DIM ** -0.5
    bi = jnp.arange(B)[:, None, None, None]
    hi = jnp.arange(H)[None, :, None, None]
    block_ids = jnp.arange(nb)
    key_off = jnp.arange(MOBA_BLOCK)
    q_off = jnp.arange(Q_CHUNK)

    def chunk(ci):
        q0 = ci * Q_CHUNK
        own = q0 // MOBA_BLOCK
        qc = lax.dynamic_slice_in_dim(q, q0, Q_CHUNK, axis=2)
        g = jnp.einsum('bhcd,bhnd->bhcn', qc.astype(jnp.float32), k_mean)
        g = jnp.where(block_ids < own, g, -jnp.inf)
        _, idx = lax.top_k(g, topk)
        valid = idx < own
        k_sel = kb[bi, hi, idx]
        v_sel = vb[bi, hi, idx]
        s_sel = jnp.einsum('bhcd,bhcjkd->bhcjk', qc, k_sel).astype(jnp.float32) * scale
        s_sel = jnp.where(valid[..., None], s_sel, NEG_2)
        k_own = lax.dynamic_index_in_dim(kb, own, axis=2, keepdims=False)
        v_own = lax.dynamic_index_in_dim(vb, own, axis=2, keepdims=False)
        s_own = jnp.einsum('bhcd,bhkd->bhck', qc, k_own).astype(jnp.float32) * scale
        qpos = q0 + q_off
        kpos = own * MOBA_BLOCK + key_off
        s_own = jnp.where(kpos[None, :] <= qpos[:, None], s_own, NEG_2)
        s = jnp.concatenate([s_sel.reshape(B, H, Q_CHUNK, topk * MOBA_BLOCK), s_own], axis=-1)
        p = jax.nn.softmax(s, axis=-1).astype(v.dtype)
        p_sel = p[..., :topk * MOBA_BLOCK].reshape(B, H, Q_CHUNK, topk, MOBA_BLOCK)
        p_own = p[..., topk * MOBA_BLOCK:]
        return (jnp.einsum('bhcjk,bhcjkd->bhcd', p_sel, v_sel)
                + jnp.einsum('bhck,bhkd->bhcd', p_own, v_own))

    out = lax.map(chunk, jnp.arange(n_chunks))
    out = jnp.transpose(out, (1, 2, 0, 3, 4)).reshape(B, H, S, HEAD_DIM)
    return out.transpose(0, 2, 1, 3).reshape(B, S, TOK_WIDTH)

def mem_cross_attention(qm, mem_n, w_mem_kv, q_gain, k_gain):
    B, S, _ = qm.shape
    M = mem_n.shape[1]
    k, v = jnp.split(mem_n @ w_mem_kv, 2, axis=-1)
    q = rms_norm(qm.reshape(B, S, MEM_HEADS, HEAD_DIM), q_gain)
    k = rms_norm(k.reshape(B, M, MEM_HEADS, HEAD_DIM), k_gain)
    v = v.reshape(B, M, MEM_HEADS, HEAD_DIM)
    s = jnp.einsum('bshd,bmhd->bhsm', q, k).astype(jnp.float32) * (HEAD_DIM ** -0.5)
    p = jax.nn.softmax(s, axis=-1).astype(v.dtype)
    o = jnp.einsum('bhsm,bmhd->bshd', p, v)
    return o.reshape(B, S, MEM_WIDTH)

def second_inputs(seed: int = 0) -> dict:
    key = jax.random.key(seed)
    ks = jax.random.split(key, 20)
    f32 = jnp.float32

    def w(k, shape, fan_in):
        return jax.random.normal(k, shape, f32) * (fan_in ** -0.5)

    def gain(k, shape):
        return 1.0 + 0.1 * jax.random.normal(k, shape, f32)

    return {
        "x": jax.random.normal(ks[0], (BATCH, SEQ, D_MODEL), f32),
        "mem": jax.random.normal(ks[1], (BATCH, MEM_LEN, D_MODEL), f32),
        "g_mix": gain(ks[2], (DEPTH_2, D_MODEL)),
        "g_mem": gain(ks[3], (DEPTH_2, D_MODEL)),
        "g_mlp": gain(ks[4], (DEPTH_2, D_MODEL)),
        "w_in_pool": w(ks[5], (N_POOL_LAYERS, D_MODEL, TOK_WIDTH + MEM_WIDTH), D_MODEL),
        "w_pool_group": w(ks[6], (N_POOL_LAYERS, POOL_GROUPS, POOL_GROUP_WIDTH, POOL_GROUP_WIDTH), POOL_GROUP_WIDTH),
        "pool_scale": gain(ks[7], (N_POOL_LAYERS, TOK_WIDTH)),
        "w_in_moba": w(ks[8], (N_MOBA_LAYERS, D_MODEL, 3 * TOK_WIDTH + MEM_WIDTH), D_MODEL),
        "moba_q_gain": gain(ks[9], (N_MOBA_LAYERS, HEAD_DIM)),
        "moba_k_gain": gain(ks[10], (N_MOBA_LAYERS, HEAD_DIM)),
        "w_mem_kv": w(ks[11], (DEPTH_2, D_MODEL, 2 * MEM_WIDTH), D_MODEL),
        "mem_q_gain": gain(ks[12], (DEPTH_2, HEAD_DIM)),
        "mem_k_gain": gain(ks[13], (DEPTH_2, HEAD_DIM)),
        "w_out": w(ks[14], (DEPTH_2, TOK_WIDTH + MEM_WIDTH, D_MODEL), TOK_WIDTH + MEM_WIDTH),
        "w_ff1": w(ks[15], (DEPTH_2, D_MODEL, D_FF), D_MODEL),
        "w_ff2": w(ks[16], (DEPTH_2, D_FF, D_MODEL), D_FF),
    }

def second_block(x, mem, g_mix, g_mem, g_mlp, w_in_pool, w_pool_group, pool_scale,
              w_in_moba, moba_q_gain, moba_k_gain, w_mem_kv, mem_q_gain, mem_k_gain,
              w_out, w_ff1, w_ff2):
    S = x.shape[1]
    cos, sin = rope_tables(S)
    for i in range(DEPTH_2):
        j = i // N_MIXERS
        u = rms_norm(x, g_mix[i])
        mem_n = rms_norm(mem, g_mem[i])
        if i % N_MIXERS == 0:
            h = u @ w_in_pool[j]
            tok = pool_mixer(h[..., :TOK_WIDTH], w_pool_group[j], pool_scale[j])
            qm = h[..., TOK_WIDTH:]
        else:
            h = u @ w_in_moba[j]
            tok = moba_mixer(h[..., :3 * TOK_WIDTH], moba_q_gain[j], moba_k_gain[j], cos, sin)
            qm = h[..., 3 * TOK_WIDTH:]
        mo = mem_cross_attention(qm, mem_n, w_mem_kv[i], mem_q_gain[i], mem_k_gain[i])
        x = x + jnp.concatenate([tok, mo], axis=-1) @ w_out[i]
        u = rms_norm(x, g_mlp[i])
        x = x + jnp.square(jax.nn.relu(u @ w_ff1[i])) @ w_ff2[i]
    return x


def setup_inputs(seed=0):
    out = dict(first_inputs(seed))
    for name, value in second_inputs(seed + 1).items():
        if name != "x":
            out[name + "_2"] = value
    return out


def reference(
    x, p, w_in, b_forget, w_branch_a, w_branch_b, w_merge, w_out, g_pre, g_post, w_ple,
    w_ple_gate, g_ple, mem_2, g_mix_2, g_mem_2, g_mlp_2, w_in_pool_2, w_pool_group_2,
    pool_scale_2, w_in_moba_2, moba_q_gain_2, moba_k_gain_2, w_mem_kv_2, mem_q_gain_2,
    mem_k_gain_2, w_out_2, w_ff1_2, w_ff2_2,
):
    x = first_block(
        x, p, w_in, b_forget, w_branch_a, w_branch_b, w_merge, w_out, g_pre, g_post, w_ple,
        w_ple_gate, g_ple,
    )
    return second_block(
        x, mem_2, g_mix_2, g_mem_2, g_mlp_2, w_in_pool_2, w_pool_group_2, pool_scale_2,
        w_in_moba_2, moba_q_gain_2, moba_k_gain_2, w_mem_kv_2, mem_q_gain_2, mem_k_gain_2,
        w_out_2, w_ff1_2, w_ff2_2,
    )


_drawn_inputs = setup_inputs


def setup_inputs(seed=0):
    import zlib

    import numpy as np

    out = dict(_drawn_inputs(seed))
    spreads = {}
    factors = {'g_post': 4.299,
     'g_ple': 4.56,
     'g_mem_2': 8.0,
     'moba_q_gain_2': 8.0,
     'moba_k_gain_2': 8.0,
     'mem_q_gain_2': 8.0,
     'mem_k_gain_2': 8.0}
    for name, (base, spread) in spreads.items():
        noise = np.random.default_rng([zlib.crc32(name.encode()), seed]).standard_normal(out[name].shape)
        drawn = base * np.exp(spread * noise) if base else spread * noise
        out[name] = __import__('jax').numpy.asarray(drawn.astype(out[name].dtype))
    for name, factor in factors.items():
        out[name] = (out[name] * factor).astype(out[name].dtype)
    return out
```

```python
from contextlib import ExitStack

import numpy as np

import concourse.bass as bass
from concourse import mybir

ALU = mybir.AluOpType
ACT = mybir.ActivationFunctionType
AX = mybir.AxisListType
F32 = mybir.dt.float32
F32R = mybir.dt.float32r
BF16 = mybir.dt.bfloat16

P = 128
S = 256
NT = S // P
D = 1024
KT = D // P
HD = 64
WA = 512
DIN = 3792
NBLK_IN = 8
CIN = DIN // NBLK_IN
CB = 512
UNIT = 4 * CB
EPS = 1e-6
NEG = -1e30
TOPK = S // 4
SCALE = HD ** -0.5
IDX_SCALE = (8 ** -0.5) * (64 ** -0.5)
FILL = 1e8
TAKEN = -3.4e38
QA, KA, VA, GA, QI, KI, WI, QB, KB, VB, FB, GB = 0, 512, 576, 640, 1152, 1664, 1728, 1736, 2248, 2760, 3272, 3280
TOKW = 768
GW = TOKW // 4
GC = GW // 2
FF = 8
LOOK = 3
RAW = 2
RING = 4

U_IN = 0
U_MERGE = U_IN + 2 * NBLK_IN
U_KV = U_MERGE + 8
U_BR = U_KV + 4
U_WO = U_BR + 4
U_PLE = U_WO + 4
U_GATE = U_PLE + 1
U_POOL = U_GATE + 4
U_OUT0 = U_POOL + 4
U_FF0 = U_OUT0 + 4
U_MOBA = U_FF0 + 4 * FF
U_OUT1 = U_MOBA + 10
U_FF1 = U_OUT1 + 4
N_UNITS = U_FF1 + 4 * FF
N_SMALL = 22

HEADS = [("fox", j) for j in range(8)] + [("dsa", j) for j in range(8)] + [("mem0", j) for j in range(4)] \
    + [("moba", j) for j in range(12)] + [("mem1", j) for j in range(4)]
N_HEADS = len(HEADS)


def width0(h):
    return S if HEADS[h][0].startswith("mem") else P


RUN1 = [("idx", j) for j in range(8)] + list(range(16))
RUN2 = list(range(16, 20))
RUN3 = list(range(20, N_HEADS))


def pair_of(run, pr):
    first = run[2 * pr]
    return ("idx", first[1] // 2) if isinstance(first, tuple) else (HEADS[first][0], first // 2)


def parts_at(run, s):
    out = []
    n_pairs = len(run) // 2
    nxt = (s + 1) // 2 if s % 2 else s // 2 + 1
    if s < 0:
        nxt = 0
    if nxt < n_pairs:
        kind, pr = pair_of(run, nxt)
        before = pair_of(run, nxt - 1)[0] if nxt else ""
        if s < 0 or s % 2 == 0:
            out.append(("qi" if kind == "idx" else "q", pr))
        if s < 0 or s % 2:
            if kind == "idx":
                out += [("ki", 0)] if nxt == 0 else []
            elif kind == "dsa":
                out += [("ka", 0)] if before != "dsa" else []
            else:
                out.append(("k", pr))
    if s >= 2 and s % 2 == 0:
        kind, pr = pair_of(run, s // 2 - 1)
        if kind in ("fox", "dsa"):
            out.append(("gate", pr))
    return out


def run_steps(run):
    return range(-1, len(run) + 2)


PARTS = [part for run in (RUN1, RUN2, RUN3) for s in run_steps(run) for part in parts_at(run, s)]
PART = {part: n for n, part in enumerate(PARTS)}
PART_SLOT = {part: n % 2 for n, part in enumerate(q for q in PARTS if q[0] in ("qi", "q"))}
PART_SLOT.update({("k", pr): PART_SLOT[("q", pr)] for what, pr in PARTS if what == "k"})
GATES = [pr for what, pr in PARTS if what == "gate"]

BLOCKS = ["in"] * NBLK_IN + ["merge"] * 4 + ["kv"] * 2 + ["br"] * 4 + ["wo"] * 2 + ["ple"] * 2 + ["gate"] * 2 \
    + ["pool"] * 2 + ["out"] * 2 + ["moba"] * 5 + ["out"] * 2
READERS = {"in": "av", "merge": "a", "kv": "av", "br": "v", "wo": "v", "ple": "av", "gate": "a", "pool": "av",
           "out": "v", "moba": "av"}


def pair_bank(k):
    return 0 if B_MERGE <= k < B_BR else 2 * (k % 2)


def freed(k, engine):
    return 2 + sum(engine in READERS[b] for b in BLOCKS[:k + 1])


B_MERGE, B_KV, B_BR, B_WO, B_PLE, B_GATE, B_POOL, B_OUT0, B_MOBA, B_OUT1 = 8, 12, 14, 18, 20, 22, 24, 26, 28, 33


STEPS = 8 + 16 + 2


def after_step(n):
    if n < 0:
        return []
    if n < 8:
        return [("merge", n)]
    if n < 12:
        return [("group", 0, n - 8)]
    if n < 14:
        return [("kv", n - 12)]
    if n < 18:
        return [("group", 1, n - 14)]
    if n < 20:
        return [("kv", n - 16)]
    return []


G_H = 0
G_MEM = G_H + 4
G_MERGED = G_MEM + 8
G_P = G_MERGED + 4
G_X = G_P + 1
G_MIX0 = G_X + 4
G_TOK0 = G_MIX0 + 4
G_MLP0 = G_TOK0 + 3
G_FF0 = G_MLP0 + 4
G_MIX1 = G_FF0 + 2 * FF
G_MLP1 = G_MIX1 + 4
G_FF1 = G_MLP1 + 4


def build(nc, a, out):
    with ExitStack() as ctx:
        def sb(name, shape, dt=F32):
            return ctx.enter_context(nc.sbuf_tensor(name, shape, dt))

        def sem(name):
            return ctx.enter_context(nc.semaphore(name))

        raw = sb("raw", [P, RAW, UNIT])
        w_hi = sb("w_hi", [P, RING, UNIT], F32R)
        w_lo = sb("w_lo", [P, RING, UNIT], F32R)
        x = sb("x", [P, NT, D])
        tok = sb("tok", [P, NT, D])
        a_hi = sb("a_hi", [P, KT, S], F32R)
        a_lo = sb("a_lo", [P, KT, S], F32R)
        b_hi = sb("b_hi", [P, KT, S], F32R)
        b_lo = sb("b_lo", [P, KT, S], F32R)
        proj = sb("proj", [P, NT * DIN])
        m = sb("m", [P, NT * 2 * D])
        qk = sb("qk", [P, 2, 2, S])
        kT = sb("kT", [P, S])
        memkv = sb("memkv", [P, 2, NT, CB])
        ident = sb("ident", [P, P])
        ident_b = sb("ident_b", [P, P], BF16)
        mask = sb("mask", [P, P])
        mask_b = sb("mask_b", [P, P], BF16)
        tri = sb("tri", [P, S])
        rope_a = sb("rope_a", [P, 2, NT, 8])
        rope_m = sb("rope_m", [P, 2, NT, 32])
        gain_rows = sb("gain_rows", [56, P])
        gain_cols = sb("gain_cols", [P, 56])
        gain_bc = sb("gain_bc", [P, D])
        head_gain = sb("head_gain", [P, 6, HD])
        bias_f = sb("bias_f", [P, 8])
        prob = sb("prob", [P, 2, 2 * S])
        probT = sb("probT", [P, 2, 2 * S])
        top8 = sb("top8", [P, NT, 8])
        sel_b = sb("sel_b", [P, P + S], BF16)
        wis = sb("wis", [P, NT, 8])
        fgt = sb("fgt", [P, 6, NT, 8])
        mx = sb("mx", [P, N_HEADS, NT])
        nmx = sb("nmx", [P, N_HEADS, NT])
        psums = sb("psums", [P, N_HEADS, NT])
        prec = sb("prec", [P, N_HEADS, NT])
        stat = sb("stat", [P, 3, 8, 2 * NT])
        hstat = sb("hstat", [P, 2, 5, NT * 12])
        half = sb("half", [P, NT * 12])

        bank = [ctx.enter_context(nc.psum_tensor(f"bank{i}", [P, 512], F32)) for i in range(8)]
        b_t, b_io, b_s, b_v, b_tr = bank[2], bank[3], bank[4:6], bank[7], bank[6:8]

        def group_bank(g):
            return b_tr[0 if G_MEM <= g < G_MERGED else g % 2]

        pj = proj[:].rearrange("p (t n) -> p t n", t=NT)
        xf = x[:].rearrange("p t n -> p (t n)")
        score, gate_s, gated, cT = xf[:, 0:P + S], xf[:, 384:640], xf[:, 640:896], xf[0:8, 896:1152]
        rope_t = xf[:, 1152:1728].rearrange("p (q t n d) -> p q t n d", q=4, t=NT, n=9)
        k_twice = xf[:, 1728:1984].rearrange("p (t q d) -> p t q d", t=NT, q=2)
        memk_tmp, memq_tmp = xf[:, 1152:1664], m[:, 4 * D - NT * S:4 * D]
        m_sig = m[:].rearrange("p (t n) -> p t n", t=NT)
        e_tok = m[:, 0:NT * D].rearrange("p (t n) -> p t n", t=NT)
        m_junk = m[:, NT * D:].rearrange("p (t n) -> p t n", t=NT)
        band = m[:, 0:NT * 4 * S].rearrange("p (t g n) -> p t g n", t=NT, g=4)
        w_group = m[0:GC, NT * 4 * S:NT * 4 * S + 8 * GW].rearrange("p (g c n) -> p g c n", g=4, c=2)
        h_pool = proj[:, 0:NT * D].rearrange("p (t n) -> p t n", t=NT)
        dT = proj[0:GC, NT * D:NT * D + 8 * S].rearrange("p (g c n) -> p g c n", g=4, c=2)
        h_moba = proj[:, 0:NT * 2560].rearrange("p (t n) -> p t n", t=NT)
        hidden = tok[:, :, 0:CB]

        raw_landed = [sem(f"raw_landed{i}") for i in range(RAW)]
        hi_ready, lo_ready, unit_used = sem("hi_ready"), sem("lo_ready"), sem("unit_used")
        free_a, free_v = sem("banks_free_a"), sem("banks_free_v")
        tr_ready, tr_hi, tr_lo = sem("tr_ready"), sem("tr_hi"), sem("tr_lo")
        x_landed, const_landed, mem_landed, p_landed, bc_landed = (sem(n) for n in (
            "x_landed", "const_landed", "mem_landed", "p_landed", "bc_landed"))
        pool_landed, x_again, out_landed = sem("pool_landed"), sem("x_again"), sem("out_landed")
        consts_made, gains_tr, gains_made = sem("consts_made"), sem("gains_tr"), sem("gains_made")
        sq_done, rstd_done, normed = sem("sq_done"), sem("rstd_done"), sem("normed")
        part_tr, part_cp, gate_cp, tanh_done = sem("part_tr"), sem("part_cp"), sem("gate_cp"), sem("tanh_done")
        idx_s, idx_relu, idx_acc, sel_made = sem("idx_s"), sem("idx_relu"), sem("idx_acc"), sem("sel_made")
        rope_idx, rope_dsa, wi_made = sem("rope_idx"), sem("rope_dsa"), sem("wi_made")
        f_abs, f_ln, f_log, c_ready, c_made = sem("f_abs"), sem("f_ln"), sem("f_log"), sem("c_ready"), sem("c_made")
        s_ready, max_done, exp_done, p_ready, pt_ready, pt_copied, pv_done, pair_read = (sem(n) for n in (
            "s_ready", "max_done", "exp_done", "p_ready", "pt_ready", "pt_copied", "pv_done", "pair_read"))
        pair_tmp, pair_hi, pair_lo = sem("pair_tmp"), sem("pair_hi"), sem("pair_lo")
        memk_made, memq_made, moba_q_made, moba_k_made = (sem(n) for n in (
            "memk_made", "memq_made", "moba_q_made", "moba_k_made"))
        merge_tanh, merge_sig, merged, x_post, gate_tanh, z_made, x_ple = (sem(n) for n in (
            "merge_tanh", "merge_sig", "merged", "x_post", "gate_tanh", "z_made", "x_ple"))
        ple_block, d_copied_a, d_copied_v = sem("ple_block"), sem("d_copied_a"), sem("d_copied_v")
        d_ready, y_ready, y_made, x_mix, x_mlp = (sem(n) for n in (
            "d_ready", "y_ready", "y_made", "x_mix", "x_mlp"))
        ff_relu, ff_sq, ff_done = sem("ff_relu"), sem("ff_sq"), sem("ff_done")
        head_sum, head_rs = sem("head_sum"), sem("head_rs")
        act_chain, vec_chain, pool_chain = sem("act_chain"), sem("vec_chain"), sem("pool_chain")

        class Linker:

            def __init__(self, eng, chain):
                self.eng, self.chain, self.n = eng, chain, 0

            def step(self):
                self.n += 1
                return self.chain, 1

            def wait(self):
                self.eng.wait_ge(self.chain, self.n)

            def __call__(self, ins):
                ins.then_inc(*self.step())
                self.wait()

        def head_cols(h):
            kind, j = HEADS[h]
            pr = j // 2
            h0 = pj[:, :, :]
            moba = proj[:, 0:NT * 2560].rearrange("p (t n) -> p t n", t=NT)
            pool = proj[:, 0:NT * D].rearrange("p (t n) -> p t n", t=NT)
            if kind == "fox":
                return dict(q=h0[:, :, QB + P * pr:QB + P * pr + P], k=h0[:, :, KB + P * pr:KB + P * pr + P],
                            gate=h0[:, :, GB + P * pr:GB + P * pr + P], v=h0[:, :, VB + HD * j:VB + HD * j + HD])
            if kind == "dsa":
                return dict(q=h0[:, :, QA + P * pr:QA + P * pr + P], gate=h0[:, :, GA + P * pr:GA + P * pr + P],
                            v=h0[:, :, VA:VA + HD])
            if kind == "moba":
                return dict(q=moba[:, :, P * pr:P * pr + P], k=moba[:, :, TOKW + P * pr:TOKW + P * pr + P],
                            v=moba[:, :, 2 * TOKW + HD * j:2 * TOKW + HD * j + HD])
            lay = int(kind[3])
            src = pool[:, :, TOKW:] if lay == 0 else moba[:, :, 3 * TOKW:]
            return dict(q=src[:, :, P * pr:P * pr + P], k=memkv[:, lay, :, P * pr:P * pr + P],
                        v=memkv[:, lay, :, S + HD * j:S + HD * j + HD])

        def pair_ktile(pr):
            kind, j = HEADS[2 * pr]
            return {"fox": 4, "dsa": 0, "mem0": 6, "moba": 0, "mem1": 6}[kind] + j // 2

        def unit_source(u):
            def cut(w, half_, c, n=CB):
                return w.rearrange("(k p) n -> p k n", p=P)[:, 4 * half_:4 * half_ + 4, c * n:c * n + n]
            if U_MERGE <= u < U_KV:
                return cut(a["w_merge"][0], u % 2, (u - U_MERGE) // 2)
            if U_KV <= u < U_BR:
                return cut(a["w_mem_kv_2"][(u - U_KV) // 2], u % 2, 0)
            if U_BR <= u < U_WO:
                return cut(a["w_branch_b" if (u - U_BR) % 2 else "w_branch_a"][0], 0, (u - U_BR) // 2)
            if U_WO <= u < U_PLE:
                return cut(a["w_out"][0], (u - U_WO) % 2, (u - U_WO) // 2)
            if u == U_PLE:
                return a["w_ple"][0].rearrange("(k p) n -> p k n", p=P)
            if U_GATE <= u < U_POOL:
                return cut(a["w_ple_gate"][0], (u - U_GATE) % 2, (u - U_GATE) // 2)
            if U_POOL <= u < U_OUT0:
                return cut(a["w_in_pool_2"][0], (u - U_POOL) % 2, (u - U_POOL) // 2)
            if U_OUT0 <= u < U_FF0:
                return cut(a["w_out_2"][0], (u - U_OUT0) % 2, (u - U_OUT0) // 2)
            if U_MOBA <= u < U_OUT1:
                return cut(a["w_in_moba_2"][0], (u - U_MOBA) % 2, (u - U_MOBA) // 2)
            if U_OUT1 <= u < U_FF1:
                return cut(a["w_out_2"][1], (u - U_OUT1) % 2, (u - U_OUT1) // 2)
            base, lay = (U_FF0, 0) if u < U_MOBA else (U_FF1, 1)
            r = u - base
            if r < 2:
                return cut(a["w_ff1_2"][lay], r, 0)
            i, r = divmod(r - 2, 4)
            if r < 2 and i < FF - 1:
                return cut(a["w_ff1_2"][lay], r, i + 1)
            return a["w_ff2_2"][lay].rearrange("(i k p) n -> p i k n", p=P, k=4)[:, i, :, (r % 2) * CB:(r % 2) * CB + CB]

        def unit_size(u):
            return 4 * CIN if u < U_MERGE else UNIT

        def head_squares(eng, link, v, n, slot, tmp):
            sq = tmp.rearrange("p (t n d) -> p t n d", t=NT, d=HD)
            link(eng.tensor_tensor(sq, v, v, ALU.mult))
            for w in (32, 16, 8, 4, 2, 1):
                link(eng.tensor_tensor(sq[:, :, :, 0:w], sq[:, :, :, 0:w], sq[:, :, :, w:2 * w], ALU.add))
            mean = hstat[:, slot, 0, 0:NT * n].rearrange("p (t n) -> p t n", t=NT)
            return eng.tensor_scalar(mean, sq[:, :, :, 0], 1.0 / HD, EPS, ALU.mult, ALU.add)

        def head_rstd(eng, n, slot):
            return eng.tensor_tensor(hstat[:, slot, 1, 0:NT * n], hstat[:, slot, 0, 0:NT * n], half[:, 0:NT * n], ALU.pow)

        def head_scale(eng, link, v, n, gain, slot):
            r = hstat[:, slot, 1, 0:NT * n].rearrange("p (t n) -> p t n", t=NT)
            for t in range(NT):
                eng.tensor_tensor(v[:, t], v[:, t], r[:, t].unsqueeze(2).to_broadcast([P, n, HD]), ALU.mult)\
                   .then_inc(*link.step())
            link.wait()
            for t in range(NT):
                eng.tensor_tensor(v[:, t], v[:, t], gain.unsqueeze(1).to_broadcast([P, n, HD]), ALU.mult)\
                   .then_inc(*link.step())
            link.wait()

        def rotate_heads(eng, link, v, n, tmp):
            old = tmp.rearrange("p (q t n d) -> p q t n d", q=2, t=NT, d=HD // 2)
            x1, x2 = v[:, :, :, 0:HD // 2], v[:, :, :, HD // 2:HD]
            for t in range(NT):
                cs, sn = (rope_m[:, q, t, :].unsqueeze(1).to_broadcast([P, n, HD // 2]) for q in range(2))
                eng.tensor_tensor(old[:, 0, t], x1[:, t], sn, ALU.mult).then_inc(*link.step())
                eng.tensor_tensor(old[:, 1, t], x2[:, t], sn, ALU.mult).then_inc(*link.step())
                link.wait()
                eng.tensor_tensor(x1[:, t], x1[:, t], cs, ALU.mult).then_inc(*link.step())
                eng.tensor_tensor(x2[:, t], x2[:, t], cs, ALU.mult).then_inc(*link.step())
                link.wait()
                eng.tensor_tensor(x1[:, t], x1[:, t], old[:, 1, t], ALU.subtract).then_inc(*link.step())
                eng.tensor_tensor(x2[:, t], x2[:, t], old[:, 0, t], ALU.add).then_inc(*link.step())
            link.wait()

        block = ctx.enter_context(nc.Block())

        @block.sync
        def _(sp):
            def load(u, slot, src, n):
                if not isinstance(u, int) or u >= RAW:
                    sp.wait_ge(lo_ready, u - RAW + 1)
                k = src.shape[1]
                dst = raw[:, slot, 0:n].rearrange("p (k n) -> p k n", k=k)
                sp.dma_start(dst, src).then_inc(raw_landed[slot], 16)

            for t in range(NT):
                sp.dma_start(x[:, t, :], a["x"][0, t * P:(t + 1) * P, :]).then_inc(x_landed, 16)
            w_in = a["w_in"][0].rearrange("(k p) n -> p k n", p=P)
            for u in range(2):
                load(u, u, w_in[:, 4 * u:4 * u + 4, 0:CIN], 4 * CIN)
            with sp.Fori(1, NBLK_IN) as b:
                for r in range(2):
                    load(2 * b + r, r, w_in[:, 4 * r:4 * r + 4, bass.ds(b * CIN, CIN)], 4 * CIN)

            def mlp(base, lay):
                w1 = a["w_ff1_2"][lay].rearrange("(k p) n -> p k n", p=P)
                w2 = a["w_ff2_2"][lay].rearrange("(i k p) n -> p i k n", p=P, k=4)
                for u in range(base, base + 2):
                    load(u, u % RAW, unit_source(u), UNIT)
                with sp.Fori(0, FF - 1) as i:
                    for r in range(2):
                        load(base + 2 + 4 * i + r, (base + r) % RAW,
                             w1[:, 4 * r:4 * r + 4, bass.ds(i * CB + CB, CB)], UNIT)
                    for r in range(2):
                        src = w2[:, bass.ds(i, 1), :, r * CB:r * CB + CB].rearrange("p i k n -> p (i k) n")
                        load(base + 4 + 4 * i + r, (base + r) % RAW, src, UNIT)
                for u in range(base + 4 * FF - 2, base + 4 * FF):
                    load(u, u % RAW, unit_source(u), UNIT)

            for u in range(U_MERGE, U_FF0):
                load(u, u % RAW, unit_source(u), UNIT)
            mlp(U_FF0, 0)
            for u in range(U_MOBA, U_FF1):
                load(u, u % RAW, unit_source(u), UNIT)
            mlp(U_FF1, 1)
            for t in range(NT):
                sp.wait_ge(x_mlp, NT + t + 1)
                sp.dma_start(out[0, t * P:(t + 1) * P, :], x[:, t, :]).then_inc(out_landed, 16)
            sp.wait_ge(out_landed, 16 * NT)

        @block.gpsimd
        def _(gp):
            link = Linker(gp, pool_chain)
            small = [(ident[:], a["c_ident"]), (mask[:], a["c_mask"]), (tri[:], a["c_tri"]),
                     (gain_rows[0:8, :], a["g_pre"][0].rearrange("(k p) -> k p", p=P)),
                     (gain_rows[8:24, :], a["g_mix_2"].rearrange("l (k p) -> (l k) p", p=P)),
                     (gain_rows[24:40, :], a["g_mem_2"].rearrange("l (k p) -> (l k) p", p=P)),
                     (gain_rows[40:56, :], a["g_mlp_2"].rearrange("l (k p) -> (l k) p", p=P)),
                     (bias_f[:], a["b_forget"][0].partition_broadcast(P)),
                     (head_gain[:, 0, :], a["moba_q_gain_2"][0].partition_broadcast(P)),
                     (head_gain[:, 1, :], a["moba_k_gain_2"][0].partition_broadcast(P))]
            small += [(rope_a[:, cs, t, :], a["c_rope_a"][cs, t * P:(t + 1) * P, :]) for cs in range(2) for t in range(NT)]
            small += [(rope_m[:, cs, t, :], a["c_rope_m"][cs, t * P:(t + 1) * P, :]) for cs in range(2) for t in range(NT)]
            small += [(head_gain[:, 2 + lay, :], a["mem_q_gain_2"][lay].partition_broadcast(P)) for lay in range(2)]
            small += [(head_gain[:, 4 + lay, :], a["mem_k_gain_2"][lay].partition_broadcast(P)) for lay in range(2)]
            assert len(small) == N_SMALL
            for dst, src in small:
                gp.dma_start(dst, src).then_inc(const_landed, 16)
            link(gp.memset(half[:], -0.5))

            def rstd(r, count, cols, eps):
                link(gp.tensor_scalar(stat[:, 1, r, 0:cols], stat[:, 0, r, 0:cols], 1.0 / count, eps, ALU.mult, ALU.add))
                gp.tensor_tensor(stat[:, 2, r, 0:cols], stat[:, 1, r, 0:cols], half[:, 0:cols], ALU.pow).then_inc(rstd_done, 1)

            gp.wait_ge(sq_done, 2)
            rstd(0, D, NT, EPS)
            gp.wait_ge(tr_ready, G_H + 4)
            for t in range(NT):
                gp.dma_start(tok[:, t, :], a["mem_2"][0, t * P:(t + 1) * P, :]).then_inc(mem_landed, 16)
            gp.wait_ge(free_a, freed(NBLK_IN - 1, "a"))
            gp.wait_ge(free_v, freed(NBLK_IN - 1, "v"))
            gp.wait_ge(const_landed, 16 * N_SMALL)
            for c0, done in ((QI, rope_idx), (QA, rope_dsa)):
                v = pj[:, :, c0:c0 + 9 * HD].rearrange("p t (n d) -> p t n d", d=HD)
                x1, x2 = v[:, :, :, 0:8], v[:, :, :, 8:16]
                for t in range(NT):
                    cs, sn = (rope_a[:, q, t, :].unsqueeze(1).to_broadcast([P, 9, 8]) for q in range(2))
                    gp.tensor_tensor(rope_t[:, 0, t], x1[:, t], cs, ALU.mult)
                    gp.tensor_tensor(rope_t[:, 1, t], x2[:, t], sn, ALU.mult)
                    gp.tensor_tensor(rope_t[:, 2, t], x2[:, t], cs, ALU.mult)
                    link(gp.tensor_tensor(rope_t[:, 3, t], x1[:, t], sn, ALU.mult))
                    link(gp.tensor_tensor(x1[:, t], rope_t[:, 0, t], rope_t[:, 1, t], ALU.subtract))
                    ins = gp.tensor_tensor(x2[:, t], rope_t[:, 2, t], rope_t[:, 3, t], ALU.add)
                    link(ins)
                if done is rope_dsa:
                    gp.wait_ge(part_tr, PART[("ki", 0)] + 1)
                for q in range(2):
                    ins = gp.tensor_copy(k_twice[:, :, q, :], pj[:, :, c0 + 8 * HD:c0 + 9 * HD])
                link(ins)
                gp.sem_inc(done, 1)
            gp.wait_ge(sq_done, 4)
            rstd(1, D, NT, EPS)
            gp.dma_start(gain_bc[:], a["g_post"][0].partition_broadcast(P)).then_inc(bc_landed, 16)
            for lay in range(2):
                gp.wait_ge(free_a, freed(B_KV + lay, "a"))
                gp.wait_ge(free_v, freed(B_KV + lay, "v"))
                if lay == 1:
                    gp.wait_ge(tr_ready, G_MEM + 8)
                v = memkv[:, lay, :, 0:S].rearrange("p t (n d) -> p t n d", d=HD)
                link(head_squares(gp, link, v, 4, 0, memk_tmp))
                link(head_rstd(gp, 4, 0))
                head_scale(gp, link, v, 4, head_gain[:, 4 + lay, :], 0)
                gp.sem_inc(memk_made, 1)
            gp.wait_ge(pair_lo, 8)
            for t in range(NT):
                gp.dma_start(x[:, t, :], a["x"][0, t * P:(t + 1) * P, :]).then_inc(x_again, 16)
            gp.wait_ge(tr_ready, G_MERGED + 4)
            for t in range(NT):
                gp.dma_start(tok[:, t, 0:S], a["p"][0, 0, t * P:(t + 1) * P, :]).then_inc(p_landed, 16)
            gp.wait_ge(sq_done, 6)
            link(gp.tensor_tensor(stat[:, 0, 2, 0:NT], stat[:, 0, 2, 0:NT], stat[:, 0, 2, NT:2 * NT], ALU.add))
            rstd(2, D, NT, EPS)
            gp.wait_ge(x_post, NT)
            gp.dma_start(gain_bc[:], a["g_ple"][0].partition_broadcast(P)).then_inc(bc_landed, 16)
            gp.wait_ge(sq_done, 8)
            rstd(3, D, NT, 4 * EPS)
            gp.wait_ge(x_ple, NT)
            gp.dma_start(gain_bc[:, 0:TOKW], a["pool_scale_2"][0].partition_broadcast(P)).then_inc(pool_landed, 16)
            for t in range(NT):
                gp.dma_start(band[:, t], a["c_band"][:, t * P:(t + 1) * P, :].rearrange("g p n -> p g n"))\
                    .then_inc(pool_landed, 16)
            for g in range(4):
                gp.dma_start(w_group[:, g], a["w_pool_group_2"][0, g].rearrange("(c p) n -> p c n", p=GC))\
                    .then_inc(pool_landed, 16)
            gp.wait_ge(sq_done, 10)
            rstd(4, D, NT, EPS)
            gp.wait_ge(free_a, freed(B_POOL + 1, "a"))
            gp.wait_ge(free_v, freed(B_POOL + 1, "v"))
            v = proj[:, 0:NT * D].rearrange("p (t n) -> p t n", t=NT)[:, :, TOKW:].rearrange("p t (n d) -> p t n d", d=HD)
            link(head_squares(gp, link, v, 4, 0, memq_tmp))
            link(head_rstd(gp, 4, 0))
            head_scale(gp, link, v, 4, head_gain[:, 2, :], 0)
            gp.sem_inc(memq_made, 1)
            gp.wait_ge(sq_done, 12)
            rstd(5, D, NT, EPS)
            gp.wait_ge(sq_done, 14)
            rstd(6, D, NT, EPS)
            gp.wait_ge(free_a, freed(B_MOBA + 4, "a"))
            gp.wait_ge(free_v, freed(B_MOBA + 4, "v"))
            moba = proj[:, 0:NT * 2560].rearrange("p (t n) -> p t n", t=NT)
            v = moba[:, :, TOKW:2 * TOKW].rearrange("p t (n d) -> p t n d", d=HD)
            link(head_squares(gp, link, v, 12, 0, m[:, 0:NT * TOKW]))
            link(head_rstd(gp, 12, 0))
            gp.wait_ge(head_sum, 1)
            head_rstd(gp, 12, 1).then_inc(head_rs, 1)
            head_scale(gp, link, v, 12, head_gain[:, 1, :], 0)
            rotate_heads(gp, link, v, 12, m[:, 0:NT * TOKW])
            gp.sem_inc(moba_k_made, 1)
            v = moba[:, :, 3 * TOKW:].rearrange("p t (n d) -> p t n d", d=HD)
            link(head_squares(gp, link, v, 4, 0, memq_tmp))
            link(head_rstd(gp, 4, 0))
            head_scale(gp, link, v, 4, head_gain[:, 3, :], 0)
            gp.sem_inc(memq_made, 1)
            gp.wait_ge(sq_done, 16)
            rstd(7, D, NT, EPS)

        @block.scalar
        def _(act):
            def split(u, slot, land, n):
                act.wait_ge(raw_landed[land], 16 * (u // RAW + 1))
                if u >= RING:
                    act.wait_ge(unit_used, u - RING + 2)
                act.activation(w_hi[:, slot, 0:n], raw[:, land, 0:n], ACT.Copy).then_inc(hi_ready, 1)

            def unit(u):
                v = u + LOOK
                if v < N_UNITS:
                    split(v, v % RING, v % RAW, unit_size(v))

            def group(g, dst, k, gain=None):
                act.wait_ge(tr_ready, g + 1)
                ps = group_bank(g)
                if gain is None:
                    act.activation(dst[:, k:k + 2, :], ps[:, :].rearrange("p (k n) -> p k n", k=2), ACT.Copy)\
                       .then_inc(tr_hi, 1)
                else:
                    act.activation(dst[:, k, :], ps[:, 0:S], ACT.Copy, scale=gain_cols[:, gain + k:gain + k + 1])
                    act.activation(dst[:, k + 1, :], ps[:, S:2 * S], ACT.Copy,
                                   scale=gain_cols[:, gain + k + 1:gain + k + 2]).then_inc(tr_hi, 1)

            def squares(r, src, junk):
                for t in range(NT):
                    act.activation(junk[t], src[:, t], ACT.Square, accum_out=stat[:, 0, r, t:t + 1])\
                       .then_inc(sq_done, 1)

            def block_done(u):
                act.wait_ge(unit_used, u + 2)

            def part(what, pr):
                act.wait_ge(part_tr, PART[(what, pr)] + 1)
                ps = b_io[:, 0:S]
                if what == "gate":
                    if GATES.index(pr):
                        act.wait_ge(pair_lo, GATES.index(pr))
                    act.activation(gated[:], ps, ACT.Tanh, scale=0.5).then_inc(part_cp, 1)
                    return
                dst = {"ki": kT[:], "ka": kT[:]}.get(what)
                if dst is None:
                    dst = qk[:, PART_SLOT[(what, pr)], 0 if what in ("qi", "q") else 1, :]
                act.activation(dst, ps, ACT.Copy).then_inc(part_cp, 1)

            def step(run, s):
                for what in parts_at(run, s):
                    part(*what)
                if 0 <= s < len(run):
                    h = run[s]
                    if isinstance(h, tuple):
                        n = h[1]
                        act.wait_ge(idx_s, n + 1)
                        if n >= 2:
                            act.wait_ge(idx_acc, n - 1)
                        act.activation(prob[:, n % 2, 0:P + S], b_s[n % 2][:, 0:P + S], ACT.Relu).then_inc(idx_relu, 1)
                    else:
                        w0 = width0(h)
                        act.wait_ge(max_done, h + 1)
                        if h < 2:
                            act.wait_ge(idx_acc, 7 + h)
                        else:
                            act.wait_ge(pt_ready, h - 1)
                        act.activation(prob[:, h % 2, 0:w0], b_s[h % 2][:, 0:w0], ACT.Exp, scale=SCALE,
                                       bias=nmx[:, h, 0:1], accum_out=psums[:, h, 0:1])
                        act.activation(prob[:, h % 2, w0:w0 + S], b_s[h % 2][:, w0:w0 + S], ACT.Exp, scale=SCALE,
                                       bias=nmx[:, h, 1:2], accum_out=psums[:, h, 1:2]).then_inc(exp_done, 1)
                if 1 <= s <= len(run) and not isinstance(run[s - 1], tuple):
                    h = run[s - 1]
                    n = width0(h) + S
                    act.wait_ge(pt_ready, h + 1)
                    if h >= 2:
                        act.wait_ge(pv_done, h - 1)
                    act.activation(probT[:, h % 2, 0:n], b_t[:, 0:n], ACT.Copy).then_inc(pt_copied, 1)
                if 2 <= s and not isinstance(run[s - 2], tuple) and run[s - 2] % 2:
                    h = run[s - 2]
                    pr = h // 2
                    if HEADS[h][0] in ("fox", "dsa"):
                        act.wait_ge(pair_tmp, GATES.index(pr) + 1)
                        act.activation(b_hi[:, pair_ktile(pr), :], gated[:], ACT.Copy).then_inc(pair_hi, 1)
                    else:
                        act.wait_ge(pv_done, h + 1)
                        act.activation(b_hi[:, pair_ktile(pr), :], b_v[:, 0:S], ACT.Copy).then_inc(pair_hi, 1)

            act.sem_inc(free_a, 2)
            act.wait_ge(x_landed, 16 * NT)
            squares(0, x, [tok[:, t] for t in range(NT)])
            for u in range(LOOK):
                split(u, u % RING, u % RAW, unit_size(u))
            act.wait_ge(gains_made, 1)
            for g in range(4):
                group(G_H + g, a_hi, 2 * g, 0)

            def evac_in(b, r):
                act.activation(proj[:, bass.ds(b * CIN, CIN)], bank[2 * r][:, 0:CIN], ACT.Copy).then_inc(free_a, 1)

            with act.Fori(0, NBLK_IN // 2 - 1) as i:
                for j in range(4):
                    c = j + LOOK
                    act.wait_ge(raw_landed[c % RAW], (i * 2 + (c // RAW + 1)) * 16)
                    act.wait_ge(unit_used, i * 4 + (c - RING + 2))
                    act.activation(w_hi[:, c % RING, 0:4 * CIN], raw[:, c % RAW, 0:4 * CIN], ACT.Copy).then_inc(hi_ready, 1)
                    if j % 2:
                        act.wait_ge(unit_used, i * 4 + (j + 2))
                        evac_in(i * 2 + j // 2, j // 2)
            for u in range(U_MERGE - 4, U_MERGE):
                unit(u)
                if u % 2:
                    block_done(u)
                    evac_in(u // 2, u // 2 % 2)

            act.wait_ge(f_abs, 1)
            act.activation(fgt[:, 2], fgt[:, 1], ACT.Exp).then_inc(act_chain, 1)
            act.wait_ge(act_chain, 1)
            act.activation(fgt[:, 3], fgt[:, 2], ACT.Ln, bias=1.0).then_inc(f_ln, 1)

            for s in run_steps(RUN1):
                step(RUN1, s)
                if s == 7:
                    act.wait_ge(mem_landed, 16 * NT)
                    squares(1, tok, [b_hi[:, 4 * t:4 * t + 4, :].rearrange("p k n -> p (k n)") for t in range(NT)])
                for what in after_step(s):
                    if what[0] == "merge":
                        u = U_MERGE + what[1]
                        unit(u)
                        if u % 2:
                            block_done(u)
                            for t in range(NT):
                                c = what[1] // 2 * CB
                                act.activation(m_sig[:, t, c:c + CB], bank[t][:, :], ACT.Tanh, scale=0.5)\
                                   .then_inc(merge_tanh, 1)
                            act.wait_ge(merge_tanh, (what[1] // 2 + 1) * NT)
                            act.sem_inc(free_a, 1)
                    elif what[0] == "kv":
                        u = U_KV + what[1]
                        unit(u)
                        if u % 2:
                            block_done(u)
                            act.activation(memkv[:, what[1] // 2, 0, :], bank[0][:, :], ACT.Copy).then_inc(free_a, 1)
                    else:
                        group(G_MEM + 4 * what[1] + what[2], a_hi, 2 * what[2], 24 + 8 * what[1])
            for u in range(U_BR, U_WO):
                unit(u)
            for g in range(4):
                group(G_MERGED + g, a_hi, 2 * g)
            for c in range(2):
                unit(U_WO + 2 * c)
                unit(U_WO + 2 * c + 1)
                block_done(U_WO + 2 * c + 1)
                for t in range(NT):
                    ins = act.activation(m_junk[:, t, c * CB:c * CB + CB], bank[pair_bank(B_WO + c) + t][:, :], ACT.Square,
                                         accum_out=stat[:, 0, 2, NT * c + t:NT * c + t + 1])
                    if c == 1:
                        ins.then_inc(sq_done, 1)
            group(G_P, b_hi, 0)
            unit(U_PLE)
            for c in range(2):
                act.wait_ge(ple_block, c + 1)
                act.activation(e_tok[:, 0, c * CB:c * CB + CB], bank[pair_bank(B_PLE + c)][:, :], ACT.Copy)\
                   .then_inc(free_a, 1)
            for g in range(4):
                group(G_X + g, a_hi, 2 * g)
            for c in range(2):
                unit(U_GATE + 2 * c)
                unit(U_GATE + 2 * c + 1)
                block_done(U_GATE + 2 * c + 1)
                for t in range(NT):
                    act.activation(tok[:, t, c * CB:c * CB + CB], bank[pair_bank(B_GATE + c) + t][:, :], ACT.Tanh, scale=0.5)\
                       .then_inc(gate_tanh, 1)
                act.wait_ge(gate_tanh, NT * (c + 1))
                act.sem_inc(free_a, 1)
            act.wait_ge(z_made, 2)
            squares(3, tok, [m_junk[:, t, :] for t in range(NT)])

            def norm_of_x(r, ready, count, g0, gain):
                act.wait_ge(ready, count)
                squares(r, x, [tok[:, t] for t in range(NT)])
                for g in range(4):
                    group(g0 + g, a_hi, 2 * g, gain)

            def mlp(base, lay, g0):
                def hidden_relu(i):
                    for t in range(NT):
                        ins = act.activation(hidden[:, t], b_s[t][:, :], ACT.Relu)
                    ins.then_inc(ff_relu, 1)
                unit(base)
                unit(base + 1)
                block_done(base + 1)
                hidden_relu(0)

                def chunk(i, peeled):
                    for r in range(4):
                        c = 2 + r + LOOK
                        if peeled:
                            unit(base + 2 + 4 * i + r)
                        else:
                            act.wait_ge(raw_landed[(base + c) % RAW], (i * 2 + ((base + c) // RAW + 1)) * 16)
                            act.wait_ge(unit_used, i * 4 + (base + c - RING + 2))
                            act.activation(w_hi[:, (base + c) % RING, :], raw[:, (base + c) % RAW, :], ACT.Copy)\
                               .then_inc(hi_ready, 1)
                        if r == 0:
                            for q in range(2):
                                act.wait_ge(tr_ready, i * 2 + (g0 + q + 1))
                                act.activation(b_hi[:, 2 * q:2 * q + 2, :],
                                               b_tr[(g0 + q) % 2][:, :].rearrange("p (k n) -> p k n", k=2), ACT.Copy)\
                                   .then_inc(tr_hi, 1)
                        if r == 1:
                            act.wait_ge(unit_used, i * 4 + (base + 3 + 2))
                            hidden_relu(i + 1)
                with act.Fori(0, FF - 2) as i:
                    chunk(i, False)
                chunk(FF - 2, True)
                for q in range(2):
                    group(g0 + 2 * (FF - 1) + q, b_hi, 2 * q)
                unit(base + 4 * FF - 2)
                unit(base + 4 * FF - 1)

            norm_of_x(4, x_ple, NT, G_MIX0, 8)
            for c in range(2):
                unit(U_POOL + 2 * c)
                unit(U_POOL + 2 * c + 1)
                block_done(U_POOL + 2 * c + 1)
                act.activation(h_pool[:, 0, c * CB:c * CB + CB], bank[pair_bank(B_POOL + c)][:, :], ACT.Copy)\
                   .then_inc(free_a, 1)
            for g in range(4):
                act.wait_ge(d_ready, 2 * g + 1)
                act.activation(dT[:, g, 0, :], b_io[0:GC, 0:S], ACT.Copy).then_inc(d_copied_a, 1)
            for g in range(3):
                group(G_TOK0 + g, b_hi, 2 * g)
            for s in run_steps(RUN2):
                step(RUN2, s)
            for u in range(U_OUT0, U_FF0):
                unit(u)
            norm_of_x(5, x_mix, NT, G_MLP0, 40)
            mlp(U_FF0, 0, G_FF0)
            norm_of_x(6, x_mlp, NT, G_MIX1, 16)
            for c in range(5):
                unit(U_MOBA + 2 * c)
                unit(U_MOBA + 2 * c + 1)
                block_done(U_MOBA + 2 * c + 1)
                act.activation(h_moba[:, 0, c * CB:c * CB + CB], bank[pair_bank(B_MOBA + c)][:, :], ACT.Copy)\
                   .then_inc(free_a, 1)
            for s in run_steps(RUN3):
                step(RUN3, s)
            for u in range(U_OUT1, U_FF1):
                unit(u)
            norm_of_x(7, x_mix, 2 * NT, G_MLP1, 48)
            mlp(U_FF1, 1, G_FF1)

        @block.vector
        def _(dve):
            link = Linker(dve, vec_chain)

            def unit(u):
                v = u + LOOK
                if v < N_UNITS:
                    split(v)

            def split(v):
                n = unit_size(v)
                dve.wait_ge(hi_ready, v + 1)
                dve.tensor_tensor(w_lo[:, v % RING, 0:n], raw[:, v % RAW, 0:n], w_hi[:, v % RING, 0:n].bitcast(F32),
                                  ALU.subtract).then_inc(lo_ready, 1)

            def group(g, hi, lo, k, gain=None):
                dve.wait_ge(tr_hi, g + 1)
                ps = group_bank(g)
                if gain is None:
                    dve.tensor_tensor(lo[:, k:k + 2, :], ps[:, :].rearrange("p (k n) -> p k n", k=2),
                                      hi[:, k:k + 2, :].bitcast(F32), ALU.subtract).then_inc(tr_lo, 1)
                else:
                    for q in range(2):
                        ins = dve.scalar_tensor_tensor(lo[:, k + q, :], ps[:, q * S:q * S + S],
                                                       gain_cols[:, gain + k + q:gain + k + q + 1],
                                                       hi[:, k + q, :].bitcast(F32), ALU.mult, ALU.subtract)
                    ins.then_inc(tr_lo, 1)

            def block_done(u):
                dve.wait_ge(unit_used, u + 2)

            def norm(r, count, src):
                dve.wait_ge(rstd_done, count)
                for t in range(NT):
                    dve.tensor_scalar(tok[:, t, :], src[:, t, :], stat[:, 2, r, t:t + 1], None, ALU.mult).then_inc(normed, 1)

            def step(run, s):
                for what, pr in parts_at(run, s):
                    if what == "gate":
                        dve.wait_ge(part_cp, PART[(what, pr)] + 1)
                        dve.scalar_tensor_tensor(gate_s[:], gated[:], 1.0, b_io[:, 0:S], ALU.add, ALU.mult)\
                           .then_inc(gate_cp, 1)
                if 0 <= s < len(run):
                    h = run[s]
                    if isinstance(h, tuple):
                        n = h[1]
                        dve.wait_ge(idx_relu, n + 1)
                        for t, c, w in ((0, 0, P), (1, P, S)):
                            src, w_ = prob[:, n % 2, c:c + w], wis[:, t, n:n + 1]
                            if n == 0:
                                ins = dve.tensor_scalar(score[:, c:c + w], src, w_, None, ALU.mult)
                            else:
                                ins = dve.scalar_tensor_tensor(score[:, c:c + w], src, w_, score[:, c:c + w],
                                                               ALU.mult, ALU.add)
                        ins.then_inc(idx_acc, 1)
                        dve.wait_ge(idx_acc, n + 1)
                    else:
                        w0 = width0(h)
                        dve.wait_ge(s_ready, h + 1)
                        dve.tensor_reduce(mx[:, h, 0:1], b_s[h % 2][:, 0:w0], AX.X, ALU.max)
                        link(dve.tensor_reduce(mx[:, h, 1:2], b_s[h % 2][:, w0:w0 + S], AX.X, ALU.max))
                        dve.tensor_scalar(nmx[:, h, :], mx[:, h, :], -SCALE, None, ALU.mult).then_inc(max_done, 1)
                        if h < TOPK // 8:
                            select_round(h)
                        dve.wait_ge(exp_done, h + 1)
                        link(dve.reciprocal(prec[:, h, :], psums[:, h, :]))
                        dve.tensor_scalar(prob[:, h % 2, 0:w0], prob[:, h % 2, 0:w0], prec[:, h, 0:1], None, ALU.mult)
                        dve.tensor_scalar(prob[:, h % 2, w0:w0 + S], prob[:, h % 2, w0:w0 + S], prec[:, h, 1:2], None,
                                          ALU.mult).then_inc(p_ready, 1)
                if 2 <= s and not isinstance(run[s - 2], tuple) and run[s - 2] % 2:
                    h = run[s - 2]
                    pr = h // 2
                    kt = pair_ktile(pr)
                    if HEADS[h][0] in ("fox", "dsa"):
                        dve.wait_ge(pv_done, h + 1)
                        dve.wait_ge(gate_cp, GATES.index(pr) + 1)
                        dve.scalar_tensor_tensor(gated[:], b_v[:, 0:S], 0.5, gate_s[:], ALU.mult, ALU.mult)\
                           .then_inc(pair_tmp, 1)
                        dve.wait_ge(pair_hi, pr + 1)
                        dve.tensor_tensor(b_lo[:, kt, :], gated[:], b_hi[:, kt, :].bitcast(F32), ALU.subtract)\
                           .then_inc(pair_lo, 1)
                    else:
                        dve.wait_ge(pair_hi, pr + 1)
                        dve.tensor_tensor(b_lo[:, kt, :], b_v[:, 0:S], b_hi[:, kt, :].bitcast(F32), ALU.subtract)\
                           .then_inc(pair_lo, 1)

            def select_round(n):
                if n == 0:
                    for c in (0, P + P):
                        ins = dve.scalar_tensor_tensor(score[:, c:c + P], mask[:], FILL, score[:, c:c + P], ALU.mult, ALU.add)
                    link(ins)
                for t, c, w in ((0, 0, P), (1, P, S)):
                    ins = dve.max(top8[:, t, :], score[:, c:c + w])
                link(ins)
                for t, c, w in ((0, 0, P), (1, P, S)):
                    ins = dve.match_replace(score[:, c:c + w], top8[:, t, :], score[:, c:c + w], TAKEN)
                link(ins)
                if n == TOPK // 8 - 1:
                    dve.tensor_scalar(sel_b[:], score[:], TAKEN / 2, NEG, ALU.is_ge, ALU.mult).then_inc(sel_made, 1)

            dve.sem_inc(free_v, 2)
            dve.wait_ge(const_landed, 16 * N_SMALL)
            dve.tensor_copy(ident_b[:], ident[:])
            dve.tensor_copy(mask_b[:], mask[:]).then_inc(consts_made, 1)
            dve.wait_ge(gains_tr, 1)
            dve.tensor_copy(gain_cols[:], b_t[:, 0:56]).then_inc(gains_made, 1)
            dve.wait_ge(gains_made, 1)
            for u in range(LOOK):
                split(u)
            norm(0, 1, x)
            for g in range(4):
                group(G_H + g, a_hi, a_lo, 2 * g, 0)

            def evac_in(b, r):
                dve.tensor_copy(proj[:, bass.ds(b * CIN + DIN, CIN)], bank[2 * r + 1][:, 0:CIN]).then_inc(free_v, 1)

            with dve.Fori(0, NBLK_IN // 2 - 1) as i:
                for j in range(4):
                    c = j + LOOK
                    dve.wait_ge(hi_ready, i * 4 + (c + 1))
                    dve.tensor_tensor(w_lo[:, c % RING, 0:4 * CIN], raw[:, c % RAW, 0:4 * CIN],
                                      w_hi[:, c % RING, 0:4 * CIN].bitcast(F32), ALU.subtract).then_inc(lo_ready, 1)
                    if j % 2:
                        dve.wait_ge(unit_used, i * 4 + (j + 2))
                        evac_in(i * 2 + j // 2, j // 2)
            for u in range(U_MERGE - 4, U_MERGE):
                unit(u)
                if u % 2:
                    block_done(u)
                    evac_in(u // 2, u // 2 % 2)

            dve.wait_ge(free_a, freed(NBLK_IN - 1, "a"))
            dve.wait_ge(free_v, freed(NBLK_IN - 1, "v"))
            link(dve.tensor_tensor(fgt[:, 0], pj[:, :, FB:FB + 8], bias_f[:].unsqueeze(1).to_broadcast([P, NT, 8]), ALU.add))
            link(dve.tensor_scalar(fgt[:, 4], fgt[:, 0], -1.0, None, ALU.mult))
            dve.tensor_tensor(fgt[:, 1], fgt[:, 0], fgt[:, 4], ALU.min).then_inc(f_abs, 1)
            link(dve.tensor_scalar(fgt[:, 5], fgt[:, 0], 0.0, None, ALU.min))
            link(dve.tensor_scalar(wis[:], pj[:, :, WI:WI + 8], IDX_SCALE, None, ALU.mult))
            dve.wait_ge(f_ln, 1)
            dve.tensor_tensor(fgt[:, 4], fgt[:, 5], fgt[:, 3], ALU.subtract).then_inc(f_log, 1)
            dve.wait_ge(c_ready, 1)
            dve.tensor_scalar(cT[:], b_t[0:8, 0:S], -1.0 / SCALE, None, ALU.mult).then_inc(c_made, 1)

            for s in run_steps(RUN1):
                step(RUN1, s)
                if s == 7:
                    norm(1, 2, tok)
                for what in after_step(s):
                    if what[0] == "merge":
                        unit(U_MERGE + what[1])
                        if what[1] % 2:
                            c = what[1] // 2 * CB
                            dve.wait_ge(merge_tanh, (what[1] // 2 + 1) * NT)
                            dve.tensor_scalar(m_sig[:, :, c:c + CB], m_sig[:, :, c:c + CB], 0.5, 0.5, ALU.mult, ALU.add)\
                               .then_inc(merge_sig, 1)
                    elif what[0] == "kv":
                        u = U_KV + what[1]
                        unit(u)
                        if u % 2:
                            block_done(u)
                            dve.tensor_copy(memkv[:, what[1] // 2, 1, :], bank[1][:, :]).then_inc(free_v, 1)
                    else:
                        group(G_MEM + 4 * what[1] + what[2], a_hi, a_lo, 2 * what[2], 24 + 8 * what[1])
            dve.wait_ge(merge_sig, 4)
            for c in range(2):
                cols = slice(c * CB, c * CB + CB)
                for r in range(2):
                    u = U_BR + 2 * c + r
                    unit(u)
                    block_done(u)
                    for t in range(NT):
                        ps = bank[pair_bank(B_BR + 2 * c + r) + t][:, :]
                        g = m_sig[:, t, r * D + c * CB:r * D + c * CB + CB]
                        if r == 0:
                            ins = dve.tensor_tensor(tok[:, t, cols], ps, g, ALU.mult)
                        else:
                            ins = dve.tensor_tensor(g, ps, g, ALU.mult)
                    ins.then_inc(free_v, 1)
                    dve.wait_ge(free_v, freed(B_BR + 2 * c + r, "v"))
                for t in range(NT):
                    g = m_sig[:, t, D + c * CB:D + c * CB + CB]
                    dve.tensor_tensor(tok[:, t, cols], tok[:, t, cols], g, ALU.add).then_inc(merged, 1)
            for g in range(4):
                group(G_MERGED + g, a_hi, a_lo, 2 * g)
            for u in range(U_WO, U_PLE):
                unit(u)
            group(G_P, b_hi, b_lo, 0)
            unit(U_PLE)
            dve.wait_ge(bc_landed, 16)
            dve.wait_ge(rstd_done, 3)
            o_tok = m[:, NT * D:].rearrange("p (t n) -> p t n", t=NT)
            for c in range(2):
                cols = slice(c * CB, c * CB + CB)
                for t in range(NT):
                    ins = dve.scalar_tensor_tensor(o_tok[:, t, cols], bank[pair_bank(B_WO + c) + t][:, :],
                                                   stat[:, 2, 2, t:t + 1], gain_bc[:, cols], ALU.mult, ALU.mult)
                ins.then_inc(free_v, 1)
            dve.wait_ge(free_v, freed(B_WO + 1, "v"))
            dve.wait_ge(x_again, 16 * NT)
            for t in range(NT):
                dve.tensor_tensor(x[:, t, :], x[:, t, :], o_tok[:, t, :], ALU.add).then_inc(x_post, 1)
            for c in range(2):
                dve.wait_ge(ple_block, c + 1)
                dve.tensor_copy(e_tok[:, 1, c * CB:c * CB + CB], bank[pair_bank(B_PLE + c) + 1][:, :]).then_inc(free_v, 1)
            for g in range(4):
                group(G_X + g, a_hi, a_lo, 2 * g)
            for c in range(2):
                cols = slice(c * CB, c * CB + CB)
                unit(U_GATE + 2 * c)
                unit(U_GATE + 2 * c + 1)
                dve.wait_ge(gate_tanh, NT * (c + 1))
                dve.wait_ge(free_a, freed(B_PLE + 1, "a"))
                dve.wait_ge(free_v, freed(B_PLE + 1, "v"))
                dve.scalar_tensor_tensor(tok[:, :, cols], tok[:, :, cols], 1.0, e_tok[:, :, cols], ALU.add, ALU.mult)\
                   .then_inc(z_made, 1)
            dve.wait_ge(rstd_done, 4)
            dve.wait_ge(bc_landed, 32)
            for t in range(NT):
                ins = dve.scalar_tensor_tensor(tok[:, t, :], tok[:, t, :], stat[:, 2, 3, t:t + 1], gain_bc[:],
                                               ALU.mult, ALU.mult)
            link(ins)
            for t in range(NT):
                dve.tensor_tensor(x[:, t, :], x[:, t, :], tok[:, t, :], ALU.add).then_inc(x_ple, 1)

            def norm_of_x(r, count, g0, gain):
                norm(r, count, x)
                for g in range(4):
                    group(g0 + g, a_hi, a_lo, 2 * g, gain)

            def add_out(u, b, done):
                for c in range(2):
                    unit(u + 2 * c)
                    unit(u + 2 * c + 1)
                    block_done(u + 2 * c + 1)
                    for t in range(NT):
                        xs = x[:, t, c * CB:c * CB + CB]
                        ins = dve.tensor_tensor(xs, xs, bank[pair_bank(b + c) + t][:, :], ALU.add)
                    ins.then_inc(free_v, 1)
                dve.wait_ge(free_v, freed(b + 1, "v"))
                dve.sem_inc(done, NT)

            def mlp(base, lay, g0):
                def hidden_square(n):
                    dve.wait_ge(ff_relu, n)
                    dve.tensor_tensor(hidden, hidden, hidden, ALU.mult).then_inc(ff_sq, 1)
                unit(base)
                unit(base + 1)
                hidden_square(lay * FF + 1)

                def chunk(i, peeled):
                    for r in range(4):
                        c = 2 + r + LOOK
                        if peeled:
                            unit(base + 2 + 4 * i + r)
                        else:
                            dve.wait_ge(hi_ready, i * 4 + (base + c + 1))
                            dve.tensor_tensor(w_lo[:, (base + c) % RING, :], raw[:, (base + c) % RAW, :],
                                              w_hi[:, (base + c) % RING, :].bitcast(F32), ALU.subtract).then_inc(lo_ready, 1)
                        if r == 0:
                            for q in range(2):
                                dve.wait_ge(tr_hi, i * 2 + (g0 + q + 1))
                                dve.tensor_tensor(b_lo[:, 2 * q:2 * q + 2, :],
                                                  b_tr[(g0 + q) % 2][:, :].rearrange("p (k n) -> p k n", k=2),
                                                  b_hi[:, 2 * q:2 * q + 2, :].bitcast(F32), ALU.subtract).then_inc(tr_lo, 1)
                        if r == 1:
                            hidden_square(i + (lay * FF + 2))
                with dve.Fori(0, FF - 2) as i:
                    chunk(i, False)
                chunk(FF - 2, True)
                for q in range(2):
                    group(g0 + 2 * (FF - 1) + q, b_hi, b_lo, 2 * q)
                unit(base + 4 * FF - 2)
                unit(base + 4 * FF - 1)
                block_done(base + 4 * FF - 1)
                for t in range(NT):
                    for c in range(2):
                        xs = x[:, t, c * CB:c * CB + CB]
                        ins = dve.tensor_tensor(xs, xs, bank[2 * c + t][:, :], ALU.add)
                    ins.then_inc(x_mlp, 1)
                dve.wait_ge(x_mlp, NT * (lay + 1))

            norm_of_x(4, 5, G_MIX0, 8)
            for c in range(2):
                unit(U_POOL + 2 * c)
                unit(U_POOL + 2 * c + 1)
                block_done(U_POOL + 2 * c + 1)
                dve.tensor_copy(h_pool[:, 1, c * CB:c * CB + CB], bank[pair_bank(B_POOL + c) + 1][:, :]).then_inc(free_v, 1)
            for g in range(4):
                dve.wait_ge(d_ready, 2 * g + 2)
                dve.tensor_copy(dT[:, g, 1, :], b_t[0:GC, 0:S]).then_inc(d_copied_v, 1)
            dve.wait_ge(pool_landed, 16 * 7)
            dve.wait_ge(y_ready, 1)
            for t in range(NT):
                for q in range(2):
                    cols = slice(q * 2 * GW, q * 2 * GW + 2 * GW)
                    ins = dve.tensor_tensor(tok[:, t, cols], bank[2 * t + q][:, 0:2 * GW], gain_bc[:, cols], ALU.mult)
            ins.then_inc(y_made, 1)
            for g in range(3):
                group(G_TOK0 + g, b_hi, b_lo, 2 * g)
            for s in run_steps(RUN2):
                step(RUN2, s)
            add_out(U_OUT0, B_OUT0, x_mix)
            norm_of_x(5, 6, G_MLP0, 40)
            mlp(U_FF0, 0, G_FF0)
            norm_of_x(6, 7, G_MIX1, 16)
            for c in range(5):
                unit(U_MOBA + 2 * c)
                unit(U_MOBA + 2 * c + 1)
                block_done(U_MOBA + 2 * c + 1)
                dve.tensor_copy(h_moba[:, 1, c * CB:c * CB + CB], bank[pair_bank(B_MOBA + c) + 1][:, :]).then_inc(free_v, 1)
            dve.wait_ge(free_a, freed(B_MOBA + 4, "a"))
            dve.wait_ge(free_v, freed(B_MOBA + 4, "v"))
            v = h_moba[:, :, 0:TOKW].rearrange("p t (n d) -> p t n d", d=HD)
            head_squares(dve, link, v, 12, 1, m[:, NT * TOKW:2 * NT * TOKW]).then_inc(head_sum, 1)
            dve.wait_ge(head_rs, 1)
            head_scale(dve, link, v, 12, head_gain[:, 0, :], 1)
            rotate_heads(dve, link, v, 12, m[:, NT * TOKW:2 * NT * TOKW])
            dve.sem_inc(moba_q_made, 1)
            for s in run_steps(RUN3):
                step(RUN3, s)
            add_out(U_OUT1, B_OUT1, x_mix)
            norm_of_x(7, 8, G_MLP1, 48)
            mlp(U_FF1, 1, G_FF1)

        @block.tensor
        def _(pe):
            def product(u, slot, hi, lo, k0, banks, first, last, n=CB, kts=4, col=0, used=True):
                pe.wait_ge(lo_ready, u + 1)
                pitch = n if kts == 4 else D
                for k in range(kts):
                    w = slice(k * pitch + col, k * pitch + col + n)
                    for t in range(NT):
                        ts = slice(t * P, t * P + P)
                        for q, (xa, wa) in enumerate(((hi, w_hi), (hi, w_lo), (lo, w_hi))):
                            ins = pe.matmul(banks[t][:, 0:n], xa[:, k0 + k, ts], wa[:, slot, w],
                                            start=first and k == 0 and q == 0, stop=last and k == kts - 1 and q == 2)
                if used:
                    ins.then_inc(unit_used, 1)
                return ins

            def banks_free(k, one=False):
                j = k - (1 if one else 2)
                if j < 0 or "a" in READERS[BLOCKS[j]]:
                    pe.wait_ge(free_a, freed(j, "a"))
                if j < 0 or "v" in READERS[BLOCKS[j]]:
                    pe.wait_ge(free_v, freed(j, "v"))

            def dense(u0, k, hi, lo):
                banks_free(k)
                b = bank[pair_bank(k):pair_bank(k) + 2]
                product(u0, u0 % RING, hi, lo, 0, b, True, False)
                product(u0 + 1, (u0 + 1) % RING, hi, lo, 4, b, False, True)

            def group(g, src, k, kts=2):
                if g >= 2:
                    pe.wait_ge(tr_lo, g if G_MEM < g < G_MERGED else g - 1)
                ps = group_bank(g)
                for kk in range(2):
                    for t in range(NT):
                        ins = pe.transpose(ps[:, kk * S + t * P:kk * S + t * P + P],
                                           src[:, t, (k + kk) * P:(k + kk) * P + P], ident[:])
                ins.then_inc(tr_ready, 1)

            def part(what, pr):
                n = PART[(what, pr)]
                if n:
                    pe.wait_ge(part_cp, n)
                before = PARTS[n - 1] if n else None
                if before and before[0] == "gate":
                    pe.wait_ge(gate_cp, GATES.index(before[1]) + 1)
                if what in ("ki", "qi"):
                    pe.wait_ge(rope_idx, 1)
                elif what == "ka":
                    pe.wait_ge(rope_dsa, 1)
                else:
                    kind, j = HEADS[2 * pr]
                    if kind == "dsa" and what == "q":
                        pe.wait_ge(rope_dsa, 1)
                    if kind == "moba":
                        pe.wait_ge(moba_q_made if what == "q" else moba_k_made, 1)
                    if kind[:3] == "mem":
                        pe.wait_ge(memq_made if what == "q" else memk_made, int(kind[3]) + 1)
                for t in range(NT):
                    if what in ("ki", "ka"):
                        src = k_twice[:, t].rearrange("p q d -> p (q d)")
                    elif what == "qi":
                        src = pj[:, t, QI + P * pr:QI + P * pr + P]
                    else:
                        src = head_cols(2 * pr)[what][:, t]
                    ins = pe.transpose(b_io[:, t * P:t * P + P], src, ident[:])
                ins.then_inc(part_tr, 1)

            def logits(ps, q, k, w0, stop):
                pe.matmul(ps[:, 0:w0], q[:, 0:P], k[:, 0:w0], start=True, stop=stop)
                return pe.matmul(ps[:, w0:w0 + S], q[:, P:S], k[:, 0:S], start=True, stop=stop)

            def step(run, s):
                for what in parts_at(run, s):
                    part(*what)
                if 0 <= s < len(run):
                    h = run[s]
                    if isinstance(h, tuple):
                        n = h[1]
                        rows = slice(HD * (n % 2), HD * (n % 2) + HD)
                        pe.wait_ge(part_cp, PART[("qi", n // 2)] + 1)
                        pe.wait_ge(part_cp, PART[("ki", 0)] + 1)
                        if n >= 2:
                            pe.wait_ge(idx_relu, n - 1)
                        logits(b_s[n % 2], qk[rows, PART_SLOT[("qi", n // 2)], 0], kT[rows], P, True).then_inc(idx_s, 1)
                    else:
                        kind, j = HEADS[h]
                        rows = slice(HD * (h % 2), HD * (h % 2) + HD)
                        slot = PART_SLOT[("q", h // 2)]
                        pe.wait_ge(part_cp, PART[("q", h // 2)] + 1)
                        pe.wait_ge(part_cp, PART[("ka", 0) if kind == "dsa" else ("k", h // 2)] + 1)
                        if h < 2:
                            pe.wait_ge(idx_relu, 7 + h)
                        else:
                            pe.wait_ge(exp_done, h - 1)
                        k = kT[rows] if kind == "dsa" else qk[rows, slot, 1]
                        ps, w0 = b_s[h % 2], width0(h)
                        free = kind[:3] == "mem"
                        for t, c, w in ((0, 0, w0), (1, w0, S)):
                            ins = pe.matmul(ps[:, c:c + w], qk[rows, slot, 0, t * P:t * P + P], k[:, 0:w],
                                            start=True, stop=free)
                            if kind == "fox":
                                pe.wait_ge(c_made, 1)
                                pe.matmul(ps[:, c:c + w], ident[0:8, j:j + 1].to_broadcast([8, P]), cT[:, 0:w],
                                          start=False, stop=False)
                            if kind == "dsa":
                                pe.wait_ge(sel_made, 1)
                                pe.matmul(ps[:, c:c + w], ident_b[:], sel_b[:, c:c + w], start=False, stop=False)
                            if not free:
                                ins = pe.matmul(ps[:, c + w - P:c + w], ident_b[:], mask_b[:], start=False, stop=True)
                        ins.then_inc(s_ready, 1)
                if 1 <= s <= len(run) and not isinstance(run[s - 1], tuple):
                    h = run[s - 1]
                    w0 = width0(h)
                    pe.wait_ge(p_ready, h + 1)
                    if h:
                        pe.wait_ge(pt_copied, h)
                    pr = prob[:, h % 2]
                    cuts = [0, w0] + ([P, w0 + P] if w0 == S else [w0 + P])
                    for q, c in enumerate(cuts):
                        ins = pe.transpose(b_t[:, q * P:q * P + P], pr[:, c:c + P], ident[:])
                    ins.then_inc(pt_ready, 1)
                if 2 <= s and not isinstance(run[s - 2], tuple):
                    h = run[s - 2]
                    rows = slice(HD * (h % 2), HD * (h % 2) + HD)
                    v, pT = head_cols(h)["v"], probT[:, h % 2]
                    pe.wait_ge(pt_copied, h + 1)
                    if h % 2 == 0 and h:
                        pe.wait_ge(pair_lo, h // 2)
                    pe.matmul(b_v[rows, 0:S], v[:, 0], pT[:, 0:S], start=True, stop=False)
                    c = S if width0(h) == S else P
                    pe.matmul(b_v[rows, S - c:S], v[:, 1], pT[:, S:S + c], start=False, stop=True)\
                      .then_inc(pv_done, 1)

            pe.sem_inc(unit_used, 1)
            pe.wait_ge(const_landed, 16 * N_SMALL)
            pe.transpose(b_t[:, 0:56], gain_rows[:], ident[0:56, 0:56]).then_inc(gains_tr, 1)
            pe.wait_ge(consts_made, 1)
            pe.wait_ge(normed, 2)
            for g in range(4):
                group(G_H + g, tok, 2 * g)
            pe.wait_ge(tr_lo, G_H + 4)
            with pe.Fori(0, NBLK_IN // 2) as i:
                for r in range(2):
                    pe.wait_ge(free_a, i * 2 + (r + 1))
                    pe.wait_ge(free_v, i * 2 + (r + 1))
                    b = bank[2 * r:2 * r + 2]
                    product(i * 4 + 2 * r, 2 * r, a_hi, a_lo, 0, b, True, False, CIN)
                    product(i * 4 + (2 * r + 1), 2 * r + 1, a_hi, a_lo, 4, b, False, True, CIN)
            pe.wait_ge(f_log, 1)
            pe.wait_ge(free_v, freed(NBLK_IN - 1, "v"))
            pe.wait_ge(free_a, freed(NBLK_IN - 1, "a"))
            pe.matmul(b_t[0:8, 0:S], fgt[:, 4, 0], tri[:], start=True, stop=False)
            pe.matmul(b_t[0:8, P:S], fgt[:, 4, 1], tri[:, 0:P], start=False, stop=True).then_inc(c_ready, 1)
            pe.wait_ge(c_made, 1)

            for s in run_steps(RUN1):
                step(RUN1, s)
                for what in after_step(s):
                    if what[0] in ("merge", "kv"):
                        k, q = divmod(what[1], 2)
                        u = (U_MERGE if what[0] == "merge" else U_KV) + what[1]
                        if q == 0:
                            banks_free((B_MERGE if what[0] == "merge" else B_KV) + k, one=True)
                            if what[0] == "kv":
                                pe.wait_ge(tr_lo, G_MEM + 4 * (k + 1))
                        product(u, u % RING, a_hi, a_lo, 4 * q, bank[0:2], q == 0, q == 1)
                    else:
                        pe.wait_ge(normed, 4)
                        group(G_MEM + 4 * what[1] + what[2], tok, 2 * what[2])
            pe.wait_ge(pair_lo, 8)
            for c in range(4):
                k = B_BR + c
                banks_free(k)
                if c == 0:
                    banks_free(k, one=True)
                u = U_BR + c
                product(u, u % RING, b_hi, b_lo, 4 * (c % 2), bank[pair_bank(k):pair_bank(k) + 2], True, True)
            pe.wait_ge(merged, 2 * NT)
            for g in range(4):
                group(G_MERGED + g, tok, 2 * g)
            pe.wait_ge(tr_lo, G_MERGED + 4)
            for c in range(2):
                dense(U_WO + 2 * c, B_WO + c, a_hi, a_lo)
            pe.wait_ge(p_landed, 16 * NT)
            group(G_P, tok, 0)
            pe.wait_ge(tr_lo, G_P + 1)
            for c in range(2):
                banks_free(B_PLE + c)
                b = bank[pair_bank(B_PLE + c):pair_bank(B_PLE + c) + 2]
                ins = product(U_PLE, U_PLE % RING, b_hi, b_lo, 0, b, True, True, CB, 2, c * CB, used=False)
                ins.then_inc(ple_block, 1)
            pe.wait_ge(ple_block, 2)
            pe.sem_inc(unit_used, 1)
            pe.wait_ge(x_post, NT)
            for g in range(4):
                group(G_X + g, x, 2 * g)
            pe.wait_ge(tr_lo, G_X + 4)
            for c in range(2):
                dense(U_GATE + 2 * c, B_GATE + c, a_hi, a_lo)

            def norm_of_x(count, g0):
                pe.wait_ge(normed, count)
                for g in range(4):
                    group(g0 + g, tok, 2 * g)
                pe.wait_ge(tr_lo, g0 + 4)

            def mlp(base, lay, g0):
                def up(u, half_, slot):
                    product(u, slot, a_hi, a_lo, 4 * half_, b_s, half_ == 0, half_ == 1)
                up(base, 0, base % RING)
                up(base + 1, 1, (base + 1) % RING)

                def chunk(i, first, last):
                    s = [(base + 2 + r) % RING for r in range(4)]
                    if not last:
                        pe.wait_ge(ff_relu, i + (lay * FF + 1))
                        up(i * 4 + (base + 2), 0, s[0])
                    pe.wait_ge(ff_sq, i + (lay * FF + 1))
                    for q in range(2):
                        pe.wait_ge(tr_lo, i * 2 + (g0 + q - 1))
                        for kk in range(2):
                            for t in range(NT):
                                c = (2 * q + kk) * P
                                ins = pe.transpose(b_tr[(g0 + q) % 2][:, kk * S + t * P:kk * S + t * P + P],
                                                   hidden[:, t, c:c + P], ident[:])
                        ins.then_inc(tr_ready, 1)
                    if not last:
                        up(i * 4 + (base + 3), 1, s[1])
                    pe.wait_ge(tr_lo, i * 2 + (g0 + 2))
                    for c in range(2):
                        u, slot = (base + 4 * FF - 2 + c, (base + 4 * FF - 2 + c) % RING) if last else (i * 4 + (base + 4 + c), s[2 + c])
                        product(u, slot, b_hi, b_lo, 0, bank[2 * c:2 * c + 2], first, last)
                chunk(0, True, False)
                with pe.Fori(1, FF - 1) as i:
                    chunk(i, False, False)
                chunk(FF - 1, False, True)

            norm_of_x(6, G_MIX0)
            for c in range(2):
                dense(U_POOL + 2 * c, B_POOL + c, a_hi, a_lo)
            pe.wait_ge(free_a, freed(B_POOL + 1, "a"))
            pe.wait_ge(free_v, freed(B_POOL + 1, "v"))
            pe.wait_ge(pool_landed, 16 * 7)
            for g in range(4):
                for c in range(2):
                    if g:
                        pe.wait_ge(d_copied_v if c else d_copied_a, g)
                    cols = slice(g * GW + c * GC, g * GW + c * GC + GC)
                    pe.matmul((b_io, b_t)[c][0:GC, 0:S], h_pool[:, 0, cols], band[:, 0, g], start=True, stop=False)
                    pe.matmul((b_io, b_t)[c][0:GC, 0:S], h_pool[:, 1, cols], band[:, 1, g], start=False, stop=True)\
                      .then_inc(d_ready, 1)
            pe.wait_ge(d_copied_a, 4)
            pe.wait_ge(d_copied_v, 4)
            for t in range(NT):
                for g in range(4):
                    for c in range(2):
                        ins = pe.matmul(bank[2 * t + g // 2][:, g % 2 * GW:g % 2 * GW + GW], dT[:, g, c, t * P:t * P + P],
                                        w_group[:, g, c], start=c == 0, stop=c == 1)
            ins.then_inc(y_ready, 1)
            pe.wait_ge(y_made, 1)
            for g in range(3):
                group(G_TOK0 + g, tok, 2 * g)
            pe.wait_ge(tr_lo, G_TOK0 + 3)
            for s in run_steps(RUN2):
                step(RUN2, s)
            pe.wait_ge(pair_lo, 10)
            for c in range(2):
                dense(U_OUT0 + 2 * c, B_OUT0 + c, b_hi, b_lo)
            norm_of_x(8, G_MLP0)
            mlp(U_FF0, 0, G_FF0)
            norm_of_x(10, G_MIX1)
            for c in range(5):
                dense(U_MOBA + 2 * c, B_MOBA + c, a_hi, a_lo)
            for s in run_steps(RUN3):
                step(RUN3, s)
            pe.wait_ge(pair_lo, N_HEADS // 2)
            for c in range(2):
                dense(U_OUT1 + 2 * c, B_OUT1 + c, b_hi, b_lo)
            norm_of_x(12, G_MLP1)
            mlp(U_FF1, 1, G_FF1)


_CONSTANTS = ["c_ident", "c_mask", "c_tri", "c_rope_a", "c_rope_m", "c_band"]
_INS = ["x", "p", "w_in", "b_forget", "w_branch_a", "w_branch_b", "w_merge", "w_out", "g_pre", "g_post", "w_ple",
        "w_ple_gate", "g_ple", "mem_2", "g_mix_2", "g_mem_2", "g_mlp_2", "w_in_pool_2", "w_pool_group_2", "pool_scale_2",
        "w_in_moba_2", "moba_q_gain_2", "moba_k_gain_2", "w_mem_kv_2", "mem_q_gain_2", "mem_k_gain_2", "w_out_2",
        "w_ff1_2", "w_ff2_2"]


def constants():
    f = np.float32
    pos = np.arange(S, dtype=f)[:, None]
    ang_a = pos * (f(500000.0) ** (-np.arange(8, dtype=f) / f(8)))[None, :]
    ang_m = pos * (f(10000.0) ** (-np.arange(0, HD, 2, dtype=f) / f(HD)))[None, :]
    q, k = np.arange(P)[:, None], np.arange(P)[None, :]
    tri = np.concatenate([(q <= k), np.ones((P, P), bool)], axis=1)
    t = np.arange(S)[None, :]
    s = np.arange(S)[:, None]
    band = np.stack([((s <= t) & (s > t - w)) / np.minimum(t + 1, w) - (s == t) for w in (2, 4, 8, 16)])
    return {
        "c_ident": np.eye(P, dtype=f),
        "c_mask": np.where(k <= q, 0.0, NEG).astype(f),
        "c_tri": tri.astype(f),
        "c_rope_a": np.stack([np.cos(ang_a), np.sin(ang_a)]).astype(f),
        "c_rope_m": np.stack([np.cos(ang_m), np.sin(ang_m)]).astype(f),
        "c_band": band.astype(f),
    }


def kernel(**inputs):
    from concourse import bacc
    from concourse.bass_utils import run_bass_kernel_spmd

    nc = bacc.Bacc("TRN2", target_bir_lowering=False, num_devices=1)
    arrays, args = {}, {}
    for name, value in [(n, inputs[n]) for n in _INS] + list(constants().items()):
        value = np.ascontiguousarray(value)
        arrays[f"in_{name}"] = value
        args[name] = nc.dram_tensor(f"in_{name}", value.shape, mybir.dt.from_np(value.dtype), kind="ExternalInput").ap()
    out = nc.dram_tensor("out_x", (1, S, D), F32, kind="ExternalOutput").ap()
    build(nc, args, out)
    r = run_bass_kernel_spmd(nc, [arrays], core_ids=[0])
    return r.results[0]["out_x"]
```

```python
from contextlib import ExitStack

import numpy as np

import concourse.bass as bass
from concourse import mybir

ALU = mybir.AluOpType
ACT = mybir.ActivationFunctionType
AX = mybir.AxisListType
F32 = mybir.dt.float32
F32R = mybir.dt.float32r
BF16 = mybir.dt.bfloat16

P = 128
S = 256
NT = S // P
D = 1024
KT = D // P
HD = 64
WA = 512
DIN = 3792
IN_BLOCKS = [(1152 + 440 * b, 440) for b in range(6)] + [(384 * b, 384) for b in range(3)]
NBLK_IN = len(IN_BLOCKS)
NBLK_LOOP = 4
CIN = IN_BLOCKS[0][1]
CB = 512
UNIT = 4 * CB
EPS = 1e-6
NEG = -1e30
TOPK = S // 4
SCALE = HD ** -0.5
IDX_SCALE = (8 ** -0.5) * (64 ** -0.5)
FILL = 1e8
TAKEN = -3.4e38
QA, KA, VA, GA, QI, KI, WI, QB, KB, VB, FB, GB = 0, 512, 576, 640, 1152, 1664, 1728, 1736, 2248, 2760, 3272, 3280
TOKW = 768
GW = TOKW // 4
GC = GW // 2
FF = 8
LOOK = 3
RAW = 2
RING = 4

U_IN = 0
U_MERGE = U_IN + 2 * NBLK_IN
U_BR = U_MERGE + 8
U_WO = U_BR + 4
U_PLE = U_WO + 4
U_GATE = U_PLE + 1
U_KV0 = U_GATE + 4
U_POOL = U_KV0 + 2
U_OUT0 = U_POOL + 4
U_FF0 = U_OUT0 + 4
U_MOBA0 = U_FF0 + 4 * FF
U_KV1 = U_MOBA0 + 2
U_MOBA = U_KV1 + 2
U_OUT1 = U_MOBA + 8
U_FF1 = U_OUT1 + 4
N_UNITS = U_FF1 + 4 * FF
N_SMALL = 10
N_EARLY = 5

HEADS = [("fox", j) for j in range(8)] + [("dsa", j) for j in range(8)] + [("mem0", j) for j in range(4)] \
    + [("mem1", j) for j in range(4)] + [("moba", j) for j in range(12)]
N_HEADS = len(HEADS)


def width0(h):
    return S if HEADS[h][0].startswith("mem") else P


RUN1 = [("idx", j) for j in range(8)] + list(range(16))
RUN2 = list(range(16, 20))
RUN3 = list(range(20, N_HEADS))
LAG_P, LAG_T, LAG_V = 1, 2, 3


def pair_of(run, pr):
    first = run[2 * pr]
    return ("idx", first[1] // 2) if isinstance(first, tuple) else (HEADS[first][0], first // 2)


def parts_at(run, s):
    out = []
    n_pairs = len(run) // 2
    nxt = (s + 1) // 2 if s % 2 else s // 2 + 1
    if s < 0:
        nxt = 0
    if nxt < n_pairs:
        kind, pr = pair_of(run, nxt)
        before = pair_of(run, nxt - 1)[0] if nxt else ""
        if s < 0 or s % 2 == 0:
            out.append(("qi" if kind == "idx" else "q", pr))
        if s < 0 or s % 2:
            if kind == "idx":
                out += [("ki", 0)] if nxt == 0 else []
            elif kind == "dsa":
                out += [("ka", 0)] if before != "dsa" else []
            else:
                out.append(("k", pr))
    if s >= 3 and s % 2:
        kind, pr = pair_of(run, (s - 3) // 2)
        if kind in ("fox", "dsa"):
            out.append(("gate", pr))
    return out


def run_steps(run):
    return range(-1, len(run) + LAG_V)


PARTS = [part for run in (RUN1, RUN2, RUN3) for s in run_steps(run) for part in parts_at(run, s)]
PART = {part: n for n, part in enumerate(PARTS)}
PART_SLOT = {part: n % 2 for n, part in enumerate(q for q in PARTS if q[0] in ("qi", "q"))}
PART_SLOT.update({("k", pr): PART_SLOT[("q", pr)] for what, pr in PARTS if what == "k"})
GATES = [pr for what, pr in PARTS if what == "gate"]

BLOCKS = ["in"] * NBLK_IN + ["merge"] * 4 + ["brb"] * 2 + ["bra"] * 2 + ["wo"] * 2 + ["ple"] * 2 + ["gate"] * 2 \
    + ["kv"] + ["pool"] * 2 + ["out"] * 2 + ["moba", "kv"] + ["moba"] * 4 + ["out"] * 2
READERS = {"in": "av", "merge": "a", "kv": "av", "brb": "v", "bra": "v", "wo": "v", "ple": "a", "gate": "a",
           "pool": "av", "out": "", "moba": "av"}
B_MERGE = NBLK_IN
B_BR, B_WO, B_PLE, B_GATE, B_KV0, B_POOL, B_OUT0, B_MOBA0, B_KV1, B_MOBA, B_OUT1 = (
    B_MERGE + n for n in (4, 8, 10, 12, 14, 15, 17, 19, 20, 21, 25))
BANK_OF = {k: 0 for k in (*range(NBLK_LOOP + 1, B_BR + 2), *range(B_MOBA0, B_OUT1 + 1))}
BANK_OF |= {B_BR + 2: 2, B_BR + 3: 0, B_WO: 2, B_WO + 1: 0, B_PLE: 4, B_PLE + 1: 6, B_GATE: 2, B_GATE + 1: 0,
            B_KV0: 2, B_POOL: 2, B_POOL + 1: 0, B_OUT0: 0, B_OUT0 + 1: 2, B_KV1: 2, B_OUT1 + 1: 2}


def pair_bank(k):
    return BANK_OF.get(k, 2 * (k % 2))


def freed(k, engine):
    return 2 + sum(engine in READERS[b] for b in BLOCKS[:k + 1])


def fill_of(run, s):
    def unit_of(first, block, n):
        return [(first + n, block + n // 2, n % 2)]
    if run is RUN1:
        if 0 <= s < 2:
            return unit_of(U_IN + 10, 5, s)
        if 8 <= s < 14:
            return unit_of(U_IN + 12, 6, s - 8)
        if 14 <= s < 22:
            return unit_of(U_MERGE, B_MERGE, s - 14)
        if 22 <= s < 24:
            return [(U_BR + s - 22, B_BR + s - 22, 2)]
    if run is RUN2:
        return [(U_POOL + 3, B_POOL + 1, 1)] if s == 0 else []
    if run is RUN3:
        if s in MOBA_FILL:
            return unit_of(U_MOBA + 2, B_MOBA + 1, MOBA_FILL.index(s))
        return [(U_OUT1, B_OUT1, 0)] if s == 15 else []
    return []


MOBA_FILL = [0, 1, 3, 4, 6, 8]
MOBA_BLOCKS = [(0, 9), (3, 6), (1, 4), (2, 7), (5, 8)]
MOBA_AT = {piece: 256 * n for n, piece in enumerate(q for b in MOBA_BLOCKS for q in b)}

G_H = 0
G_MERGED = G_H + 4
G_P = G_MERGED + 4
G_X = G_P + 1
G_MEM0 = G_X + 4
G_MIX0 = G_MEM0 + 4
G_TOK0 = G_MIX0 + 4
G_MLP0 = G_TOK0 + 3
G_FF0 = G_MLP0 + 4
G_MIX1 = G_FF0 + 2 * FF
G_MEM1 = G_MIX1 + 4
G_MLP1 = G_MEM1 + 4
G_FF1 = G_MLP1 + 4
X_PLE, X_OUT0, X_FF0, X_OUT1, X_FF1 = 0, 2, 4, 6, 8
GAIN_PRE, GAIN_MIX, GAIN_MEM, GAIN_MLP = 0, 8, 24, 40


def build(nc, a, out):
    with ExitStack() as ctx:
        def sb(name, shape, dt=F32):
            return ctx.enter_context(nc.sbuf_tensor(name, shape, dt))

        def sem(name):
            return ctx.enter_context(nc.semaphore(name))

        raw = sb("raw", [P, RAW, UNIT])
        w_hi = sb("w_hi", [P, RING, UNIT], F32R)
        w_lo = sb("w_lo", [P, RING, UNIT], F32R)
        x = sb("x", [P, NT, D])
        tok = sb("tok", [P, NT, D])
        a_hi = sb("a_hi", [P, KT, S], F32R)
        a_lo = sb("a_lo", [P, KT, S], F32R)
        b_hi = sb("b_hi", [P, KT, S], F32R)
        b_lo = sb("b_lo", [P, KT, S], F32R)
        proj = sb("proj", [P, NT * DIN])
        m = sb("m", [P, NT * 2 * D])
        qk = sb("qk", [P, 2, 2, S])
        kT = sb("kT", [P, S])
        memkv = sb("memkv", [P, 2, NT, CB])
        ident = sb("ident", [P, P])
        ident_b = sb("ident_b", [P, P], BF16)
        mask = sb("mask", [P, P])
        mask_b = sb("mask_b", [P, P], BF16)
        tri = sb("tri", [P, S])
        rope_a = sb("rope_a", [P, 2, NT, 8])
        rope_m = sb("rope_m", [P, 2, NT, 32])
        gain_rows = sb("gain_rows", [56, P])
        gain_cols = sb("gain_cols", [P, 56])
        gain_bc = sb("gain_bc", [P, D])
        head_gain = sb("head_gain", [P, 6, HD])
        bias_f = sb("bias_f", [P, 8])
        prob = sb("prob", [P, 2, 2 * S])
        probT = sb("probT", [P, 2, 2 * S])
        top8 = sb("top8", [P, NT, 8])
        sel_b = sb("sel_b", [P, P + S], BF16)
        wis = sb("wis", [P, NT, 8])
        fgt = sb("fgt", [P, 6, NT, 8])
        mx = sb("mx", [P, N_HEADS, NT])
        nmx = sb("nmx", [P, N_HEADS, NT])
        psums = sb("psums", [P, N_HEADS, NT])
        prec = sb("prec", [P, N_HEADS, NT])
        stat = sb("stat", [P, 4, 8, 2 * NT])
        hstat = sb("hstat", [P, 2, 2, NT * 4])
        half = sb("half", [P, NT * 4])

        bank = [ctx.enter_context(nc.psum_tensor(f"bank{i}", [P, 512], F32)) for i in range(8)]
        b_t, b_io, b_s, b_v, b_tr = bank[2], bank[3], bank[4:6], bank[7], bank[6:8]

        def group_bank(g):
            return b_tr[g % 2]

        pj = proj[:].rearrange("p (t n) -> p t n", t=NT)
        xf = x[:].rearrange("p t n -> p (t n)")
        score, gate_s, gated, cT = xf[:, 0:P + S], xf[:, 384:640], xf[:, 640:896], xf[0:8, 896:1152]
        rope_t = xf[:, 1152:1728].rearrange("p (q t n d) -> p q t n d", q=4, t=NT, n=9)
        k_twice = xf[:, 1728:1984].rearrange("p (t q d) -> p t q d", t=NT, q=2)
        mem_tmp = probT[:, 0, :]
        p_tok = prob[:, :, 0:S]
        m_sig = m[:].rearrange("p (t n) -> p t n", t=NT)
        e_tok = m[:, 0:NT * D].rearrange("p (t n) -> p t n", t=NT)
        m_lo = m[:, 0:NT * D].rearrange("p (t n) -> p t n", t=NT)
        m_hi = m[:, NT * D:].rearrange("p (t n) -> p t n", t=NT)
        band = m[:, 0:NT * 4 * S].rearrange("p (t g n) -> p t g n", t=NT, g=4)
        w_group = m[0:GC, NT * 4 * S:NT * 4 * S + 8 * GW].rearrange("p (g c n) -> p g c n", g=4, c=2)
        h_pool = proj[:, 0:NT * D].rearrange("p (t n) -> p t n", t=NT)
        dT = proj[0:GC, NT * D:NT * D + 8 * S].rearrange("p (g c n) -> p g c n", g=4, c=2)
        h_moba = proj[:, 0:NT * 2560].rearrange("p (t n) -> p t n", t=NT)
        hidden = tok[:, :, 0:CB]

        raw_landed = [sem(f"raw_landed{i}") for i in range(RAW)]
        hi_ready, lo_ready, unit_used = sem("hi_ready"), sem("lo_ready"), sem("unit_used")
        free_a, free_v = sem("banks_free_a"), sem("banks_free_v")
        tr_ready, tr_hi, tr_lo = sem("tr_ready"), sem("tr_hi"), sem("tr_lo")
        x_landed, const_landed, mem_landed, p_landed, bc_landed = (sem(n) for n in (
            "x_landed", "const_landed", "mem_landed", "p_landed", "bc_landed"))
        pool_landed, x_again, out_landed = sem("pool_landed"), sem("x_again"), sem("out_landed")
        consts_made, gains_tr, gains_made = sem("consts_made"), sem("gains_tr"), sem("gains_made")
        sq_done, rstd_done = sem("sq_done"), sem("rstd_done")
        part_tr, part_cp, gate_cp = sem("part_tr"), sem("part_cp"), sem("gate_cp")
        idx_s, idx_relu, idx_acc, sel_made = sem("idx_s"), sem("idx_relu"), sem("idx_acc"), sem("sel_made")
        rope_idx, rope_dsa = sem("rope_idx"), sem("rope_dsa")
        f_abs, f_ln, f_log, c_ready, c_made = sem("f_abs"), sem("f_ln"), sem("f_log"), sem("c_ready"), sem("c_made")
        s_ready, max_done, exp_done, p_ready, pt_ready, pt_copied, pv_done, pair_read = (sem(n) for n in (
            "s_ready", "max_done", "exp_done", "p_ready", "pt_ready", "pt_copied", "pv_done", "pair_read"))
        pair_tmp, pair_hi, pair_lo = sem("pair_tmp"), sem("pair_hi"), sem("pair_lo")
        memk_made, memq_made, moba_made = sem("memk_made"), sem("memq_made"), sem("moba_made")
        early_landed, half_rstd, x_half = sem("early_landed"), sem("half_rstd"), sem("x_half")
        merge_sig, merged, x_post, z_made = sem("merge_sig"), sem("merged"), sem("x_post"), sem("z_made")
        ple_block, d_copied_a, d_copied_v = sem("ple_block"), sem("d_copied_a"), sem("d_copied_v")
        d_ready, y_ready, y_made = sem("d_ready"), sem("y_ready"), sem("y_made")
        ff_relu, ff_sq = sem("ff_relu"), sem("ff_sq")
        act_chain, vec_chain, pool_chain = sem("act_chain"), sem("vec_chain"), sem("pool_chain")

        class Linker:

            def __init__(self, eng, chain):
                self.eng, self.chain, self.n = eng, chain, 0

            def step(self):
                self.n += 1
                return self.chain, 1

            def wait(self):
                self.eng.wait_ge(self.chain, self.n)

            def __call__(self, ins):
                ins.then_inc(*self.step())
                self.wait()

        def head_cols(h):
            kind, j = HEADS[h]
            pr = j // 2
            h0 = pj[:, :, :]
            pool = proj[:, 0:NT * D].rearrange("p (t n) -> p t n", t=NT)
            if kind == "fox":
                return dict(q=h0[:, :, QB + P * pr:QB + P * pr + P], k=h0[:, :, KB + P * pr:KB + P * pr + P],
                            gate=h0[:, :, GB + P * pr:GB + P * pr + P], v=h0[:, :, VB + HD * j:VB + HD * j + HD])
            if kind == "dsa":
                return dict(q=h0[:, :, QA + P * pr:QA + P * pr + P], gate=h0[:, :, GA + P * pr:GA + P * pr + P],
                            v=h0[:, :, VA:VA + HD])
            if kind == "moba":
                q, k, v = (MOBA_AT[j // 4 + 3 * n] for n in range(3))
                c = P * (pr % 2)
                return dict(q=h_moba[:, :, q + c:q + c + P], k=h_moba[:, :, k + c:k + c + P],
                            v=h_moba[:, :, v + HD * (j % 4):v + HD * (j % 4) + HD])
            lay = int(kind[3])
            src = pool[:, :, TOKW:] if lay == 0 else h_moba[:, :, MOBA_AT[9]:MOBA_AT[9] + S]
            return dict(q=src[:, :, P * pr:P * pr + P], k=memkv[:, lay, :, P * pr:P * pr + P],
                        v=memkv[:, lay, :, S + HD * j:S + HD * j + HD])

        def pair_ktile(pr):
            kind, j = HEADS[2 * pr]
            return {"fox": 4, "dsa": 0, "mem0": 6, "moba": 0, "mem1": 6}[kind] + j // 2

        def unit_source(u):
            def cut(w, half_, c, n=CB):
                return w.rearrange("(k p) n -> p k n", p=P)[:, 4 * half_:4 * half_ + 4, c * n:c * n + n]
            if u < U_MERGE:
                c, n = IN_BLOCKS[u // 2]
                return a["w_in"][0].rearrange("(k p) n -> p k n", p=P)[:, 4 * (u % 2):4 * (u % 2) + 4, c:c + n]
            if U_MERGE <= u < U_BR:
                return cut(a["w_merge"][0], u % 2, (u - U_MERGE) // 2)
            if U_BR <= u < U_WO:
                return cut(a["w_branch_b" if u < U_BR + 2 else "w_branch_a"][0], 0, (u - U_BR) % 2)
            if U_WO <= u < U_PLE:
                return cut(a["w_out"][0], (u - U_WO) % 2, (u - U_WO) // 2)
            if u == U_PLE:
                return a["w_ple"][0].rearrange("(k p) n -> p k n", p=P)
            if U_GATE <= u < U_KV0:
                return cut(a["w_ple_gate"][0], (u - U_GATE) % 2, (u - U_GATE) // 2)
            if U_KV0 <= u < U_POOL:
                return cut(a["w_mem_kv_2"][0], u - U_KV0, 0)
            if U_POOL <= u < U_OUT0:
                return cut(a["w_in_pool_2"][0], (u - U_POOL) % 2, 1 - (u - U_POOL) // 2)
            if U_OUT0 <= u < U_FF0:
                return cut(a["w_out_2"][0], (u - U_OUT0) % 2, (u - U_OUT0) // 2)
            if U_MOBA0 <= u < U_OUT1 and not U_KV1 <= u < U_MOBA:
                n = u - U_MOBA0 if u < U_KV1 else u - U_MOBA + 2
                i, j = MOBA_BLOCKS[n // 2]
                w = a["w_in_moba_2"][0].rearrange("(k p) (j n) -> p k j n", p=P, n=S)
                return w[:, 4 * (n % 2):4 * (n % 2) + 4, i:j + 1:j - i, :]
            if U_KV1 <= u < U_MOBA:
                return cut(a["w_mem_kv_2"][1], u - U_KV1, 0)
            if U_OUT1 <= u < U_FF1:
                return cut(a["w_out_2"][1], (u - U_OUT1) % 2, (u - U_OUT1) // 2)
            base, lay = (U_FF0, 0) if u < U_MOBA0 else (U_FF1, 1)
            r = u - base
            if r < 2:
                return cut(a["w_ff1_2"][lay], r, 0)
            i, r = divmod(r - 2, 4)
            if r < 2 and i < FF - 1:
                return cut(a["w_ff1_2"][lay], r, i + 1)
            return a["w_ff2_2"][lay].rearrange("(i k p) n -> p i k n", p=P, k=4)[:, i, :, (r % 2) * CB:(r % 2) * CB + CB]

        def landed(u):
            two = [v for v in range(U_MOBA0, min(u + 1, U_OUT1)) if not U_KV1 <= v < U_MOBA and v % RAW == u % RAW]
            return u // RAW + 1 + len(two)

        def unit_size(u):
            return 4 * IN_BLOCKS[u // 2][1] if u < U_MERGE else UNIT

        def head_squares(eng, link, v, n, slot, tmp):
            sq = tmp.rearrange("p (t n d) -> p t n d", t=NT, d=HD)
            link(eng.tensor_tensor(sq, v, v, ALU.mult))
            for w in (32, 16, 8, 4, 2, 1):
                link(eng.tensor_tensor(sq[:, :, :, 0:w], sq[:, :, :, 0:w], sq[:, :, :, w:2 * w], ALU.add))
            mean = hstat[:, slot, 0, 0:NT * n].rearrange("p (t n) -> p t n", t=NT)
            return eng.tensor_scalar(mean, sq[:, :, :, 0], 1.0 / HD, EPS, ALU.mult, ALU.add)

        def head_rstd(eng, n, slot):
            return eng.tensor_tensor(hstat[:, slot, 1, 0:NT * n], hstat[:, slot, 0, 0:NT * n], half[:, 0:NT * n], ALU.pow)

        def head_scale(eng, link, v, n, gain, slot):
            r = hstat[:, slot, 1, 0:NT * n].rearrange("p (t n) -> p t n", t=NT)
            for t in range(NT):
                eng.tensor_tensor(v[:, t], v[:, t], r[:, t].unsqueeze(2).to_broadcast([P, n, HD]), ALU.mult)\
                   .then_inc(*link.step())
            link.wait()
            for t in range(NT):
                eng.tensor_tensor(v[:, t], v[:, t], gain.unsqueeze(1).to_broadcast([P, n, HD]), ALU.mult)\
                   .then_inc(*link.step())
            link.wait()

        def rotate_heads(eng, link, v, n, tmp):
            old = tmp.rearrange("p (q t n d) -> p q t n d", q=2, t=NT, d=HD // 2)
            x1, x2 = v[:, :, :, 0:HD // 2], v[:, :, :, HD // 2:HD]
            for t in range(NT):
                cs, sn = (rope_m[:, q, t, :].unsqueeze(1).to_broadcast([P, n, HD // 2]) for q in range(2))
                eng.tensor_tensor(old[:, 0, t], x1[:, t], sn, ALU.mult).then_inc(*link.step())
                eng.tensor_tensor(old[:, 1, t], x2[:, t], sn, ALU.mult).then_inc(*link.step())
                link.wait()
                eng.tensor_tensor(x1[:, t], x1[:, t], cs, ALU.mult).then_inc(*link.step())
                eng.tensor_tensor(x2[:, t], x2[:, t], cs, ALU.mult).then_inc(*link.step())
                link.wait()
                eng.tensor_tensor(x1[:, t], x1[:, t], old[:, 1, t], ALU.subtract).then_inc(*link.step())
                eng.tensor_tensor(x2[:, t], x2[:, t], old[:, 0, t], ALU.add).then_inc(*link.step())
            link.wait()

        block = ctx.enter_context(nc.Block())

        @block.sync
        def _(sp):
            def load(u, slot, src, n):
                if not isinstance(u, int) or u >= RAW:
                    sp.wait_ge(lo_ready, u - RAW + 1)
                if len(src.shape) == 3:
                    sp.dma_start(raw[:, slot, 0:n].rearrange("p (k n) -> p k n", k=src.shape[1]), src)\
                        .then_inc(raw_landed[slot], 16)
                else:
                    dst = raw[:, slot, 0:n].rearrange("p (k j n) -> p k j n", k=src.shape[1], j=2)
                    for j in range(2):
                        sp.dma_start(dst[:, :, j, :], src[:, :, j, :]).then_inc(raw_landed[slot], 16)

            def load_plain(first, last):
                for u in range(first, last):
                    load(u, u % RAW, unit_source(u), unit_size(u))

            for t in range(NT):
                sp.dma_start(x[:, t, :], a["x"][0, t * P:(t + 1) * P, :]).then_inc(x_landed, 16)
            w_in = a["w_in"][0].rearrange("(k p) n -> p k n", p=P)
            load_plain(0, 2)
            with sp.Fori(1, NBLK_LOOP) as b:
                for r in range(2):
                    load(2 * b + r, r, w_in[:, 4 * r:4 * r + 4, bass.ds(b * CIN + IN_BLOCKS[0][0], CIN)], 4 * CIN)

            def mlp(base, lay):
                w1 = a["w_ff1_2"][lay].rearrange("(k p) n -> p k n", p=P)
                w2 = a["w_ff2_2"][lay].rearrange("(i k p) n -> p i k n", p=P, k=4)
                load_plain(base, base + 2)
                with sp.Fori(0, FF - 1) as i:
                    for r in range(2):
                        load(base + 2 + 4 * i + r, (base + r) % RAW,
                             w1[:, 4 * r:4 * r + 4, bass.ds(i * CB + CB, CB)], UNIT)
                    for r in range(2):
                        src = w2[:, bass.ds(i, 1), :, r * CB:r * CB + CB].rearrange("p i k n -> p (i k) n")
                        load(base + 4 + 4 * i + r, (base + r) % RAW, src, UNIT)
                load_plain(base + 4 * FF - 2, base + 4 * FF)

            load_plain(2 * NBLK_LOOP, U_FF0)
            mlp(U_FF0, 0)
            load_plain(U_MOBA0, U_FF1)
            mlp(U_FF1, 1)
            for c in range(2):
                sp.wait_ge(x_half, X_FF1 + c + 1)
                sp.dma_start(out[0].rearrange("(t p) n -> p t n", p=P)[:, :, c * CB:c * CB + CB],
                             x[:, :, c * CB:c * CB + CB]).then_inc(out_landed, 16)
            sp.wait_ge(out_landed, 16 * NT)

        @block.gpsimd
        def _(gp):
            link = Linker(gp, pool_chain)
            small = [(mask[:], a["c_mask"]), (tri[:], a["c_tri"]),
                     (bias_f[:], a["b_forget"][0].partition_broadcast(P)),
                     (rope_a[:], a["c_rope_a"].rearrange("c (t p) n -> p c t n", p=P)),
                     (rope_m[:], a["c_rope_m"].rearrange("c (t p) n -> p c t n", p=P)),
                     (head_gain[:, 0, :], a["moba_q_gain_2"][0].partition_broadcast(P)),
                     (head_gain[:, 1, :], a["moba_k_gain_2"][0].partition_broadcast(P)),
                     (head_gain[:, 2:4, :], a["mem_q_gain_2"].partition_broadcast(P)),
                     (head_gain[:, 4:6, :], a["mem_k_gain_2"].partition_broadcast(P)),
                     (gain_bc[:], a["g_post"][0].partition_broadcast(P))]
            link(gp.memset(half[:], -0.5))

            def rstd(r, count, cols, eps):
                link(gp.tensor_scalar(stat[:, 1, r, 0:cols], stat[:, 0, r, 0:cols], 1.0 / count, eps, ALU.mult, ALU.add))
                gp.tensor_tensor(stat[:, 2, r, 0:cols], stat[:, 1, r, 0:cols], half[:, 0:cols], ALU.pow).then_inc(rstd_done, 1)

            gp.wait_ge(sq_done, 2)
            rstd(0, D, NT, EPS)
            gp.wait_ge(rstd_done, 1)
            gp.tensor_scalar(stat[:, 3, 0, 0:NT], stat[:, 2, 0, 0:NT], 0.5, None, ALU.mult).then_inc(half_rstd, 1)
            for dst, src in small:
                gp.dma_start(dst, src).then_inc(const_landed, 16)
            assert len(small) == N_SMALL

            def blocks_read(k):
                gp.wait_ge(free_a, freed(k, "a"))
                gp.wait_ge(free_v, freed(k, "v"))

            def rotate(c0, done):
                v = pj[:, :, c0:c0 + 9 * HD].rearrange("p t (n d) -> p t n d", d=HD)
                x1, x2 = v[:, :, :, 0:8], v[:, :, :, 8:16]
                for t in range(NT):
                    cs, sn = (rope_a[:, q, t, :].unsqueeze(1).to_broadcast([P, 9, 8]) for q in range(2))
                    for q, (src, f) in enumerate(((x1, cs), (x2, sn), (x2, cs), (x1, sn))):
                        gp.tensor_tensor(rope_t[:, q, t], src[:, t], f, ALU.mult).then_inc(*link.step())
                link.wait()
                gp.tensor_tensor(x1, rope_t[:, 0], rope_t[:, 1], ALU.subtract).then_inc(*link.step())
                gp.tensor_tensor(x2, rope_t[:, 2], rope_t[:, 3], ALU.add).then_inc(*link.step())
                link.wait()
                if done is rope_dsa:
                    gp.wait_ge(part_tr, PART[("ki", 0)] + 1)
                for q in range(2):
                    gp.tensor_copy(k_twice[:, :, q, :], pj[:, :, c0 + 8 * HD:c0 + 9 * HD]).then_inc(*link.step())
                link.wait()
                gp.sem_inc(done, 1)

            gp.wait_ge(const_landed, 16 * N_SMALL)
            blocks_read(1)
            rotate(QI, rope_idx)
            blocks_read(7)
            rotate(QA, rope_dsa)
            gp.wait_ge(pt_ready, 16)
            gp.wait_ge(pt_copied, 16)
            gp.dma_start(p_tok, a["p"][0, 0].rearrange("(t p) n -> p t n", p=P)).then_inc(p_landed, 16)
            gp.wait_ge(pair_lo, 8)
            gp.dma_start(x[:], a["x"][0].rearrange("(t p) n -> p t n", p=P)).then_inc(x_again, 16)
            gp.wait_ge(tr_ready, G_MERGED + 4)
            gp.dma_start(tok[:], a["mem_2"][0].rearrange("(t p) n -> p t n", p=P)).then_inc(mem_landed, 16)

            def rstd_of_halves(r, eps):
                gp.wait_ge(sq_done, 2 * r + 2)
                link(gp.tensor_tensor(stat[:, 0, r, 0:NT], stat[:, 0, r, 0:NT], stat[:, 0, r, NT:2 * NT], ALU.add))
                rstd(r, D, NT, eps)

            gp.wait_ge(sq_done, 4)
            rstd(1, D, NT, EPS)
            rstd_of_halves(2, EPS)
            gp.wait_ge(x_post, 2)
            gp.dma_start(gain_bc[:], a["g_ple"][0].partition_broadcast(P)).then_inc(bc_landed, 16)
            rstd_of_halves(3, 4 * EPS)

            def mem_keys(lay, k):
                blocks_read(k)
                v = memkv[:, lay, :, 0:S].rearrange("p t (n d) -> p t n d", d=HD)
                link(head_squares(gp, link, v, 4, 0, mem_tmp))
                link(head_rstd(gp, 4, 0))
                head_scale(gp, link, v, 4, head_gain[:, 4 + lay, :], 0)
                gp.sem_inc(memk_made, 1)

            def mem_queries(lay, k, v):
                blocks_read(k)
                v = v.rearrange("p t (n d) -> p t n d", d=HD)
                link(head_squares(gp, link, v, 4, 0, mem_tmp))
                link(head_rstd(gp, 4, 0))
                head_scale(gp, link, v, 4, head_gain[:, 2 + lay, :], 0)
                gp.sem_inc(memq_made, 1)

            mem_keys(0, B_KV0)
            gp.wait_ge(x_half, X_PLE + 2)
            gp.dma_start(gain_bc[:, 0:TOKW], a["pool_scale_2"][0].partition_broadcast(P)).then_inc(pool_landed, 16)
            gp.wait_ge(sq_done, 10)
            rstd(4, D, NT, EPS)
            for t in range(NT):
                gp.dma_start(band[:, t], a["c_band"][:, t * P:(t + 1) * P, :].rearrange("g p n -> p g n"))\
                    .then_inc(pool_landed, 16)
            for g in range(4):
                gp.dma_start(w_group[:, g], a["w_pool_group_2"][0, g].rearrange("(c p) n -> p c n", p=GC))\
                    .then_inc(pool_landed, 16)
            mem_queries(0, B_POOL, h_pool[:, :, TOKW:D])
            gp.wait_ge(sq_done, 12)
            rstd(5, D, NT, EPS)
            gp.wait_ge(tr_ready, G_FF0 + 2 * FF)
            gp.dma_start(tok[:], a["mem_2"][0].rearrange("(t p) n -> p t n", p=P)).then_inc(mem_landed, 16)
            gp.wait_ge(sq_done, 14)
            rstd(6, D, NT, EPS)
            mem_queries(1, B_MOBA0, h_moba[:, :, MOBA_AT[9]:MOBA_AT[9] + S])
            mem_keys(1, B_KV1)
            for n, (kq, kk) in enumerate(((B_MOBA0, B_MOBA), (B_MOBA + 1, B_MOBA + 1), (B_MOBA + 2, B_MOBA + 3))):
                for q, k in ((0, kq), (1, kk)):
                    blocks_read(k)
                    c = MOBA_AT[n + 3 * q]
                    v = h_moba[:, :, c:c + S].rearrange("p t (n d) -> p t n d", d=HD)
                    link(head_squares(gp, link, v, 4, q, m[:, 0:NT * S]))
                    link(head_rstd(gp, 4, q))
                    head_scale(gp, link, v, 4, head_gain[:, q, :], q)
                    rotate_heads(gp, link, v, 4, m[:, NT * S:2 * NT * S])
                    gp.sem_inc(moba_made, 1)
            gp.wait_ge(sq_done, 16)
            rstd(7, D, NT, EPS)

        @block.scalar
        def _(act):
            def split(u, slot, land, n):
                act.wait_ge(raw_landed[land], 16 * landed(u))
                if u >= RING:
                    act.wait_ge(unit_used, u - RING + 2)
                act.activation(w_hi[:, slot, 0:n], raw[:, land, 0:n], ACT.Copy).then_inc(hi_ready, 1)

            def unit(u):
                v = u + LOOK
                if v < N_UNITS:
                    split(v, v % RING, v % RAW, unit_size(v))

            def group(g, dst, k, gain=None):
                act.wait_ge(tr_ready, g + 1)
                ps = group_bank(g)
                if gain is None:
                    act.activation(dst[:, k:k + 2, :], ps[:, :].rearrange("p (k n) -> p k n", k=2), ACT.Copy)\
                       .then_inc(tr_hi, 1)
                else:
                    act.activation(dst[:, k, :], ps[:, 0:S], ACT.Copy, scale=gain_cols[:, gain + k:gain + k + 1])
                    act.activation(dst[:, k + 1, :], ps[:, S:2 * S], ACT.Copy,
                                   scale=gain_cols[:, gain + k + 1:gain + k + 2]).then_inc(tr_hi, 1)

            def groups(g0, first, dst, gain=None):
                for q in range(first, first + 2):
                    group(g0 + q, dst, 2 * q, gain)

            def squares(r, src, junk):
                for t in range(NT):
                    act.activation(junk[t], src[:, t], ACT.Square, accum_out=stat[:, 0, r, t:t + 1])\
                       .then_inc(sq_done, 1)

            def squares_half(r, c, src):
                for t in range(NT):
                    ins = act.activation(m_hi[:, t, c * CB:c * CB + CB], src[t], ACT.Square,
                                         accum_out=stat[:, 0, r, NT * c + t:NT * c + t + 1])
                    if c == 1:
                        ins.then_inc(sq_done, 1)

            def x_squares(r, count, junk):
                act.wait_ge(x_half, count)
                squares(r, x, [junk[:, t] for t in range(NT)])

            def block_done(u):
                act.wait_ge(unit_used, u + 2)

            def scaled(dst, k, r, n=CB):
                act.wait_ge(rstd_done, r + 1)
                act.activation(dst, bank[pair_bank(k)][:, 0:n], ACT.Copy, scale=stat[:, 2, r, 0:1]).then_inc(free_a, 1)

            def evac(k):
                kind = BLOCKS[k]
                if kind == "in":
                    c, n = IN_BLOCKS[k]
                    scaled(pj[:, 0, c:c + n], k, 0, n)
                if kind == "merge":
                    c = (k - B_MERGE) * CB
                    for t in range(NT):
                        ins = act.activation(m_sig[:, t, c:c + CB], bank[pair_bank(k) + t][:, :], ACT.Tanh,
                                             scale=stat[:, 3, 0, t:t + 1])
                    ins.then_inc(free_a, 1)
                if kind == "kv":
                    scaled(memkv[:, int(k == B_KV1), 0, :], k, 1)
                if kind == "pool":
                    c = (1 - (k - B_POOL)) * CB
                    scaled(h_pool[:, 0, c:c + CB], k, 4)
                if kind == "moba":
                    c = (0 if k == B_MOBA0 else k - B_MOBA + 1) * CB
                    scaled(h_moba[:, 0, c:c + CB], k, 6)

            def dense(u, k):
                unit(u)
                unit(u + 1)
                block_done(u + 1)
                evac(k)

            def fill(run, s):
                for u, k, half_ in fill_of(run, s):
                    unit(u)
                    if half_ and BLOCKS[k] != "brb":
                        block_done(u)
                        evac(k)

            def part(what, pr):
                act.wait_ge(part_tr, PART[(what, pr)] + 1)
                ps = b_io[:, 0:S]
                if what == "gate":
                    if GATES.index(pr):
                        act.wait_ge(pair_lo, GATES.index(pr))
                    act.activation(gated[:], ps, ACT.Tanh, scale=0.5).then_inc(part_cp, 1)
                    return
                dst = {"ki": kT[:], "ka": kT[:]}.get(what)
                if dst is None:
                    dst = qk[:, PART_SLOT[(what, pr)], 0 if what in ("qi", "q") else 1, :]
                act.activation(dst, ps, ACT.Copy).then_inc(part_cp, 1)

            def step(run, s):
                for what in parts_at(run, s):
                    part(*what)
                if 0 <= s < len(run):
                    h = run[s]
                    if isinstance(h, tuple):
                        n = h[1]
                        act.wait_ge(idx_s, n + 1)
                        if n >= 2:
                            act.wait_ge(idx_acc, n - 1)
                        act.activation(prob[:, n % 2, 0:P + S], b_s[n % 2][:, 0:P + S], ACT.Relu).then_inc(idx_relu, 1)
                    else:
                        w0 = width0(h)
                        act.wait_ge(max_done, h + 1)
                        if h < 2:
                            act.wait_ge(idx_acc, 7 + h)
                        else:
                            act.wait_ge(pt_ready, h - 1)
                        act.activation(prob[:, h % 2, 0:w0], b_s[h % 2][:, 0:w0], ACT.Exp, scale=SCALE,
                                       bias=nmx[:, h, 0:1], accum_out=psums[:, h, 0:1])
                        act.activation(prob[:, h % 2, w0:w0 + S], b_s[h % 2][:, w0:w0 + S], ACT.Exp, scale=SCALE,
                                       bias=nmx[:, h, 1:2], accum_out=psums[:, h, 1:2]).then_inc(exp_done, 1)
                if LAG_T <= s < len(run) + LAG_T and not isinstance(run[s - LAG_T], tuple):
                    h = run[s - LAG_T]
                    n = width0(h) + S
                    act.wait_ge(pt_ready, h + 1)
                    if h >= 2:
                        act.wait_ge(pv_done, h - 1)
                    act.activation(probT[:, h % 2, 0:n], b_t[:, 0:n], ACT.Copy).then_inc(pt_copied, 1)
                if LAG_V <= s and not isinstance(run[s - LAG_V], tuple) and run[s - LAG_V] % 2:
                    h = run[s - LAG_V]
                    pr = h // 2
                    if HEADS[h][0] in ("fox", "dsa"):
                        act.wait_ge(pair_tmp, GATES.index(pr) + 1)
                        act.activation(b_hi[:, pair_ktile(pr), :], gated[:], ACT.Copy).then_inc(pair_hi, 1)
                    else:
                        act.wait_ge(pv_done, h + 1)
                        act.activation(b_hi[:, pair_ktile(pr), :], b_v[:, 0:S], ACT.Copy).then_inc(pair_hi, 1)

            early = [(ident[:], a["c_ident"]),
                     (gain_rows[0:8, :], a["g_pre"][0].rearrange("(k p) -> k p", p=P)),
                     (gain_rows[8:24, :], a["g_mix_2"].rearrange("l (k p) -> (l k) p", p=P)),
                     (gain_rows[24:40, :], a["g_mem_2"].rearrange("l (k p) -> (l k) p", p=P)),
                     (gain_rows[40:56, :], a["g_mlp_2"].rearrange("l (k p) -> (l k) p", p=P))]
            assert len(early) == N_EARLY
            for dst, src in early:
                act.dma_start(dst, src).then_inc(early_landed, 16)
            act.sem_inc(free_a, 2)
            act.wait_ge(gains_made, 1)
            groups(G_H, 0, a_hi, GAIN_PRE)
            groups(G_H, 2, a_hi, GAIN_PRE)
            split(0, 0, 0, unit_size(0))
            split(1, 1, 1, unit_size(1))
            squares(0, x, [tok[:, t] for t in range(NT)])
            split(2, 2, 0, unit_size(2))
            act.wait_ge(rstd_done, 1)
            with act.Fori(0, NBLK_LOOP // 2) as i:
                for j in range(4):
                    c = j + LOOK
                    act.wait_ge(raw_landed[c % RAW], (i * 2 + (c // RAW + 1)) * 16)
                    act.wait_ge(unit_used, i * 4 + (c - RING + 2))
                    act.activation(w_hi[:, c % RING, 0:4 * CIN], raw[:, c % RAW, 0:4 * CIN], ACT.Copy).then_inc(hi_ready, 1)
                    if j % 2:
                        act.wait_ge(unit_used, i * 4 + (j + 2))
                        act.activation(proj[:, bass.ds((i * 2 + j // 2) * CIN + IN_BLOCKS[0][0], CIN)],
                                       bank[2 * (j // 2)][:, 0:CIN], ACT.Copy, scale=stat[:, 2, 0, 0:1]).then_inc(free_a, 1)
            dense(2 * NBLK_LOOP, NBLK_LOOP)

            act.wait_ge(f_abs, 1)
            act.activation(fgt[:, 2], fgt[:, 1], ACT.Exp).then_inc(act_chain, 1)
            act.wait_ge(act_chain, 1)
            act.activation(fgt[:, 3], fgt[:, 2], ACT.Ln, bias=1.0).then_inc(f_ln, 1)
            act.wait_ge(half_rstd, 1)

            for s in run_steps(RUN1):
                step(RUN1, s)
                fill(RUN1, s)
            unit(U_BR + 2)
            unit(U_BR + 3)
            groups(G_MERGED, 0, a_hi)
            unit(U_WO)
            groups(G_MERGED, 2, a_hi)
            unit(U_WO + 1)
            block_done(U_WO + 1)
            squares_half(2, 0, [bank[pair_bank(B_WO) + t][:, :] for t in range(NT)])
            unit(U_WO + 2)
            group(G_P, b_hi, 0)
            act.wait_ge(mem_landed, 16)
            squares(1, tok, [part_[:, 4:8, :].rearrange("p k n -> p (k n)") for part_ in (b_hi, b_lo)])
            unit(U_WO + 3)
            block_done(U_WO + 3)
            squares_half(2, 1, [bank[pair_bank(B_WO + 1) + t][:, :] for t in range(NT)])
            unit(U_PLE)
            for c in range(2):
                act.wait_ge(ple_block, c + 1)
                for t in range(NT):
                    ins = act.activation(e_tok[:, t, c * CB:c * CB + CB], bank[pair_bank(B_PLE + c) + t][:, :], ACT.Copy)
                ins.then_inc(free_a, 1)

            def gate_half(c):
                for t in range(NT):
                    ins = act.activation(m_hi[:, t, c * CB:c * CB + CB], bank[pair_bank(B_GATE + c) + t][:, :], ACT.Tanh,
                                         scale=0.5)
                ins.then_inc(free_a, 1)

            def gated_squares(c):
                act.wait_ge(z_made, c + 1)
                squares_half(3, c, [e_tok[:, t, c * CB:c * CB + CB] for t in range(NT)])

            groups(G_X, 0, a_hi)
            unit(U_GATE)
            groups(G_X, 2, a_hi)
            unit(U_GATE + 1)
            groups(G_MEM0, 0, b_hi, GAIN_MEM)
            block_done(U_GATE + 1)
            gate_half(0)
            unit(U_GATE + 2)
            gated_squares(0)
            unit(U_GATE + 3)
            groups(G_MEM0, 2, b_hi, GAIN_MEM)
            block_done(U_GATE + 3)
            gate_half(1)
            gated_squares(1)
            unit(U_KV0)
            unit(U_KV0 + 1)
            groups(G_MIX0, 0, a_hi, GAIN_MIX)
            block_done(U_KV0 + 1)
            evac(B_KV0)

            def mlp(base, lay, r, gx, g0, gain):
                def hidden_relu(i):
                    for t in range(NT):
                        ins = act.activation(hidden[:, t], b_s[t][:, :], ACT.Relu, scale=stat[:, 2, r, t:t + 1])
                    ins.then_inc(ff_relu, 1)
                unit(base)
                groups(gx, 2, a_hi, gain)
                x_squares(r, X_OUT0 + 2 if lay == 0 else X_OUT1 + 2, tok)
                unit(base + 1)
                block_done(base + 1)
                act.wait_ge(rstd_done, r + 1)
                hidden_relu(0)

                def chunk(i, peeled):
                    for r_ in range(4):
                        c = 2 + r_ + LOOK
                        if peeled:
                            unit(base + 2 + 4 * i + r_)
                        else:
                            act.wait_ge(raw_landed[(base + c) % RAW], (i * 2 + landed(base + c)) * 16)
                            act.wait_ge(unit_used, i * 4 + (base + c - RING + 2))
                            act.activation(w_hi[:, (base + c) % RING, :], raw[:, (base + c) % RAW, :], ACT.Copy)\
                               .then_inc(hi_ready, 1)
                        if r_ == 0:
                            for q in range(2):
                                act.wait_ge(tr_ready, i * 2 + (g0 + q + 1))
                                act.activation(b_hi[:, 2 * q:2 * q + 2, :],
                                               b_tr[(g0 + q) % 2][:, :].rearrange("p (k n) -> p k n", k=2), ACT.Copy)\
                                   .then_inc(tr_hi, 1)
                        if r_ == 1:
                            act.wait_ge(unit_used, i * 4 + (base + 3 + 2))
                            hidden_relu(i + 1)
                with act.Fori(0, FF - 2) as i:
                    chunk(i, False)
                chunk(FF - 2, True)
                for q in range(2):
                    group(g0 + 2 * (FF - 1) + q, b_hi, 2 * q)
                unit(base + 4 * FF - 2)
                unit(base + 4 * FF - 1)

            unit(U_POOL)
            groups(G_MIX0, 2, a_hi, GAIN_MIX)
            x_squares(4, X_PLE + 2, tok)
            unit(U_POOL + 1)
            block_done(U_POOL + 1)
            evac(B_POOL)
            unit(U_POOL + 2)
            for s in run_steps(RUN2):
                step(RUN2, s)
                fill(RUN2, s)
            for g in range(4):
                act.wait_ge(d_ready, 2 * g + 1)
                act.activation(dT[:, g, 0, :], b_io[0:GC, 0:S], ACT.Copy).then_inc(d_copied_a, 1)
            groups(G_TOK0, 0, b_hi)
            unit(U_OUT0)
            group(G_TOK0 + 2, b_hi, 4)
            unit(U_OUT0 + 1)
            unit(U_OUT0 + 2)
            groups(G_MLP0, 0, a_hi, GAIN_MLP)
            unit(U_OUT0 + 3)
            mlp(U_FF0, 0, 5, G_MLP0, G_FF0, GAIN_MLP)
            groups(G_MIX1, 0, a_hi, GAIN_MIX + 8)
            unit(U_MOBA0)
            groups(G_MIX1, 2, a_hi, GAIN_MIX + 8)
            x_squares(6, X_FF0 + 2, m_hi)
            unit(U_MOBA0 + 1)
            groups(G_MEM1, 0, b_hi, GAIN_MEM + 8)
            block_done(U_MOBA0 + 1)
            evac(B_MOBA0)
            unit(U_KV1)
            groups(G_MEM1, 2, b_hi, GAIN_MEM + 8)
            unit(U_KV1 + 1)
            block_done(U_KV1 + 1)
            evac(B_KV1)
            dense(U_MOBA, B_MOBA)
            for s in run_steps(RUN3):
                step(RUN3, s)
                fill(RUN3, s)
            unit(U_OUT1 + 1)
            unit(U_OUT1 + 2)
            groups(G_MLP1, 0, a_hi, GAIN_MLP + 8)
            unit(U_OUT1 + 3)
            mlp(U_FF1, 1, 7, G_MLP1, G_FF1, GAIN_MLP + 8)

        @block.vector
        def _(dve):
            link = Linker(dve, vec_chain)

            def unit(u):
                v = u + LOOK
                if v < N_UNITS:
                    split(v)

            def split(v):
                n = unit_size(v)
                dve.wait_ge(hi_ready, v + 1)
                dve.tensor_tensor(w_lo[:, v % RING, 0:n], raw[:, v % RAW, 0:n], w_hi[:, v % RING, 0:n].bitcast(F32),
                                  ALU.subtract).then_inc(lo_ready, 1)

            def group(g, hi, lo, k, gain=None):
                dve.wait_ge(tr_hi, g + 1)
                ps = group_bank(g)
                if gain is None:
                    dve.tensor_tensor(lo[:, k:k + 2, :], ps[:, :].rearrange("p (k n) -> p k n", k=2),
                                      hi[:, k:k + 2, :].bitcast(F32), ALU.subtract).then_inc(tr_lo, 1)
                else:
                    for q in range(2):
                        ins = dve.scalar_tensor_tensor(lo[:, k + q, :], ps[:, q * S:q * S + S],
                                                       gain_cols[:, gain + k + q:gain + k + q + 1],
                                                       hi[:, k + q, :].bitcast(F32), ALU.mult, ALU.subtract)
                    ins.then_inc(tr_lo, 1)

            def groups(g0, first, hi, lo, gain=None):
                for q in range(first, first + 2):
                    group(g0 + q, hi, lo, 2 * q, gain)

            def block_done(u):
                dve.wait_ge(unit_used, u + 2)

            def scaled(dst, k, r, n=CB):
                dve.wait_ge(rstd_done, r + 1)
                dve.tensor_scalar(dst, bank[pair_bank(k) + 1][:, 0:n], stat[:, 2, r, 1:2], None, ALU.mult)\
                   .then_inc(free_v, 1)

            def evac(k):
                kind = BLOCKS[k]
                if kind == "in":
                    c, n = IN_BLOCKS[k]
                    scaled(pj[:, 1, c:c + n], k, 0, n)
                if kind == "merge":
                    c = (k - B_MERGE) * CB
                    dve.wait_ge(free_a, freed(k, "a"))
                    dve.tensor_scalar(m_sig[:, :, c:c + CB], m_sig[:, :, c:c + CB], 0.5, 0.5, ALU.mult, ALU.add)\
                       .then_inc(merge_sig, 1)
                if kind == "brb":
                    dve.wait_ge(merge_sig, 4)
                    c = D + (k - B_BR) * CB
                    for t in range(NT):
                        g = m_sig[:, t, c:c + CB]
                        ins = dve.tensor_tensor(g, g, bank[pair_bank(k) + t][:, :], ALU.mult)
                    ins.then_inc(free_v, 1)
                if kind == "kv":
                    scaled(memkv[:, int(k == B_KV1), 1, :], k, 1)
                if kind == "pool":
                    c = (1 - (k - B_POOL)) * CB
                    scaled(h_pool[:, 1, c:c + CB], k, 4)
                if kind == "moba":
                    c = (0 if k == B_MOBA0 else k - B_MOBA + 1) * CB
                    scaled(h_moba[:, 1, c:c + CB], k, 6)

            def dense(u, k):
                unit(u)
                unit(u + 1)
                block_done(u + 1)
                evac(k)

            def fill(run, s):
                for u, k, half_ in fill_of(run, s):
                    unit(u)
                    if half_:
                        block_done(u)
                        evac(k)

            def add_half(c, b):
                for t in range(NT):
                    xs = x[:, t, c * CB:c * CB + CB]
                    ins = dve.tensor_tensor(xs, xs, bank[b + t][:, :], ALU.add)
                ins.then_inc(x_half, 1)

            def select_round(n):
                if n == 0:
                    for c in (0, P + P):
                        ins = dve.scalar_tensor_tensor(score[:, c:c + P], mask[:], FILL, score[:, c:c + P], ALU.mult, ALU.add)
                    link(ins)
                for t, c, w in ((0, 0, P), (1, P, S)):
                    ins = dve.max(top8[:, t, :], score[:, c:c + w])
                link(ins)
                for t, c, w in ((0, 0, P), (1, P, S)):
                    ins = dve.match_replace(score[:, c:c + w], top8[:, t, :], score[:, c:c + w], TAKEN)
                link(ins)
                if n == TOPK // 8 - 1:
                    dve.tensor_scalar(sel_b[:], score[:], TAKEN / 2, NEG, ALU.is_ge, ALU.mult).then_inc(sel_made, 1)

            def step(run, s):
                if 0 <= s < len(run):
                    h = run[s]
                    if isinstance(h, tuple):
                        n = h[1]
                        dve.wait_ge(idx_relu, n + 1)
                        for t, c, w in ((0, 0, P), (1, P, S)):
                            src, w_ = prob[:, n % 2, c:c + w], wis[:, t, n:n + 1]
                            if n == 0:
                                ins = dve.tensor_scalar(score[:, c:c + w], src, w_, None, ALU.mult)
                            else:
                                ins = dve.scalar_tensor_tensor(score[:, c:c + w], src, w_, score[:, c:c + w],
                                                               ALU.mult, ALU.add)
                        ins.then_inc(idx_acc, 1)
                        dve.wait_ge(idx_acc, n + 1)
                    else:
                        w0 = width0(h)
                        dve.wait_ge(s_ready, h + 1)
                        dve.tensor_reduce(mx[:, h, 0:1], b_s[h % 2][:, 0:w0], AX.X, ALU.max)
                        link(dve.tensor_reduce(mx[:, h, 1:2], b_s[h % 2][:, w0:w0 + S], AX.X, ALU.max))
                        dve.tensor_scalar(nmx[:, h, :], mx[:, h, :], -SCALE, None, ALU.mult).then_inc(max_done, 1)
                for what, pr in parts_at(run, s):
                    if what == "gate":
                        dve.wait_ge(part_cp, PART[(what, pr)] + 1)
                        dve.scalar_tensor_tensor(gate_s[:], gated[:], 1.0, b_io[:, 0:S], ALU.add, ALU.mult)\
                           .then_inc(gate_cp, 1)
                if LAG_P <= s < len(run) + LAG_P and not isinstance(run[s - LAG_P], tuple):
                    h = run[s - LAG_P]
                    w0 = width0(h)
                    dve.wait_ge(exp_done, h + 1)
                    link(dve.reciprocal(prec[:, h, :], psums[:, h, :]))
                    dve.tensor_scalar(prob[:, h % 2, 0:w0], prob[:, h % 2, 0:w0], prec[:, h, 0:1], None, ALU.mult)
                    dve.tensor_scalar(prob[:, h % 2, w0:w0 + S], prob[:, h % 2, w0:w0 + S], prec[:, h, 1:2], None,
                                      ALU.mult).then_inc(p_ready, 1)
                if LAG_V <= s and not isinstance(run[s - LAG_V], tuple) and run[s - LAG_V] % 2:
                    h = run[s - LAG_V]
                    pr = h // 2
                    kt = pair_ktile(pr)
                    if HEADS[h][0] in ("fox", "dsa"):
                        dve.wait_ge(pv_done, h + 1)
                        dve.wait_ge(gate_cp, GATES.index(pr) + 1)
                        dve.scalar_tensor_tensor(gated[:], b_v[:, 0:S], 0.5, gate_s[:], ALU.mult, ALU.mult)\
                           .then_inc(pair_tmp, 1)
                        dve.wait_ge(pair_hi, pr + 1)
                        dve.tensor_tensor(b_lo[:, kt, :], gated[:], b_hi[:, kt, :].bitcast(F32), ALU.subtract)\
                           .then_inc(pair_lo, 1)
                    else:
                        dve.wait_ge(pair_hi, pr + 1)
                        dve.tensor_tensor(b_lo[:, kt, :], b_v[:, 0:S], b_hi[:, kt, :].bitcast(F32), ALU.subtract)\
                           .then_inc(pair_lo, 1)
                if 0 <= s < len(run) and not isinstance(run[s], tuple) and run[s] < TOPK // 8:
                    select_round(run[s])

            dve.sem_inc(free_v, 2)
            dve.wait_ge(gains_tr, 1)
            dve.tensor_copy(gain_cols[:], b_t[:, 0:56]).then_inc(gains_made, 1)
            dve.wait_ge(gains_made, 1)
            groups(G_H, 0, a_hi, a_lo, GAIN_PRE)
            groups(G_H, 2, a_hi, a_lo, GAIN_PRE)
            for u in range(LOOK):
                split(u)
            dve.wait_ge(rstd_done, 1)
            with dve.Fori(0, NBLK_LOOP // 2) as i:
                for j in range(4):
                    c = j + LOOK
                    dve.wait_ge(hi_ready, i * 4 + (c + 1))
                    dve.tensor_tensor(w_lo[:, c % RING, 0:4 * CIN], raw[:, c % RAW, 0:4 * CIN],
                                      w_hi[:, c % RING, 0:4 * CIN].bitcast(F32), ALU.subtract).then_inc(lo_ready, 1)
                    if j % 2:
                        dve.wait_ge(unit_used, i * 4 + (j + 2))
                        dve.tensor_scalar(proj[:, bass.ds((i * 2 + j // 2) * CIN + (DIN + IN_BLOCKS[0][0]), CIN)],
                                          bank[2 * (j // 2) + 1][:, 0:CIN], stat[:, 2, 0, 1:2], None, ALU.mult)\
                           .then_inc(free_v, 1)
            dense(2 * NBLK_LOOP, NBLK_LOOP)

            dve.wait_ge(const_landed, 16 * N_SMALL)
            dve.wait_ge(free_a, freed(NBLK_LOOP, "a"))
            dve.wait_ge(free_v, freed(NBLK_LOOP, "v"))
            link(dve.tensor_tensor(fgt[:, 0], pj[:, :, FB:FB + 8], bias_f[:].unsqueeze(1).to_broadcast([P, NT, 8]), ALU.add))
            link(dve.tensor_scalar(fgt[:, 4], fgt[:, 0], -1.0, None, ALU.mult))
            dve.tensor_tensor(fgt[:, 1], fgt[:, 0], fgt[:, 4], ALU.min).then_inc(f_abs, 1)
            link(dve.tensor_scalar(fgt[:, 5], fgt[:, 0], 0.0, None, ALU.min))
            link(dve.tensor_scalar(wis[:], pj[:, :, WI:WI + 8], IDX_SCALE, None, ALU.mult))
            dve.tensor_copy(ident_b[:], ident[:])
            dve.tensor_copy(mask_b[:], mask[:]).then_inc(consts_made, 1)

            for s in run_steps(RUN1):
                step(RUN1, s)
                if s == 0:
                    dve.wait_ge(f_ln, 1)
                    dve.tensor_tensor(fgt[:, 4], fgt[:, 5], fgt[:, 3], ALU.subtract).then_inc(f_log, 1)
                if s == 1:
                    dve.wait_ge(c_ready, 1)
                    dve.tensor_scalar(cT[:], b_t[0:8, 0:S], -1.0 / SCALE, None, ALU.mult).then_inc(c_made, 1)
                fill(RUN1, s)
            for c in range(2):
                cols = slice(c * CB, c * CB + CB)
                unit_ = U_BR + 2 + c
                if c:
                    unit(U_BR + 3)
                    groups(G_MERGED, 0, a_hi, a_lo)
                else:
                    unit(U_BR + 2)
                block_done(unit_)
                for t in range(NT):
                    ins = dve.tensor_tensor(tok[:, t, cols], bank[pair_bank(B_BR + 2 + c) + t][:, :], m_sig[:, t, cols],
                                            ALU.mult)
                ins.then_inc(free_v, 1)
                dve.wait_ge(free_v, freed(B_BR + 2 + c, "v"))
                dve.tensor_tensor(tok[:, :, cols], tok[:, :, cols], m_sig[:, :, D + c * CB:D + c * CB + CB], ALU.add)\
                   .then_inc(merged, 1)
            groups(G_MERGED, 2, a_hi, a_lo)
            unit(U_WO)
            unit(U_WO + 1)
            unit(U_WO + 2)
            group(G_P, b_hi, b_lo, 0)
            unit(U_WO + 3)
            unit(U_PLE)
            dve.wait_ge(rstd_done, 3)
            dve.wait_ge(x_again, 16)
            for c in range(2):
                cols = slice(c * CB, c * CB + CB)
                for t in range(NT):
                    ins = dve.scalar_tensor_tensor(m_hi[:, t, cols], bank[pair_bank(B_WO + c) + t][:, :],
                                                   stat[:, 2, 2, t:t + 1], gain_bc[:, cols], ALU.mult, ALU.mult)
                ins.then_inc(free_v, 1)
                dve.wait_ge(free_v, freed(B_WO + c, "v"))
                dve.tensor_tensor(x[:, :, cols], x[:, :, cols], m_hi[:, :, cols], ALU.add).then_inc(x_post, 1)

            def gated_half(c):
                cols = slice(c * CB, c * CB + CB)
                dve.wait_ge(free_a, freed(B_GATE + c, "a"))
                dve.scalar_tensor_tensor(e_tok[:, :, cols], m_hi[:, :, cols], 1.0, e_tok[:, :, cols], ALU.add, ALU.mult)\
                   .then_inc(z_made, 1)

            groups(G_X, 0, a_hi, a_lo)
            unit(U_GATE)
            groups(G_X, 2, a_hi, a_lo)
            unit(U_GATE + 1)
            groups(G_MEM0, 0, b_hi, b_lo, GAIN_MEM)
            gated_half(0)
            unit(U_GATE + 2)
            unit(U_GATE + 3)
            groups(G_MEM0, 2, b_hi, b_lo, GAIN_MEM)
            gated_half(1)
            dve.wait_ge(z_made, 2)
            dve.wait_ge(bc_landed, 16)
            for t in range(NT):
                ins = dve.tensor_tensor(tok[:, t, :], e_tok[:, t, :], gain_bc[:], ALU.mult)
            link(ins)
            unit(U_KV0)
            dve.wait_ge(rstd_done, 4)
            for c in range(2):
                cols = slice(c * CB, c * CB + CB)
                for t in range(NT):
                    ins = dve.scalar_tensor_tensor(x[:, t, cols], tok[:, t, cols], stat[:, 2, 3, t:t + 1], x[:, t, cols],
                                                   ALU.mult, ALU.add)
                ins.then_inc(x_half, 1)
            unit(U_KV0 + 1)
            groups(G_MIX0, 0, a_hi, a_lo, GAIN_MIX)
            block_done(U_KV0 + 1)
            evac(B_KV0)

            def mlp(base, lay, gx, g0, gain):
                def hidden_square(n):
                    dve.wait_ge(ff_relu, n)
                    dve.tensor_tensor(hidden, hidden, hidden, ALU.mult).then_inc(ff_sq, 1)
                groups(gx, 2, a_hi, a_lo, gain)
                unit(base)
                unit(base + 1)
                hidden_square(lay * FF + 1)

                def chunk(i, peeled):
                    for r in range(4):
                        c = 2 + r + LOOK
                        if peeled:
                            unit(base + 2 + 4 * i + r)
                        else:
                            dve.wait_ge(hi_ready, i * 4 + (base + c + 1))
                            dve.tensor_tensor(w_lo[:, (base + c) % RING, :], raw[:, (base + c) % RAW, :],
                                              w_hi[:, (base + c) % RING, :].bitcast(F32), ALU.subtract).then_inc(lo_ready, 1)
                        if r == 0:
                            for q in range(2):
                                dve.wait_ge(tr_hi, i * 2 + (g0 + q + 1))
                                dve.tensor_tensor(b_lo[:, 2 * q:2 * q + 2, :],
                                                  b_tr[(g0 + q) % 2][:, :].rearrange("p (k n) -> p k n", k=2),
                                                  b_hi[:, 2 * q:2 * q + 2, :].bitcast(F32), ALU.subtract).then_inc(tr_lo, 1)
                        if r == 1:
                            hidden_square(i + (lay * FF + 2))
                with dve.Fori(0, FF - 2) as i:
                    chunk(i, False)
                chunk(FF - 2, True)
                for q in range(2):
                    group(g0 + 2 * (FF - 1) + q, b_hi, b_lo, 2 * q)
                unit(base + 4 * FF - 2)
                block_done(base + 4 * FF - 2)
                add_half(0, 0)
                unit(base + 4 * FF - 1)

            def out_projection(u, k, gx, gain, filled=False):
                if not filled:
                    unit(u)
                unit(u + 1)
                block_done(u + 1)
                add_half(0, pair_bank(k))
                unit(u + 2)
                groups(gx, 0, a_hi, a_lo, gain)
                unit(u + 3)
                block_done(u + 3)
                add_half(1, pair_bank(k + 1))

            unit(U_POOL)
            groups(G_MIX0, 2, a_hi, a_lo, GAIN_MIX)
            unit(U_POOL + 1)
            block_done(U_POOL + 1)
            evac(B_POOL)
            unit(U_POOL + 2)
            for s in run_steps(RUN2):
                step(RUN2, s)
                fill(RUN2, s)
            dve.wait_ge(pool_landed, 16 * 7)
            for g in range(4):
                dve.wait_ge(d_ready, 2 * g + 2)
                dve.tensor_copy(dT[:, g, 1, :], b_t[0:GC, 0:S]).then_inc(d_copied_v, 1)
            for q in range(2):
                cols = slice(q * 2 * GW, q * 2 * GW + 2 * GW)
                dve.wait_ge(y_ready, q + 1)
                for t in range(NT):
                    ins = dve.tensor_tensor(tok[:, t, cols], bank[4 * t + q][:, 0:2 * GW], gain_bc[:, cols], ALU.mult)
                ins.then_inc(y_made, 1)
            groups(G_TOK0, 0, b_hi, b_lo)
            group(G_TOK0 + 2, b_hi, b_lo, 4)
            out_projection(U_OUT0, B_OUT0, G_MLP0, GAIN_MLP)
            mlp(U_FF0, 0, G_MLP0, G_FF0, GAIN_MLP)
            groups(G_MIX1, 0, a_hi, a_lo, GAIN_MIX + 8)
            block_done(U_MOBA0 - 1)
            add_half(1, 2)
            groups(G_MIX1, 2, a_hi, a_lo, GAIN_MIX + 8)
            unit(U_MOBA0)
            unit(U_MOBA0 + 1)
            groups(G_MEM1, 0, b_hi, b_lo, GAIN_MEM + 8)
            block_done(U_MOBA0 + 1)
            evac(B_MOBA0)
            unit(U_KV1)
            groups(G_MEM1, 2, b_hi, b_lo, GAIN_MEM + 8)
            unit(U_KV1 + 1)
            block_done(U_KV1 + 1)
            evac(B_KV1)
            dense(U_MOBA, B_MOBA)
            for s in run_steps(RUN3):
                step(RUN3, s)
                fill(RUN3, s)
            out_projection(U_OUT1, B_OUT1, G_MLP1, GAIN_MLP + 8, filled=True)
            mlp(U_FF1, 1, G_MLP1, G_FF1, GAIN_MLP + 8)
            block_done(N_UNITS - 1)
            add_half(1, 2)

        @block.tensor
        def _(pe):
            def product(u, slot, hi, lo, k0, banks, first, last, n=CB, kts=4, col=0, used=True, mid=()):
                pe.wait_ge(lo_ready, u + 1)
                pitch = n if kts == 4 else D
                for k in range(kts):
                    if k in mid:
                        mid[k]()
                    w = slice(k * pitch + col, k * pitch + col + n)
                    for t in range(NT):
                        ts = slice(t * P, t * P + P)
                        for q, (xa, wa) in enumerate(((hi, w_hi), (hi, w_lo), (lo, w_hi))):
                            ins = pe.matmul(banks[t][:, 0:n], xa[:, k0 + k, ts], wa[:, slot, w],
                                            start=first and k == 0 and q == 0, stop=last and k == kts - 1 and q == 2)
                if used:
                    ins.then_inc(unit_used, 1)
                return ins

            def blocks_read(k):
                pe.wait_ge(free_a, freed(k, "a"))
                pe.wait_ge(free_v, freed(k, "v"))

            def banks_free(k):
                before = [j for j in range(k) if pair_bank(j) == pair_bank(k)]
                blocks_read(before[-1] if before else -1)

            def banks_of(k):
                return bank[pair_bank(k):pair_bank(k) + 2]

            def dense(u0, k, hi, lo, mids=((), ())):
                banks_free(k)
                n = IN_BLOCKS[k][1] if BLOCKS[k] == "in" else CB
                for r in range(2):
                    product(u0 + r, (u0 + r) % RING, hi, lo, 4 * r, banks_of(k), r == 0, r == 1, n, mid=mids[r])

            def group(g, src, k):
                if g >= 2:
                    pe.wait_ge(tr_lo, g - 1)
                ps = group_bank(g)
                for kk in range(2):
                    for t in range(NT):
                        ins = pe.transpose(ps[:, kk * S + t * P:kk * S + t * P + P],
                                           src[:, t, (k + kk) * P:(k + kk) * P + P], ident[:])
                ins.then_inc(tr_ready, 1)

            def groups(g0, src, q, ready, count):
                def work():
                    pe.wait_ge(ready, count)
                    group(g0 + q, src, 2 * q)
                return work

            def split_by(g0, q):
                return lambda: pe.wait_ge(tr_lo, g0 + q + 1)

            def both(*works):
                def work():
                    for w in works:
                        w()
                return work

            def lower(g0, src, ready, count):
                return {2: groups(g0, src, 0, ready, count), 3: groups(g0, src, 1, ready, count)}

            def upper(g0, src, ready, count):
                return ({0: split_by(g0, 0), 2: both(split_by(g0, 1), groups(g0, src, 2, ready, count)),
                         3: groups(g0, src, 3, ready, count)},
                        {0: split_by(g0, 2), 2: split_by(g0, 3)})

            def part(what, pr):
                n = PART[(what, pr)]
                if n:
                    pe.wait_ge(part_cp, n)
                before = PARTS[n - 1] if n else None
                if before and before[0] == "gate":
                    pe.wait_ge(gate_cp, GATES.index(before[1]) + 1)
                if what in ("ki", "qi"):
                    pe.wait_ge(rope_idx, 1)
                elif what == "ka":
                    pe.wait_ge(rope_dsa, 1)
                else:
                    kind, j = HEADS[2 * pr]
                    if what == "gate":
                        blocks_read(5 if kind == "fox" else 8)
                    if kind == "dsa" and what == "q":
                        pe.wait_ge(rope_dsa, 1)
                    if kind == "moba":
                        pe.wait_ge(moba_made, 2 * (j // 4) + (1 if what == "q" else 2))
                    if kind[:3] == "mem":
                        pe.wait_ge(memq_made if what == "q" else memk_made, int(kind[3]) + 1)
                for t in range(NT):
                    if what in ("ki", "ka"):
                        src = k_twice[:, t].rearrange("p q d -> p (q d)")
                    elif what == "qi":
                        src = pj[:, t, QI + P * pr:QI + P * pr + P]
                    else:
                        src = head_cols(2 * pr)[what][:, t]
                    ins = pe.transpose(b_io[:, t * P:t * P + P], src, ident[:])
                ins.then_inc(part_tr, 1)

            def logits(ps, q, k, w0, stop):
                pe.matmul(ps[:, 0:w0], q[:, 0:P], k[:, 0:w0], start=True, stop=stop)
                return pe.matmul(ps[:, w0:w0 + S], q[:, P:S], k[:, 0:S], start=True, stop=stop)

            def step(run, s):
                for what in parts_at(run, s):
                    part(*what)
                if 0 <= s < len(run):
                    h = run[s]
                    if isinstance(h, tuple):
                        n = h[1]
                        rows = slice(HD * (n % 2), HD * (n % 2) + HD)
                        pe.wait_ge(part_cp, PART[("qi", n // 2)] + 1)
                        pe.wait_ge(part_cp, PART[("ki", 0)] + 1)
                        if n >= 2:
                            pe.wait_ge(idx_relu, n - 1)
                        logits(b_s[n % 2], qk[rows, PART_SLOT[("qi", n // 2)], 0], kT[rows], P, True).then_inc(idx_s, 1)
                    else:
                        kind, j = HEADS[h]
                        rows = slice(HD * (h % 2), HD * (h % 2) + HD)
                        slot = PART_SLOT[("q", h // 2)]
                        pe.wait_ge(part_cp, PART[("q", h // 2)] + 1)
                        pe.wait_ge(part_cp, PART[("ka", 0) if kind == "dsa" else ("k", h // 2)] + 1)
                        if h < 2:
                            pe.wait_ge(idx_relu, 7 + h)
                        else:
                            pe.wait_ge(exp_done, h - 1)
                        k = kT[rows] if kind == "dsa" else qk[rows, slot, 1]
                        ps, w0 = b_s[h % 2], width0(h)
                        free = kind[:3] == "mem"
                        for t, c, w in ((0, 0, w0), (1, w0, S)):
                            ins = pe.matmul(ps[:, c:c + w], qk[rows, slot, 0, t * P:t * P + P], k[:, 0:w],
                                            start=True, stop=free)
                            if kind == "fox":
                                pe.wait_ge(c_made, 1)
                                pe.matmul(ps[:, c:c + w], ident[0:8, j:j + 1].to_broadcast([8, P]), cT[:, 0:w],
                                          start=False, stop=False)
                            if kind == "dsa":
                                pe.wait_ge(sel_made, 1)
                                pe.matmul(ps[:, c:c + w], ident_b[:], sel_b[:, c:c + w], start=False, stop=False)
                            if not free:
                                pe.wait_ge(consts_made, 1)
                                ins = pe.matmul(ps[:, c + w - P:c + w], ident_b[:], mask_b[:], start=False, stop=True)
                        ins.then_inc(s_ready, 1)
                if LAG_T <= s < len(run) + LAG_T and not isinstance(run[s - LAG_T], tuple):
                    h = run[s - LAG_T]
                    w0 = width0(h)
                    pe.wait_ge(p_ready, h + 1)
                    if h:
                        pe.wait_ge(pt_copied, h)
                    pr = prob[:, h % 2]
                    cuts = [0, w0] + ([P, w0 + P] if w0 == S else [w0 + P])
                    for q, c in enumerate(cuts):
                        ins = pe.transpose(b_t[:, q * P:q * P + P], pr[:, c:c + P], ident[:])
                    ins.then_inc(pt_ready, 1)
                if LAG_V <= s and not isinstance(run[s - LAG_V], tuple):
                    h = run[s - LAG_V]
                    kind, j = HEADS[h]
                    rows = slice(HD * (h % 2), HD * (h % 2) + HD)
                    v, pT = head_cols(h)["v"], probT[:, h % 2]
                    if kind == "moba":
                        blocks_read(B_MOBA + (0, 2, 3)[j // 4])
                    pe.wait_ge(pt_copied, h + 1)
                    if h % 2 == 0 and h:
                        pe.wait_ge(pair_lo, h // 2)
                    pe.matmul(b_v[rows, 0:S], v[:, 0], pT[:, 0:S], start=True, stop=False)
                    c = S if width0(h) == S else P
                    pe.matmul(b_v[rows, S - c:S], v[:, 1], pT[:, S:S + c], start=False, stop=True)\
                      .then_inc(pv_done, 1)

            def fill(run, s):
                for u, k, half_ in fill_of(run, s):
                    kind = BLOCKS[k]
                    if half_ != 1:
                        banks_free(k)
                    if kind in ("brb", "out"):
                        pe.wait_ge(pair_lo, 4 if kind == "brb" else 16)
                    hi, lo = (b_hi, b_lo) if kind in ("brb", "out") else (a_hi, a_lo)
                    n = IN_BLOCKS[k][1] if kind == "in" else CB
                    product(u, u % RING, hi, lo, 4 if half_ else 0, banks_of(k), half_ != 1, half_ != 0, n)

            pe.sem_inc(unit_used, 1)
            pe.wait_ge(early_landed, 16 * N_EARLY)
            pe.transpose(b_t[:, 0:56], gain_rows[:], ident[0:56, 0:56]).then_inc(gains_tr, 1)
            pe.wait_ge(x_landed, 16 * NT)
            for g in range(4):
                group(G_H + g, x, 2 * g)
            pe.wait_ge(gains_made, 1)
            pe.wait_ge(tr_lo, G_H + 4)
            with pe.Fori(0, NBLK_LOOP // 2) as i:
                for r in range(2):
                    pe.wait_ge(free_a, i * 2 + (r + 1))
                    pe.wait_ge(free_v, i * 2 + (r + 1))
                    b = bank[2 * r:2 * r + 2]
                    product(i * 4 + 2 * r, 2 * r, a_hi, a_lo, 0, b, True, False, CIN)
                    product(i * 4 + (2 * r + 1), 2 * r + 1, a_hi, a_lo, 4, b, False, True, CIN)
            dense(2 * NBLK_LOOP, NBLK_LOOP, a_hi, a_lo)
            blocks_read(NBLK_LOOP - 1)

            for s in run_steps(RUN1):
                step(RUN1, s)
                fill(RUN1, s)
                if s == 1:
                    pe.wait_ge(f_log, 1)
                    pe.matmul(b_t[0:8, 0:S], fgt[:, 4, 0], tri[:], start=True, stop=False)
                    pe.matmul(b_t[0:8, P:S], fgt[:, 4, 1], tri[:, 0:P], start=False, stop=True).then_inc(c_ready, 1)
            pe.wait_ge(pair_lo, 8)
            for c in range(2):
                k, u = B_BR + 2 + c, U_BR + 2 + c
                banks_free(k)
                product(u, u % RING, b_hi, b_lo, 0, banks_of(k), True, True, mid=lower(G_MERGED, tok, merged, 1) if c else ())
            dense(U_WO, B_WO, a_hi, a_lo, upper(G_MERGED, tok, merged, 2))
            dense(U_WO + 2, B_WO + 1, a_hi, a_lo, ({2: groups(G_P, p_tok, 0, p_landed, 16)}, ()))
            pe.wait_ge(tr_lo, G_P + 1)
            for c in range(2):
                banks_free(B_PLE + c)
                product(U_PLE, U_PLE % RING, b_hi, b_lo, 0, banks_of(B_PLE + c), True, True, CB, 2, c * CB, used=False)\
                    .then_inc(ple_block, 1)
            pe.wait_ge(ple_block, 2)
            pe.sem_inc(unit_used, 1)
            blocks_read(B_PLE + 1)
            for q in range(2):
                groups(G_X, x, q, x_post, 1)()
            mids = upper(G_X, x, x_post, 2)
            mids[1][1] = groups(G_MEM0, tok, 0, mem_landed, 16)
            mids[1][3] = groups(G_MEM0, tok, 1, mem_landed, 16)
            dense(U_GATE, B_GATE, a_hi, a_lo, mids)
            dense(U_GATE + 2, B_GATE + 1, a_hi, a_lo, ((), {0: groups(G_MEM0, tok, 2, mem_landed, 16),
                                                            2: groups(G_MEM0, tok, 3, mem_landed, 16)}))
            pe.wait_ge(tr_lo, G_MEM0 + 4)
            dense(U_KV0, B_KV0, b_hi, b_lo, ((), lower(G_MIX0, x, x_half, X_PLE + 1)))

            def mlp(base, lay, gx, g0, x_before, after):
                def up(u, half_, slot, mid=()):
                    product(u, slot, a_hi, a_lo, 4 * half_, b_s, half_ == 0, half_ == 1, mid=mid)
                mids = upper(gx, x, x_half, x_before + 2)
                up(base, 0, base % RING, mids[0])
                up(base + 1, 1, (base + 1) % RING, mids[1])

                def chunk(i, first, last):
                    s = [(base + 2 + r) % RING for r in range(4)]
                    if not last:
                        pe.wait_ge(ff_relu, i + (lay * FF + 1))
                        up(i * 4 + (base + 2), 0, s[0])
                    pe.wait_ge(ff_sq, i + (lay * FF + 1))
                    for q in range(2):
                        pe.wait_ge(tr_lo, i * 2 + (g0 + q - 1))
                        for kk in range(2):
                            for t in range(NT):
                                c = (2 * q + kk) * P
                                ins = pe.transpose(b_tr[(g0 + q) % 2][:, kk * S + t * P:kk * S + t * P + P],
                                                   hidden[:, t, c:c + P], ident[:])
                        ins.then_inc(tr_ready, 1)
                    if not last:
                        up(i * 4 + (base + 3), 1, s[1])
                    pe.wait_ge(tr_lo, i * 2 + (g0 + 2))
                    for c in range(2):
                        u, slot = (base + 4 * FF - 2 + c, (base + 4 * FF - 2 + c) % RING) if last else (i * 4 + (base + 4 + c), s[2 + c])
                        product(u, slot, b_hi, b_lo, 0, bank[2 * c:2 * c + 2], first, last, mid=after if last and c else ())
                chunk(0, True, False)
                with pe.Fori(1, FF - 1) as i:
                    chunk(i, False, False)
                chunk(FF - 1, False, True)

            dense(U_POOL, B_POOL, a_hi, a_lo, upper(G_MIX0, x, x_half, X_PLE + 2))
            banks_free(B_POOL + 1)
            product(U_POOL + 2, (U_POOL + 2) % RING, a_hi, a_lo, 0, banks_of(B_POOL + 1), True, False)
            blocks_read(B_POOL)
            for s in run_steps(RUN2):
                step(RUN2, s)
                fill(RUN2, s)
            pe.wait_ge(pair_lo, 10)
            blocks_read(B_POOL + 1)
            pe.wait_ge(pool_landed, 16 * 7)

            def pooled(g):
                for c in range(2):
                    if g:
                        pe.wait_ge(d_copied_v if c else d_copied_a, g)
                    cols = slice(g * GW + c * GC, g * GW + c * GC + GC)
                    pe.matmul((b_io, b_t)[c][0:GC, 0:S], h_pool[:, 0, cols], band[:, 0, g], start=True, stop=False)
                    pe.matmul((b_io, b_t)[c][0:GC, P:S], h_pool[:, 1, cols], band[:, 1, g, P:S], start=False, stop=True)\
                      .then_inc(d_ready, 1)

            def mixed(g):
                pe.wait_ge(d_copied_a, g + 1)
                pe.wait_ge(d_copied_v, g + 1)
                for t in range(NT):
                    for c in range(2):
                        ins = pe.matmul(bank[4 * t + g // 2][:, g % 2 * GW:g % 2 * GW + GW], dT[:, g, c, t * P:t * P + P],
                                        w_group[:, g, c], start=c == 0, stop=c == 1)
                if g % 2:
                    ins.then_inc(y_ready, 1)

            pooled(0)
            for g in range(1, 4):
                pooled(g)
                mixed(g - 1)
            mixed(3)
            groups(G_TOK0, tok, 0, y_made, 1)()
            groups(G_TOK0, tok, 1, y_made, 2)()
            dense(U_OUT0, B_OUT0, b_hi, b_lo,
                  ({0: split_by(G_TOK0, 0), 1: groups(G_TOK0, tok, 2, y_made, 2), 2: split_by(G_TOK0, 1)},
                   {0: split_by(G_TOK0, 2)}))
            dense(U_OUT0 + 2, B_OUT0 + 1, b_hi, b_lo, (lower(G_MLP0, x, x_half, X_OUT0 + 1), ()))
            mlp(U_FF0, 0, G_MLP0, G_FF0, X_OUT0, lower(G_MIX1, x, x_half, X_FF0 + 1))
            mids = upper(G_MIX1, x, x_half, X_FF0 + 2)
            mids[1][1] = groups(G_MEM1, tok, 0, mem_landed, 32)
            mids[1][3] = groups(G_MEM1, tok, 1, mem_landed, 32)
            dense(U_MOBA0, B_MOBA0, a_hi, a_lo, mids)
            dense(U_KV1, B_KV1, b_hi, b_lo, upper(G_MEM1, tok, mem_landed, 32))
            dense(U_MOBA, B_MOBA, a_hi, a_lo)
            blocks_read(B_KV1)
            for s in run_steps(RUN3):
                step(RUN3, s)
                fill(RUN3, s)
            pe.wait_ge(pair_lo, N_HEADS // 2)
            u = U_OUT1 + 1
            product(u, u % RING, b_hi, b_lo, 4, banks_of(B_OUT1), False, True)
            dense(U_OUT1 + 2, B_OUT1 + 1, b_hi, b_lo, (lower(G_MLP1, x, x_half, X_OUT1 + 1), ()))
            mlp(U_FF1, 1, G_MLP1, G_FF1, X_OUT1, ())


_CONSTANTS = ["c_ident", "c_mask", "c_tri", "c_rope_a", "c_rope_m", "c_band"]
_INS = ["x", "p", "w_in", "b_forget", "w_branch_a", "w_branch_b", "w_merge", "w_out", "g_pre", "g_post", "w_ple",
        "w_ple_gate", "g_ple", "mem_2", "g_mix_2", "g_mem_2", "g_mlp_2", "w_in_pool_2", "w_pool_group_2", "pool_scale_2",
        "w_in_moba_2", "moba_q_gain_2", "moba_k_gain_2", "w_mem_kv_2", "mem_q_gain_2", "mem_k_gain_2", "w_out_2",
        "w_ff1_2", "w_ff2_2"]


def constants():
    f = np.float32
    pos = np.arange(S, dtype=f)[:, None]
    ang_a = pos * (f(500000.0) ** (-np.arange(8, dtype=f) / f(8)))[None, :]
    ang_m = pos * (f(10000.0) ** (-np.arange(0, HD, 2, dtype=f) / f(HD)))[None, :]
    q, k = np.arange(P)[:, None], np.arange(P)[None, :]
    tri = np.concatenate([(q <= k), np.ones((P, P), bool)], axis=1)
    t = np.arange(S)[None, :]
    s = np.arange(S)[:, None]
    band = np.stack([((s <= t) & (s > t - w)) / np.minimum(t + 1, w) - (s == t) for w in (2, 4, 8, 16)])
    return {
        "c_ident": np.eye(P, dtype=f),
        "c_mask": np.where(k <= q, 0.0, NEG).astype(f),
        "c_tri": tri.astype(f),
        "c_rope_a": np.stack([np.cos(ang_a), np.sin(ang_a)]).astype(f),
        "c_rope_m": np.stack([np.cos(ang_m), np.sin(ang_m)]).astype(f),
        "c_band": band.astype(f),
    }


def kernel(**inputs):
    from concourse import bacc
    from concourse.bass_utils import run_bass_kernel_spmd

    nc = bacc.Bacc("TRN2", target_bir_lowering=False, num_devices=1)
    arrays, args = {}, {}
    for name, value in [(n, inputs[n]) for n in _INS] + list(constants().items()):
        value = np.ascontiguousarray(value)
        arrays[f"in_{name}"] = value
        args[name] = nc.dram_tensor(f"in_{name}", value.shape, mybir.dt.from_np(value.dtype), kind="ExternalInput").ap()
    out = nc.dram_tensor("out_x", (1, S, D), F32, kind="ExternalOutput").ap()
    build(nc, args, out)
    r = run_bass_kernel_spmd(nc, [arrays], core_ids=[0])
    return r.results[0]["out_x"]
```

```python
from contextlib import ExitStack

import numpy as np

import concourse.bass as bass
from concourse import mybir

ALU = mybir.AluOpType
ACT = mybir.ActivationFunctionType
AX = mybir.AxisListType
F32 = mybir.dt.float32
F32R = mybir.dt.float32r
BF16 = mybir.dt.bfloat16

P = 128
S = 256
NT = S // P
D = 1024
KT = D // P
HD = 64
WA = 512
DIN = 3792
IN_BLOCKS = [(1152 + 440 * b, 440) for b in range(6)] + [(384 * b, 384) for b in range(3)]
NBLK_IN = len(IN_BLOCKS)
NBLK_LOOP = 4
CIN = IN_BLOCKS[0][1]
CB = 512
UNIT = 4 * CB
EPS = 1e-6
NEG = -1e30
TOPK = S // 4
SCALE = HD ** -0.5
IDX_SCALE = (8 ** -0.5) * (64 ** -0.5)
FILL = 1e8
TAKEN = -3.4e38
QA, KA, VA, GA, QI, KI, WI, QB, KB, VB, FB, GB = 0, 512, 576, 640, 1152, 1664, 1728, 1736, 2248, 2760, 3272, 3280
TOKW = 768
GW = TOKW // 4
GC = GW // 2
FF = 8
LOOK = 3
RAW = 2
RAW_IN = 4
RING = 4

U_IN = 0
U_MERGE = U_IN + 2 * NBLK_IN
U_BR = U_MERGE + 8
U_WO = U_BR + 4
U_KV1 = U_WO + 4
U_PLE = U_KV1 + 2
U_GATE = U_PLE + 1
U_KV0 = U_GATE + 4
U_POOL = U_KV0 + 2
U_OUT0 = U_POOL + 4
U_FF0 = U_OUT0 + 4
U_MOBA0 = U_FF0 + 4 * FF
U_MOBA = U_MOBA0 + 2
U_OUT1 = U_MOBA + 8
U_FF1 = U_OUT1 + 4
N_UNITS = U_FF1 + 4 * FF
N_SMALL = 13
N_EARLY = 2

HEADS = [("fox", j) for j in range(8)] + [("dsa", j) for j in range(8)] + [("mem0", j) for j in range(4)] \
    + [("mem1", j) for j in range(4)] + [("moba", j) for j in range(12)]
N_HEADS = len(HEADS)


def width0(h):
    return S if HEADS[h][0].startswith("mem") else P


RUN1 = [("idx", j) for j in range(8)] + list(range(16))
RUN2 = list(range(16, 20))
RUN3 = list(range(20, N_HEADS))
LAG_P, LAG_T, LAG_V = 1, 2, 3


def pair_of(run, pr):
    first = run[2 * pr]
    return ("idx", first[1] // 2) if isinstance(first, tuple) else (HEADS[first][0], first // 2)


def parts_at(run, s):
    out = []
    n_pairs = len(run) // 2
    nxt = (s + 1) // 2 if s % 2 else s // 2 + 1
    if s < 0:
        nxt = 0
    if nxt < n_pairs:
        kind, pr = pair_of(run, nxt)
        before = pair_of(run, nxt - 1)[0] if nxt else ""
        if s < 0 or s % 2 == 0:
            out.append(("qi" if kind == "idx" else "q", pr))
        if s < 0 or s % 2:
            if kind == "idx":
                out += [("ki", 0)] if nxt == 0 else []
            elif kind == "dsa":
                out += [("ka", 0)] if before != "dsa" else []
            else:
                out.append(("k", pr))
    if s >= 3 and s % 2:
        kind, pr = pair_of(run, (s - 3) // 2)
        if kind in ("fox", "dsa"):
            out.append(("gate", pr))
    return out


def heads_parts(run, s):
    return [part for part in parts_at(run, s) if part[0] != "gate"]


def gate_parts(run, s):
    return [part for part in parts_at(run, s) if part[0] == "gate"]


def run_steps(run):
    return range(len(run) + LAG_V)


PARTS = [part for run in (RUN1, RUN2, RUN3) for s in (-1, *run_steps(run)) for part in parts_at(run, s)]
PART = {part: n for n, part in enumerate(PARTS)}
PART_SLOT = {part: n % 2 for n, part in enumerate(q for q in PARTS if q[0] in ("qi", "q"))}
PART_SLOT.update({("k", pr): PART_SLOT[("q", pr)] for what, pr in PARTS if what == "k"})
GATES = [pr for what, pr in PARTS if what == "gate"]

BLOCKS = ["in"] * NBLK_IN + ["merge"] * 4 + ["brb"] * 2 + ["bra"] * 2 + ["wo"] * 2 + ["kv"] + ["ple"] * 2 \
    + ["gate"] * 2 + ["kv"] + ["pool"] * 2 + ["out"] * 2 + ["moba"] * 5 + ["out"] * 2
READERS = {"in": "av", "merge": "a", "kv": "av", "brb": "v", "bra": "v", "wo": "v", "ple": "a", "gate": "a",
           "pool": "av", "out": "", "moba": "av"}
B_MERGE = NBLK_IN
B_BR, B_WO, B_KV1, B_PLE, B_GATE, B_KV0, B_POOL, B_OUT0, B_MOBA0, B_MOBA, B_OUT1 = (
    B_MERGE + n for n in (4, 8, 10, 11, 13, 15, 16, 18, 20, 21, 25))
BANK_OF = {k: 0 for k in (*range(NBLK_LOOP + 1, B_BR + 2), *range(B_MOBA0, B_OUT1 + 1))}
BANK_OF |= {B_BR + 2: 2, B_BR + 3: 0, B_WO: 2, B_WO + 1: 0, B_KV1: 4, B_PLE: 2, B_PLE + 1: 4, B_GATE: 0,
            B_GATE + 1: 2, B_KV0: 4, B_POOL: 2, B_POOL + 1: 0, B_OUT0: 2, B_OUT0 + 1: 0, B_OUT1 + 1: 2,
            B_MOBA: 6}


def pair_bank(k):
    return BANK_OF.get(k, 2 * (k % 2))


def freed(k, engine):
    return 2 + sum(engine in READERS[b] for b in BLOCKS[:k + 1])


def fill_of(run, s):
    def unit_of(first, block, n):
        return [(first + n, block + n // 2, n % 2)]
    if run is RUN1:
        if s in IN_FILL:
            return unit_of(U_IN + 10, 5, IN_FILL.index(s))
        if 15 <= s < 23:
            return unit_of(U_MERGE, B_MERGE, s - 15)
        if s in (24, 26):
            return [(U_BR + s // 2 - 12, B_BR + s // 2 - 12, 2)]
    if run is RUN2:
        return []
    if run is RUN3:
        if s in MOBA_FILL:
            return unit_of(U_MOBA + 2, B_MOBA + 1, MOBA_FILL.index(s))
        return [(U_OUT1, B_OUT1, 0)] if s == run_steps(run)[-1] else []
    return []


POOL_STEPS = range(1, 5)
IN_FILL = [0, 1, 9, 10, 11, 12, 13, 14]
MOBA_FILL = [0, 1, 2, 3, 4, 5]
SQUARES_AT = {MOBA_FILL[1] + 1: ("q1", B_MOBA + 1), MOBA_FILL[1] + 2: ("k1", B_MOBA + 1),
              MOBA_FILL[3] + 1: ("q2", B_MOBA + 2), MOBA_FILL[5] + 1: ("k2", B_MOBA + 3)}
MOBA_BLOCKS = [(0, 9), (3, 6), (1, 4), (2, 7), (5, 8)]
MOBA_AT = {piece: 256 * n for n, piece in enumerate(q for b in MOBA_BLOCKS for q in b)}

G_H = 0
G_MERGED = G_H + 4
G_MEM1 = G_MERGED + 4
G_P = G_MEM1 + 4
G_X = G_P + 1
G_MEM0 = G_X + 4
G_MIX0 = G_MEM0 + 4
G_TOK0 = G_MIX0 + 4
G_MLP0 = G_TOK0 + 3
G_MIX1 = G_MLP0 + 4
G_MLP1 = G_MIX1 + 4
NORMED = ["memk1", "memk0", "memq0", "memq1", "q0", "k0", "q1", "k1", "q2", "k2"]
N_NORMED = len(NORMED)
X_PLE, X_OUT0, X_FF0, X_OUT1, X_FF1 = 0, 2, 4, 6, 8
GAIN_PRE, GAIN_MIX, GAIN_MEM, GAIN_MLP = 0, 8, 24, 40


def build(nc, a, out):
    with ExitStack() as ctx:
        def sb(name, shape, dt=F32):
            return ctx.enter_context(nc.sbuf_tensor(name, shape, dt))

        def sem(name):
            return ctx.enter_context(nc.semaphore(name))

        raw = sb("raw", [P, RAW, UNIT])
        w_hi = sb("w_hi", [P, RING, UNIT], F32R)
        w_lo = sb("w_lo", [P, RING, UNIT], F32R)
        x = sb("x", [P, NT, D])
        tok = sb("tok", [P, NT, D])
        a_hi = sb("a_hi", [P, KT, S], F32R)
        a_lo = sb("a_lo", [P, KT, S], F32R)
        b_hi = sb("b_hi", [P, KT, S], F32R)
        b_lo = sb("b_lo", [P, KT, S], F32R)
        proj = sb("proj", [P, NT * DIN])
        m = sb("m", [P, NT * 2 * D])
        qk = sb("qk", [P, 2, 2, S])
        kT = sb("kT", [P, S])
        memkv = sb("memkv", [P, 2, NT, CB])
        ident = sb("ident", [P, P])
        ident_b = sb("ident_b", [P, P], BF16)
        mask = sb("mask", [P, P])
        mask_b = sb("mask_b", [P, P], BF16)
        tri = sb("tri", [P, S])
        rope_a = sb("rope_a", [P, 2, NT, 8])
        rope_m = sb("rope_m", [P, 2, NT, 32])
        gain_cols = sb("gain_cols", [P, 56])
        gain_bc = sb("gain_bc", [P, D])
        head_gain = sb("head_gain", [P, 6, HD])
        bias_f = sb("bias_f", [P, 8])
        prob = sb("prob", [P, 2, 2 * S])
        probT = sb("probT", [P, 2, 2 * S])
        top8 = sb("top8", [P, NT, 8])
        sel_b = sb("sel_b", [P, P + S], BF16)
        wis = sb("wis", [P, NT, 8])
        fgt = sb("fgt", [P, 6, NT, 8])
        mx = sb("mx", [P, N_HEADS, NT])
        nmx = sb("nmx", [P, N_HEADS, NT])
        psums = sb("psums", [P, N_HEADS, NT])
        prec = sb("prec", [P, N_HEADS, NT])
        stat = sb("stat", [P, 4, 8, 2 * NT])
        hstat = sb("hstat", [P, N_NORMED, 2, NT * 4])
        half = sb("half", [P, NT * 4])

        bank = [ctx.enter_context(nc.psum_tensor(f"bank{i}", [P, 512], F32)) for i in range(8)]
        b_t, b_io, b_s, b_v, b_tr = bank[2], bank[3], bank[4:6], bank[7], bank[6:8]
        b_hid = bank[4:8]

        def group_bank(g):
            if g - G_MLP0 in (2, 3) or g - G_MLP1 in (2, 3):
                return bank[g % 2]
            return bank[4 + g] if g < 4 else b_tr[g % 2]

        pj = proj[:].rearrange("p (t n) -> p t n", t=NT)
        xf = x[:].rearrange("p t n -> p (t n)")
        score, gate_s, gated, cT = xf[:, 0:P + S], xf[:, 384:640], xf[:, 640:896], xf[0:8, 896:1152]
        rope_t = xf[:, 1152:1728].rearrange("p (q t n d) -> p q t n d", q=4, t=NT, n=9)
        k_twice = xf[:, 1728:1984].rearrange("p (t q d) -> p t q d", t=NT, q=2)
        mem_tmp = probT[:, 0, :]
        p_tok = prob[:, :, 0:S]
        pre_rows, gain_rows = memkv[0:8, 0, 0, 0:P], memkv[0:48, 0, 0, P:2 * P]
        landing = [raw[:, 0, :], raw[:, 1, :], m[:, 0:UNIT], m[:, UNIT:2 * UNIT]]
        m_sig = m[:].rearrange("p (t n) -> p t n", t=NT)
        e_tok = m[:, 0:NT * D].rearrange("p (t n) -> p t n", t=NT)
        m_lo = m[:, 0:NT * D].rearrange("p (t n) -> p t n", t=NT)
        m_hi = m[:, NT * D:].rearrange("p (t n) -> p t n", t=NT)
        band = m[:, 0:NT * 4 * S].rearrange("p (t g n) -> p t g n", t=NT, g=4)
        w_group = m[0:GC, NT * 4 * S:NT * 4 * S + 8 * GW].rearrange("p (g c n) -> p g c n", g=4, c=2)
        h_pool = proj[:, 0:NT * D].rearrange("p (t n) -> p t n", t=NT)
        dT = proj[0:GC, NT * D:NT * D + 8 * S].rearrange("p (g c n) -> p g c n", g=4, c=2)
        h_moba = proj[:, 0:NT * 2560].rearrange("p (t n) -> p t n", t=NT)
        rot_scaled, rot_sin = m[:, 2 * S:4 * S], m[:, 6 * S:8 * S]
        rot_tab = m[:, 4 * S:6 * S].rearrange("p (w t c d) -> p w t c d", w=2, t=NT, c=2)
        hidden = tok[:, 0, :].rearrange("p (k n) -> p k n", k=4)

        raw_landed = [sem(f"raw_landed{i}") for i in range(RAW_IN)]
        hi_ready, lo_ready, unit_used = sem("hi_ready"), sem("lo_ready"), sem("unit_used")
        free_a, free_v = sem("banks_free_a"), sem("banks_free_v")
        tr_ready, tr_hi, tr_lo = sem("tr_ready"), sem("tr_hi"), sem("tr_lo")
        x_landed, const_landed, mem_landed, p_landed, bc_landed = (sem(n) for n in (
            "x_landed", "const_landed", "mem_landed", "p_landed", "bc_landed"))
        pool_landed, x_again, out_landed = sem("pool_landed"), sem("x_again"), sem("out_landed")
        consts_made, gains_tr, gains_made = sem("consts_made"), sem("gains_tr"), sem("gains_made")
        sq_done, rstd_done = sem("sq_done"), sem("rstd_done")
        part_tr, part_cp, gate_cp = sem("part_tr"), sem("part_cp"), sem("gate_cp")
        idx_s, idx_relu, idx_acc, sel_made = sem("idx_s"), sem("idx_relu"), sem("idx_acc"), sem("sel_made")
        rope_idx, rope_dsa = sem("rope_idx"), sem("rope_dsa")
        f_abs, f_ln, f_log, c_ready, c_made = sem("f_abs"), sem("f_ln"), sem("f_log"), sem("c_ready"), sem("c_made")
        s_ready, max_done, exp_done, p_ready, pt_ready, pt_copied, pv_done, pair_read = (sem(n) for n in (
            "s_ready", "max_done", "exp_done", "p_ready", "pt_ready", "pt_copied", "pv_done", "pair_read"))
        pair_tmp, pair_hi, pair_lo = sem("pair_tmp"), sem("pair_hi"), sem("pair_lo")
        memk_made, memq_made, moba_made = sem("memk_made"), sem("memq_made"), sem("moba_made")
        early_landed, half_rstd, x_half = sem("early_landed"), sem("half_rstd"), sem("x_half")
        tile_done, x_tile = sem("tile_done"), sem("x_tile")
        merge_sig, merged, x_post, z_made = sem("merge_sig"), sem("merged"), sem("x_post"), sem("z_made")
        ple_block, d_copied_a, d_copied_v = sem("ple_block"), sem("d_copied_a"), sem("d_copied_v")
        d_ready, y_ready, y_made = sem("d_ready"), sem("y_ready"), sem("y_made")
        ff_relu, ff_sq, ff_hi, ff_lo, rstd_sq = sem("ff_relu"), sem("ff_sq"), sem("ff_hi"), sem("ff_lo"), sem("rstd_sq")
        head_sum, ident_made = sem("head_sum"), sem("ident_made")
        act_chain, vec_chain, pool_chain = sem("act_chain"), sem("vec_chain"), sem("pool_chain")

        class Linker:

            def __init__(self, eng, chain):
                self.eng, self.chain, self.n = eng, chain, 0

            def step(self):
                self.n += 1
                return self.chain, 1

            def wait(self):
                self.eng.wait_ge(self.chain, self.n)

            def __call__(self, ins):
                ins.then_inc(*self.step())
                self.wait()

        def head_cols(h):
            kind, j = HEADS[h]
            pr = j // 2
            h0 = pj[:, :, :]
            pool = proj[:, 0:NT * D].rearrange("p (t n) -> p t n", t=NT)
            if kind == "fox":
                return dict(q=h0[:, :, QB + P * pr:QB + P * pr + P], k=h0[:, :, KB + P * pr:KB + P * pr + P],
                            gate=h0[:, :, GB + P * pr:GB + P * pr + P], v=h0[:, :, VB + HD * j:VB + HD * j + HD])
            if kind == "dsa":
                return dict(q=h0[:, :, QA + P * pr:QA + P * pr + P], gate=h0[:, :, GA + P * pr:GA + P * pr + P],
                            v=h0[:, :, VA:VA + HD])
            if kind == "moba":
                q, k, v = (MOBA_AT[j // 4 + 3 * n] for n in range(3))
                c = P * (pr % 2)
                return dict(q=h_moba[:, :, q + c:q + c + P], k=h_moba[:, :, k + c:k + c + P],
                            v=h_moba[:, :, v + HD * (j % 4):v + HD * (j % 4) + HD])
            lay = int(kind[3])
            src = pool[:, :, TOKW:] if lay == 0 else h_moba[:, :, MOBA_AT[9]:MOBA_AT[9] + S]
            return dict(q=src[:, :, P * pr:P * pr + P], k=memkv[:, lay, :, P * pr:P * pr + P],
                        v=memkv[:, lay, :, S + HD * j:S + HD * j + HD])

        def pair_ktile(pr):
            kind, j = HEADS[2 * pr]
            return {"fox": 4, "dsa": 0, "mem0": 6, "moba": 0, "mem1": 6}[kind] + j // 2

        def unit_source(u):
            def cut(w, half_, c, n=CB):
                return w.rearrange("(k p) n -> p k n", p=P)[:, 4 * half_:4 * half_ + 4, c * n:c * n + n]
            if u < U_MERGE:
                c, n = IN_BLOCKS[u // 2]
                return a["w_in"][0].rearrange("(k p) n -> p k n", p=P)[:, 4 * (u % 2):4 * (u % 2) + 4, c:c + n]
            if U_MERGE <= u < U_BR:
                return cut(a["w_merge"][0], u % 2, (u - U_MERGE) // 2)
            if U_BR <= u < U_WO:
                return cut(a["w_branch_b" if u < U_BR + 2 else "w_branch_a"][0], 0, (u - U_BR) % 2)
            if U_WO <= u < U_KV1:
                return cut(a["w_out"][0], (u - U_WO) % 2, (u - U_WO) // 2)
            if u == U_PLE:
                return a["w_ple"][0].rearrange("(k p) n -> p k n", p=P)
            if U_GATE <= u < U_KV0:
                return cut(a["w_ple_gate"][0], (u - U_GATE) % 2, (u - U_GATE) // 2)
            if U_KV0 <= u < U_POOL:
                return cut(a["w_mem_kv_2"][0], u - U_KV0, 0)
            if U_POOL <= u < U_OUT0:
                return cut(a["w_in_pool_2"][0], (u - U_POOL) % 2, 1 - (u - U_POOL) // 2)
            if U_OUT0 <= u < U_FF0:
                return cut(a["w_out_2"][0], (u - U_OUT0) % 2, (u - U_OUT0) // 2)
            if U_MOBA0 <= u < U_OUT1:
                n = u - U_MOBA0
                i, j = MOBA_BLOCKS[n // 2]
                w = a["w_in_moba_2"][0].rearrange("(k p) (j n) -> p k j n", p=P, n=S)
                return w[:, 4 * (n % 2):4 * (n % 2) + 4, i:j + 1:j - i, :]
            if U_KV1 <= u < U_PLE:
                return cut(a["w_mem_kv_2"][1], u - U_KV1, 0)
            if U_OUT1 <= u < U_FF1:
                return cut(a["w_out_2"][1], (u - U_OUT1) % 2, (u - U_OUT1) // 2)
            base, lay = (U_FF0, 0) if u < U_MOBA0 else (U_FF1, 1)
            r = u - base
            if r < 2:
                return cut(a["w_ff1_2"][lay], r, 0)
            i, r = divmod(r - 2, 4)
            if r < 2 and i < FF - 1:
                return cut(a["w_ff1_2"][lay], r, i + 1)
            return a["w_ff2_2"][lay].rearrange("(i k p) n -> p i k n", p=P, k=4)[:, i, :, (r % 2) * CB:(r % 2) * CB + CB]

        def land_slot(u):
            return u % (RAW_IN if u < U_MERGE else RAW)

        def landed(u):
            before = [v for v in range(u + 1) if land_slot(v) == land_slot(u)]
            return len(before) + sum(U_MOBA0 <= v < U_OUT1 for v in before)

        def unit_size(u):
            return 4 * IN_BLOCKS[u // 2][1] if u < U_MERGE else UNIT

        def normed_heads(what):
            if what.startswith("memk"):
                v = memkv[:, int(what[4]), :, 0:S]
            elif what.startswith("memq"):
                v = h_pool[:, :, TOKW:D] if what == "memq0" else h_moba[:, :, MOBA_AT[9]:MOBA_AT[9] + S]
            else:
                c = MOBA_AT[int(what[1]) + 3 * (what[0] == "k")]
                v = h_moba[:, :, c:c + S]
            return v.rearrange("p t (n d) -> p t n d", d=HD)

        block = ctx.enter_context(nc.Block())

        @block.sync
        def _(sp):
            def load(u, slot, src, n):
                ahead = RAW_IN if isinstance(u, int) and u < U_MERGE else RAW
                if not isinstance(u, int) or u >= ahead:
                    sp.wait_ge(lo_ready, u - ahead + 1)
                if len(src.shape) == 3:
                    sp.dma_start(landing[slot][:, 0:n].rearrange("p (k n) -> p k n", k=src.shape[1]), src)\
                        .then_inc(raw_landed[slot], 16)
                else:
                    dst = landing[slot][:, 0:n].rearrange("p (k j n) -> p k j n", k=src.shape[1], j=2)
                    for j in range(2):
                        sp.dma_start(dst[:, :, j, :], src[:, :, j, :]).then_inc(raw_landed[slot], 16)

            def load_plain(first, last):
                for u in range(first, last):
                    load(u, land_slot(u), unit_source(u), unit_size(u))

            for t in range(NT):
                sp.dma_start(x[:, t, :], a["x"][0, t * P:(t + 1) * P, :]).then_inc(x_landed, 16)
            def mlp(base, lay):
                w1 = a["w_ff1_2"][lay].rearrange("(k p) n -> p k n", p=P)
                w2 = a["w_ff2_2"][lay].rearrange("(i k p) n -> p i k n", p=P, k=4)
                load_plain(base, base + 2)
                with sp.Fori(0, FF - 1) as i:
                    for r in range(2):
                        load(base + 2 + 4 * i + r, (base + r) % RAW,
                             w1[:, 4 * r:4 * r + 4, bass.ds(i * CB + CB, CB)], UNIT)
                    for r in range(2):
                        src = w2[:, bass.ds(i, 1), :, r * CB:r * CB + CB].rearrange("p i k n -> p (i k) n")
                        load(base + 4 + 4 * i + r, (base + r) % RAW, src, UNIT)
                load_plain(base + 4 * FF - 2, base + 4 * FF)

            load_plain(0, U_FF0)
            mlp(U_FF0, 0)
            load_plain(U_MOBA0, U_FF1)
            mlp(U_FF1, 1)
            sp.wait_ge(x_half, X_FF1 + 1)
            sp.dma_start(out[0].rearrange("(t p) n -> p t n", p=P)[:, :, 0:CB], x[:, :, 0:CB]).then_inc(out_landed, 16)
            for t in range(NT):
                sp.wait_ge(x_tile, t + 1)
                sp.dma_start(out[0, t * P:(t + 1) * P, CB:D], x[:, t, CB:D]).then_inc(out_landed, 16)
            sp.wait_ge(out_landed, 16 * (1 + NT))

        @block.gpsimd
        def _(gp):
            link = Linker(gp, pool_chain)
            small = [(gain_rows[0:16, :], a["g_mix_2"].rearrange("l (k p) -> (l k) p", p=P)),
                     (gain_rows[16:32, :], a["g_mem_2"].rearrange("l (k p) -> (l k) p", p=P)),
                     (gain_rows[32:48, :], a["g_mlp_2"].rearrange("l (k p) -> (l k) p", p=P)),
                     (mask[:], a["c_mask"]), (tri[:], a["c_tri"]),
                     (bias_f[:], a["b_forget"][0].partition_broadcast(P)),
                     (rope_a[:], a["c_rope_a"].rearrange("c (t p) n -> p c t n", p=P)),
                     (rope_m[:], a["c_rope_m"].rearrange("c (t p) n -> p c t n", p=P)),
                     (head_gain[:, 0, :], a["moba_q_gain_2"][0].partition_broadcast(P)),
                     (head_gain[:, 1, :], a["moba_k_gain_2"][0].partition_broadcast(P)),
                     (head_gain[:, 2:4, :], a["mem_q_gain_2"].partition_broadcast(P)),
                     (head_gain[:, 4:6, :], a["mem_k_gain_2"].partition_broadcast(P)),
                     (gain_bc[:], a["g_post"][0].partition_broadcast(P))]
            link(gp.memset(half[:], -0.5))

            def rstd(r, count, cols, eps):
                link(gp.tensor_scalar(stat[:, 1, r, 0:cols], stat[:, 0, r, 0:cols], 1.0 / count, eps, ALU.mult, ALU.add))
                gp.tensor_tensor(stat[:, 2, r, 0:cols], stat[:, 1, r, 0:cols], half[:, 0:cols], ALU.pow).then_inc(rstd_done, 1)

            gp.wait_ge(sq_done, 2)
            rstd(0, D, NT, EPS)
            gp.wait_ge(rstd_done, 1)
            gp.tensor_scalar(stat[:, 3, 0, 0:NT], stat[:, 2, 0, 0:NT], 0.5, None, ALU.mult).then_inc(half_rstd, 1)
            for dst, src in small:
                gp.dma_start(dst, src).then_inc(const_landed, 16)
            assert len(small) == N_SMALL

            def blocks_read(k):
                gp.wait_ge(free_a, freed(k, "a"))
                gp.wait_ge(free_v, freed(k, "v"))

            def rotate(c0, done):
                v = pj[:, :, c0:c0 + 9 * HD].rearrange("p t (n d) -> p t n d", d=HD)
                x1, x2 = v[:, :, :, 0:8], v[:, :, :, 8:16]
                for t in range(NT):
                    cs, sn = (rope_a[:, q, t, :].unsqueeze(1).to_broadcast([P, 9, 8]) for q in range(2))
                    for q, (src, f) in enumerate(((x1, cs), (x2, sn), (x2, cs), (x1, sn))):
                        gp.tensor_tensor(rope_t[:, q, t], src[:, t], f, ALU.mult).then_inc(*link.step())
                link.wait()
                gp.tensor_tensor(x1, rope_t[:, 0], rope_t[:, 1], ALU.subtract).then_inc(*link.step())
                gp.tensor_tensor(x2, rope_t[:, 2], rope_t[:, 3], ALU.add).then_inc(*link.step())
                link.wait()
                if done is rope_dsa:
                    gp.wait_ge(part_tr, PART[("ki", 0)] + 1)
                for q in range(2):
                    gp.tensor_copy(k_twice[:, :, q, :], pj[:, :, c0 + 8 * HD:c0 + 9 * HD]).then_inc(*link.step())
                link.wait()
                gp.sem_inc(done, 1)

            gp.wait_ge(const_landed, 16 * N_SMALL)
            blocks_read(1)
            rotate(QI, rope_idx)
            blocks_read(7)
            rotate(QA, rope_dsa)
            gp.wait_ge(pt_ready, 16)
            gp.wait_ge(pt_copied, 16)
            gp.dma_start(p_tok, a["p"][0, 0].rearrange("(t p) n -> p t n", p=P)).then_inc(p_landed, 16)
            gp.wait_ge(pair_lo, 8)
            gp.dma_start(x[:], a["x"][0].rearrange("(t p) n -> p t n", p=P)).then_inc(x_again, 16)
            gp.wait_ge(tr_ready, G_MERGED + 4)
            gp.dma_start(tok[:], a["mem_2"][0].rearrange("(t p) n -> p t n", p=P)).then_inc(mem_landed, 16)

            def rstd_of_halves(r, eps):
                gp.wait_ge(sq_done, 2 * r + 2)
                link(gp.tensor_tensor(stat[:, 0, r, 0:NT], stat[:, 0, r, 0:NT], stat[:, 0, r, NT:2 * NT], ALU.add))
                rstd(r, D, NT, eps)

            gp.wait_ge(sq_done, 4)
            rstd(1, D, NT, EPS)
            rstd_of_halves(2, EPS)
            def head_factor(what):
                i = NORMED.index(what)
                gp.wait_ge(head_sum, i + 1)
                r = hstat[:, i, 1, :]
                link(gp.tensor_scalar(r, hstat[:, i, 0, :], 1.0 / HD, EPS, ALU.mult, ALU.add))
                link(gp.tensor_tensor(r, r, half[:], ALU.pow))
                return r.rearrange("p (t n) -> p t n", t=NT).unsqueeze(3).to_broadcast([P, NT, 4, HD])

            def memq_norm(what, gain):
                i = NORMED.index(what)
                gp.wait_ge(head_sum, i + 1)
                mean, r, power = (a_.rearrange("p (t n) -> p t n", t=NT) for a_ in
                                  (hstat[:, i, 0, :], hstat[:, i, 1, :], half[:]))
                v = normed_heads(what)
                for pr in range(2):
                    hs = slice(2 * pr, 2 * pr + 2)
                    link(gp.tensor_scalar(r[:, :, hs], mean[:, :, hs], 1.0 / HD, EPS, ALU.mult, ALU.add))
                    link(gp.tensor_tensor(r[:, :, hs], r[:, :, hs], power[:, :, hs], ALU.pow))
                    link(gp.tensor_tensor(v[:, :, hs], v[:, :, hs],
                                          r[:, :, hs].unsqueeze(3).to_broadcast([P, NT, 2, HD]), ALU.mult))
                    gp.tensor_tensor(v[:, :, hs], v[:, :, hs],
                                     gain.unsqueeze(1).unsqueeze(1).to_broadcast([P, NT, 2, HD]), ALU.mult)\
                      .then_inc(memq_made, 1)

            def mem_norm(what, gain, done):
                v = normed_heads(what)
                link(gp.tensor_tensor(v, v, head_factor(what), ALU.mult))
                gp.tensor_tensor(v, v, gain.unsqueeze(1).unsqueeze(1).to_broadcast([P, NT, 4, HD]), ALU.mult)\
                  .then_inc(done, 1)

            def norm_and_rotate(what):
                v, w = normed_heads(what), int(what[0] == "k")
                scaled = rot_scaled.rearrange("p (t n d) -> p t n d", t=NT, d=HD)
                by_sin = rot_sin.rearrange("p (t n d) -> p t n d", t=NT, d=HD)
                cos, sin = (rot_tab[:, w, :, c, :].unsqueeze(2).to_broadcast([P, NT, 4, HD]) for c in range(2))
                link(gp.tensor_tensor(scaled, v, head_factor(what), ALU.mult))
                gp.tensor_tensor(v, scaled, cos, ALU.mult).then_inc(*link.step())
                link(gp.tensor_tensor(by_sin, scaled, sin, ALU.mult))
                h = HD // 2
                gp.tensor_tensor(v[:, :, :, 0:h], v[:, :, :, 0:h], by_sin[:, :, :, h:HD], ALU.subtract)\
                  .then_inc(*link.step())
                gp.tensor_tensor(v[:, :, :, h:HD], v[:, :, :, h:HD], by_sin[:, :, :, 0:h], ALU.add)\
                  .then_inc(*link.step())
                link.wait()
                gp.sem_inc(moba_made, 1)

            mem_norm("memk1", head_gain[:, 5, :], memk_made)
            gp.wait_ge(x_post, 2)
            gp.dma_start(gain_bc[:], a["g_ple"][0].partition_broadcast(P)).then_inc(bc_landed, 16)
            rstd_of_halves(3, 4 * EPS)
            gp.wait_ge(x_half, X_PLE + 2)
            gp.dma_start(gain_bc[:, 0:TOKW], a["pool_scale_2"][0].partition_broadcast(P)).then_inc(pool_landed, 16)
            for t in range(NT):
                gp.dma_start(band[:, t], a["c_band"][:, t * P:(t + 1) * P, :].rearrange("g p n -> p g n"))\
                    .then_inc(pool_landed, 16)
            for g in range(4):
                gp.dma_start(w_group[:, g], a["w_pool_group_2"][0, g].rearrange("(c p) n -> p c n", p=GC))\
                    .then_inc(pool_landed, 16)
            gp.wait_ge(sq_done, 10)
            rstd(4, D, NT, EPS)
            mem_norm("memk0", head_gain[:, 4, :], memk_made)
            memq_norm("memq0", head_gain[:, 2, :])

            def rstd_squared(r):
                gp.wait_ge(rstd_done, r + 1)
                gp.tensor_tensor(stat[:, 3, r, 0:NT], stat[:, 2, r, 0:NT], stat[:, 2, r, 0:NT], ALU.mult).then_inc(rstd_sq, 1)

            gp.wait_ge(sq_done, 12)
            rstd(5, D, NT, EPS)
            rstd_squared(5)
            for w in range(2):
                for t in range(NT):
                    for c in range(2):
                        for h in (0, HD // 2):
                            gp.tensor_tensor(rot_tab[:, w, t, c, h:h + HD // 2], rope_m[:, c, t, :],
                                             head_gain[:, w, h:h + HD // 2], ALU.mult).then_inc(*link.step())
            link.wait()
            gp.wait_ge(sq_done, 14)
            rstd(6, D, NT, EPS)
            memq_norm("memq1", head_gain[:, 3, :])
            for what in ("q0", "k0", "q1", "k1", "q2", "k2"):
                norm_and_rotate(what)
            gp.wait_ge(sq_done, 16)
            rstd(7, D, NT, EPS)
            rstd_squared(7)

        @block.scalar
        def _(act):
            def split(u, slot, land, n):
                act.wait_ge(raw_landed[land], 16 * landed(u))
                if u >= RING:
                    act.wait_ge(unit_used, u - RING + 2)
                act.activation(w_hi[:, slot, 0:n], landing[land][:, 0:n], ACT.Copy).then_inc(hi_ready, 1)

            def unit(u):
                v = u + LOOK
                if v < N_UNITS:
                    split(v, v % RING, land_slot(v), unit_size(v))

            def group(g, dst, k, gain=None):
                act.wait_ge(tr_ready, g + 1)
                ps = group_bank(g)
                if gain is None:
                    act.activation(dst[:, k:k + 2, :], ps[:, :].rearrange("p (k n) -> p k n", k=2), ACT.Copy)\
                       .then_inc(tr_hi, 1)
                else:
                    act.activation(dst[:, k, :], ps[:, 0:S], ACT.Copy, scale=gain_cols[:, gain + k:gain + k + 1])
                    act.activation(dst[:, k + 1, :], ps[:, S:2 * S], ACT.Copy,
                                   scale=gain_cols[:, gain + k + 1:gain + k + 2]).then_inc(tr_hi, 1)

            def groups(g0, first, dst, gain=None):
                for q in range(first, first + 2):
                    group(g0 + q, dst, 2 * q, gain)

            def squares(r, src, junk):
                for t in range(NT):
                    act.activation(junk[t], src[:, t], ACT.Square, accum_out=stat[:, 0, r, t:t + 1])\
                       .then_inc(sq_done, 1)

            def squares_half(r, c, src):
                for t in range(NT):
                    ins = act.activation(m_hi[:, t, c * CB:c * CB + CB], src[t], ACT.Square,
                                         accum_out=stat[:, 0, r, NT * c + t:NT * c + t + 1])
                    if c == 1:
                        ins.then_inc(sq_done, 1)

            def x_squares(r, count, junk):
                act.wait_ge(x_half, count)
                squares(r, x, [junk[:, t] for t in range(NT)])

            def block_done(u):
                act.wait_ge(unit_used, u + 2)

            def scaled(dst, k, r, n=CB):
                act.wait_ge(rstd_done, r + 1)
                act.activation(dst, bank[pair_bank(k)][:, 0:n], ACT.Copy, scale=stat[:, 2, r, 0:1]).then_inc(free_a, 1)

            def evac(k):
                kind = BLOCKS[k]
                if kind == "in":
                    c, n = IN_BLOCKS[k]
                    scaled(pj[:, 0, c:c + n], k, 0, n)
                if kind == "merge":
                    c = (k - B_MERGE) * CB
                    for t in range(NT):
                        ins = act.activation(m_sig[:, t, c:c + CB], bank[pair_bank(k) + t][:, :], ACT.Tanh,
                                             scale=stat[:, 3, 0, t:t + 1])
                    ins.then_inc(free_a, 1)
                if kind == "kv":
                    scaled(memkv[:, int(k == B_KV1), 0, :], k, 1)
                if kind == "pool":
                    c = (1 - (k - B_POOL)) * CB
                    scaled(h_pool[:, 0, c:c + CB], k, 4)
                if kind == "moba":
                    c = (0 if k == B_MOBA0 else k - B_MOBA + 1) * CB
                    scaled(h_moba[:, 0, c:c + CB], k, 6)

            def dense(u, k, run):
                unit(u)
                unit(u + 1)
                for what in parts_at(run, -1):
                    part(*what)
                block_done(u + 1)
                evac(k)

            def fill(run, s):
                for u, k, half_ in fill_of(run, s):
                    unit(u)
                    if half_ and BLOCKS[k] != "brb":
                        block_done(u)
                        evac(k)

            def part(what, pr):
                act.wait_ge(part_tr, PART[(what, pr)] + 1)
                ps = b_io[:, 0:S]
                if what == "gate":
                    if GATES.index(pr):
                        act.wait_ge(pair_lo, GATES.index(pr))
                    act.activation(gated[:], ps, ACT.Tanh, scale=0.5).then_inc(part_cp, 1)
                    return
                dst = {"ki": kT[:], "ka": kT[:]}.get(what)
                if dst is None:
                    dst = qk[:, PART_SLOT[(what, pr)], 0 if what in ("qi", "q") else 1, :]
                act.activation(dst, ps, ACT.Copy).then_inc(part_cp, 1)

            def step(run, s):
                for what in heads_parts(run, s):
                    part(*what)
                if LAG_T <= s < len(run) + LAG_T and not isinstance(run[s - LAG_T], tuple):
                    h = run[s - LAG_T]
                    n = width0(h) + S
                    act.wait_ge(pt_ready, h + 1)
                    if h >= 2:
                        act.wait_ge(pv_done, h - 1)
                    act.activation(probT[:, h % 2, 0:n], b_t[:, 0:n], ACT.Copy).then_inc(pt_copied, 1)
                if 0 <= s < len(run):
                    h = run[s]
                    if isinstance(h, tuple):
                        n = h[1]
                        act.wait_ge(idx_s, n + 1)
                        if n >= 2:
                            act.wait_ge(idx_acc, n - 1)
                        act.activation(prob[:, n % 2, 0:P + S], b_s[n % 2][:, 0:P + S], ACT.Relu).then_inc(idx_relu, 1)
                    else:
                        w0 = width0(h)
                        act.wait_ge(max_done, h + 1)
                        if h < 2:
                            act.wait_ge(idx_acc, 7 + h)
                        else:
                            act.wait_ge(pt_ready, h - 1)
                        act.activation(prob[:, h % 2, 0:w0], b_s[h % 2][:, 0:w0], ACT.Exp, scale=SCALE,
                                       bias=nmx[:, h, 0:1], accum_out=psums[:, h, 0:1])
                        act.activation(prob[:, h % 2, w0:w0 + S], b_s[h % 2][:, w0:w0 + S], ACT.Exp, scale=SCALE,
                                       bias=nmx[:, h, 1:2], accum_out=psums[:, h, 1:2]).then_inc(exp_done, 1)
                for what in gate_parts(run, s):
                    part(*what)
                if LAG_V <= s and not isinstance(run[s - LAG_V], tuple) and run[s - LAG_V] % 2:
                    h = run[s - LAG_V]
                    pr = h // 2
                    if HEADS[h][0] in ("fox", "dsa"):
                        act.wait_ge(pair_tmp, GATES.index(pr) + 1)
                        act.activation(b_hi[:, pair_ktile(pr), :], gated[:], ACT.Copy).then_inc(pair_hi, 1)
                    else:
                        act.wait_ge(pv_done, h + 1)
                        act.activation(b_hi[:, pair_ktile(pr), :], b_v[:, 0:S], ACT.Copy).then_inc(pair_hi, 1)

            early = [(ident[:], a["c_ident"]), (pre_rows, a["g_pre"][0].rearrange("(k p) -> k p", p=P))]
            assert len(early) == N_EARLY
            for dst, src in early:
                act.dma_start(dst, src).then_inc(early_landed, 16)
            act.sem_inc(free_a, 2)
            act.wait_ge(early_landed, 16 * N_EARLY)
            act.activation(ident_b[:], ident[:], ACT.Copy).then_inc(ident_made, 1)
            act.wait_ge(gains_made, 1)
            group(G_H, a_hi, 0, GAIN_PRE)
            group(G_H + 1, a_hi, 2, GAIN_PRE)
            split(0, 0, 0, unit_size(0))
            groups(G_H, 2, a_hi, GAIN_PRE)
            split(1, 1, 1, unit_size(1))
            squares(0, x, [tok[:, t] for t in range(NT)])
            split(2, 2, 2, unit_size(2))
            act.wait_ge(rstd_done, 1)
            with act.Fori(0, NBLK_LOOP // 2) as i:
                for j in range(4):
                    c = j + LOOK
                    act.wait_ge(raw_landed[c % RAW_IN], (i + (c // RAW_IN + 1)) * 16)
                    act.wait_ge(unit_used, i * 4 + (c - RING + 2))
                    act.activation(w_hi[:, c % RING, 0:4 * CIN], landing[c % RAW_IN][:, 0:4 * CIN], ACT.Copy)\
                       .then_inc(hi_ready, 1)
                    if j % 2:
                        act.wait_ge(unit_used, i * 4 + (j + 2))
                        act.activation(proj[:, bass.ds((i * 2 + j // 2) * CIN + IN_BLOCKS[0][0], CIN)],
                                       bank[2 * (j // 2)][:, 0:CIN], ACT.Copy, scale=stat[:, 2, 0, 0:1]).then_inc(free_a, 1)
            dense(2 * NBLK_LOOP, NBLK_LOOP, RUN1)

            act.wait_ge(half_rstd, 1)

            for s in run_steps(RUN1):
                step(RUN1, s)
                if s == 1:
                    act.wait_ge(f_abs, 1)
                    act.activation(fgt[:, 2], fgt[:, 1], ACT.Exp).then_inc(act_chain, 1)
                    act.wait_ge(act_chain, 1)
                    act.activation(fgt[:, 3], fgt[:, 2], ACT.Ln, bias=1.0).then_inc(f_ln, 1)
                fill(RUN1, s)
            unit(U_BR + 2)
            unit(U_BR + 3)
            groups(G_MERGED, 0, a_hi)
            unit(U_WO)
            groups(G_MERGED, 2, a_hi)
            unit(U_WO + 1)
            block_done(U_WO + 1)
            squares_half(2, 0, [bank[pair_bank(B_WO) + t][:, :] for t in range(NT)])
            unit(U_WO + 2)
            groups(G_MEM1, 0, b_hi, GAIN_MEM + 8)
            unit(U_WO + 3)
            act.wait_ge(mem_landed, 16)
            squares(1, tok, [m_lo[:, t, :] for t in range(NT)])
            groups(G_MEM1, 2, b_hi, GAIN_MEM + 8)
            block_done(U_WO + 3)
            squares_half(2, 1, [bank[pair_bank(B_WO + 1) + t][:, :] for t in range(NT)])
            unit(U_KV1)
            group(G_P, a_hi, 6)
            unit(U_KV1 + 1)
            block_done(U_KV1 + 1)
            evac(B_KV1)
            unit(U_PLE)
            groups(G_X, 0, a_hi)
            for c in range(2):
                act.wait_ge(ple_block, c + 1)
                for t in range(NT):
                    ins = act.activation(e_tok[:, t, c * CB:c * CB + CB], bank[pair_bank(B_PLE + c) + t][:, :], ACT.Copy)
                ins.then_inc(free_a, 1)

            def gate_half(c):
                for t in range(NT):
                    ins = act.activation(m_hi[:, t, c * CB:c * CB + CB], bank[pair_bank(B_GATE + c) + t][:, :], ACT.Tanh,
                                         scale=0.5)
                ins.then_inc(free_a, 1)

            def gated_squares(c):
                act.wait_ge(z_made, c + 1)
                squares_half(3, c, [e_tok[:, t, c * CB:c * CB + CB] for t in range(NT)])

            unit(U_GATE)
            groups(G_X, 2, a_hi)
            unit(U_GATE + 1)
            groups(G_MEM0, 0, b_hi, GAIN_MEM)
            block_done(U_GATE + 1)
            gate_half(0)
            unit(U_GATE + 2)
            gated_squares(0)
            unit(U_GATE + 3)
            groups(G_MEM0, 2, b_hi, GAIN_MEM)
            block_done(U_GATE + 3)
            gate_half(1)
            gated_squares(1)
            unit(U_KV0)
            groups(G_MIX0, 0, a_hi, GAIN_MIX)
            unit(U_KV0 + 1)
            block_done(U_KV0 + 1)
            evac(B_KV0)

            def mlp(base, lay, r, gx, gain):
                def hidden_relu(used, free):
                    act.wait_ge(unit_used, used)
                    if free is not None:
                        act.wait_ge(ff_lo, free)
                    for f in range(4):
                        act.activation(hidden[:, f, :], b_hid[f][:, 0:S], ACT.Relu).then_inc(ff_relu, 1)

                def hidden_hi(n, used, k=0):
                    act.wait_ge(ff_sq, n)
                    act.wait_ge(unit_used, used)
                    act.activation(b_hi[:, k:k + 4, :], hidden, ACT.Copy).then_inc(ff_hi, 1)

                unit(base)
                groups(gx, 2, a_hi, gain)
                x_squares(r, X_OUT0 + 2 if lay == 0 else X_OUT1 + 2, m_hi)
                unit(base + 1)
                hidden_relu(base + 3, lay * FF if lay else None)

                def chunk(i, peeled):
                    for r_ in range(4):
                        c = 2 + r_ + LOOK
                        if peeled:
                            unit(base + 2 + 4 * i + r_)
                        else:
                            act.wait_ge(raw_landed[(base + c) % RAW], (i * 2 + landed(base + c)) * 16)
                            act.wait_ge(unit_used, i * 4 + (base + c - RING + 2))
                            act.activation(w_hi[:, (base + c) % RING, :], raw[:, (base + c) % RAW, :], ACT.Copy)\
                               .then_inc(hi_ready, 1)
                        if r_ == 0:
                            hidden_hi(i + (lay * FF + 1), i * 4 + (base + 3))
                        if r_ == 1:
                            hidden_relu(i * 4 + (base + 5), i + (lay * FF + 1))
                with act.Fori(0, FF - 2) as i:
                    chunk(i, False)
                chunk(FF - 2, True)
                hidden_hi(lay * FF + FF, base + 2, 4)
                unit(base + 4 * FF - 2)
                unit(base + 4 * FF - 1)

            groups(G_MIX0, 2, a_hi, GAIN_MIX)
            unit(U_POOL)
            x_squares(4, X_PLE + 2, tok)
            unit(U_POOL + 1)
            block_done(U_POOL + 1)
            evac(B_POOL)
            dense(U_POOL + 2, B_POOL + 1, RUN2)
            for s in run_steps(RUN2):
                step(RUN2, s)
                fill(RUN2, s)
                if s in POOL_STEPS:
                    g = POOL_STEPS.index(s)
                    act.wait_ge(d_ready, 2 * g + 1)
                    act.activation(dT[:, g, 0, :], bank[0][0:GC, 0:S], ACT.Copy).then_inc(d_copied_a, 1)
            groups(G_TOK0, 0, b_hi)
            unit(U_OUT0)
            group(G_TOK0 + 2, b_hi, 4)
            unit(U_OUT0 + 1)
            unit(U_OUT0 + 2)
            groups(G_MLP0, 0, a_hi, GAIN_MLP)
            unit(U_OUT0 + 3)
            mlp(U_FF0, 0, 5, G_MLP0, GAIN_MLP)
            groups(G_MIX1, 0, a_hi, GAIN_MIX + 8)
            unit(U_MOBA0)
            groups(G_MIX1, 2, a_hi, GAIN_MIX + 8)
            x_squares(6, X_FF0 + 2, m_hi)
            unit(U_MOBA0 + 1)
            block_done(U_MOBA0 + 1)
            evac(B_MOBA0)
            dense(U_MOBA, B_MOBA, RUN3)
            for s in run_steps(RUN3):
                step(RUN3, s)
                fill(RUN3, s)
            unit(U_OUT1 + 1)
            unit(U_OUT1 + 2)
            groups(G_MLP1, 0, a_hi, GAIN_MLP + 8)
            unit(U_OUT1 + 3)
            mlp(U_FF1, 1, 7, G_MLP1, GAIN_MLP + 8)

        @block.vector
        def _(dve):
            link = Linker(dve, vec_chain)

            def unit(u):
                v = u + LOOK
                if v < N_UNITS:
                    split(v)

            def split(v):
                n = unit_size(v)
                dve.wait_ge(hi_ready, v + 1)
                dve.tensor_tensor(w_lo[:, v % RING, 0:n], landing[land_slot(v)][:, 0:n],
                                  w_hi[:, v % RING, 0:n].bitcast(F32), ALU.subtract).then_inc(lo_ready, 1)

            def group(g, hi, lo, k, gain=None):
                dve.wait_ge(tr_hi, g + 1)
                ps = group_bank(g)
                if gain is None:
                    dve.tensor_tensor(lo[:, k:k + 2, :], ps[:, :].rearrange("p (k n) -> p k n", k=2),
                                      hi[:, k:k + 2, :].bitcast(F32), ALU.subtract).then_inc(tr_lo, 1)
                else:
                    for q in range(2):
                        ins = dve.scalar_tensor_tensor(lo[:, k + q, :], ps[:, q * S:q * S + S],
                                                       gain_cols[:, gain + k + q:gain + k + q + 1],
                                                       hi[:, k + q, :].bitcast(F32), ALU.mult, ALU.subtract)
                    ins.then_inc(tr_lo, 1)

            def groups(g0, first, hi, lo, gain=None):
                for q in range(first, first + 2):
                    group(g0 + q, hi, lo, 2 * q, gain)

            def block_done(u):
                dve.wait_ge(unit_used, u + 2)

            def scaled(dst, k, r, n=CB):
                dve.wait_ge(rstd_done, r + 1)
                dve.tensor_scalar(dst, bank[pair_bank(k) + 1][:, 0:n], stat[:, 2, r, 1:2], None, ALU.mult)\
                   .then_inc(free_v, 1)

            def evac(k):
                kind = BLOCKS[k]
                if kind == "in":
                    c, n = IN_BLOCKS[k]
                    scaled(pj[:, 1, c:c + n], k, 0, n)
                if kind == "merge":
                    c = (k - B_MERGE) * CB
                    dve.wait_ge(free_a, freed(k, "a"))
                    dve.tensor_scalar(m_sig[:, :, c:c + CB], m_sig[:, :, c:c + CB], 0.5, 0.5, ALU.mult, ALU.add)\
                       .then_inc(merge_sig, 1)
                if kind == "brb":
                    dve.wait_ge(merge_sig, 4)
                    c = D + (k - B_BR) * CB
                    for t in range(NT):
                        g = m_sig[:, t, c:c + CB]
                        ins = dve.tensor_tensor(g, g, bank[pair_bank(k) + t][:, :], ALU.mult)
                    ins.then_inc(free_v, 1)
                if kind == "kv":
                    scaled(memkv[:, int(k == B_KV1), 1, :], k, 1)
                if kind == "pool":
                    c = (1 - (k - B_POOL)) * CB
                    scaled(h_pool[:, 1, c:c + CB], k, 4)
                if kind == "moba":
                    c = (0 if k == B_MOBA0 else k - B_MOBA + 1) * CB
                    scaled(h_moba[:, 1, c:c + CB], k, 6)

            def head_squares(what, k):
                dve.wait_ge(free_a, freed(k, "a"))
                dve.wait_ge(free_v, freed(k, "v"))
                if NORMED.index(what):
                    dve.wait_ge(head_sum, NORMED.index(what))
                sq = mem_tmp if k < B_MOBA0 else m[:, 0:2 * S]
                v = normed_heads(what)
                link(dve.tensor_tensor(sq.rearrange("p (t n d) -> p t n d", t=NT, d=HD), v, v, ALU.mult))
                dve.tensor_reduce(hstat[:, NORMED.index(what), 0, :], sq.rearrange("p (n d) -> p n d", d=HD),
                                  AX.X, ALU.add).then_inc(head_sum, 1)

            def dense(u, k):
                unit(u)
                unit(u + 1)
                block_done(u + 1)
                evac(k)

            def fill(run, s):
                for u, k, half_ in fill_of(run, s):
                    early = k == B_MOBA + 1
                    if not early:
                        unit(u)
                    if half_ and BLOCKS[k] != "merge":
                        block_done(u)
                        evac(k)
                    if early:
                        unit(u)

            def add_half(c, b, r=None):
                for t in range(NT):
                    xs = x[:, t, c * CB:c * CB + CB]
                    if r is None:
                        ins = dve.tensor_tensor(xs, xs, bank[b + t][:, :], ALU.add)
                    else:
                        ins = dve.scalar_tensor_tensor(xs, bank[b + t][:, :], stat[:, 3, r, t:t + 1], xs, ALU.mult, ALU.add)
                ins.then_inc(x_half, 1)

            def select_round(n):
                if n == 0:
                    for c in (0, P + P):
                        ins = dve.scalar_tensor_tensor(score[:, c:c + P], mask[:], FILL, score[:, c:c + P], ALU.mult, ALU.add)
                    link(ins)
                for t, c, w in ((0, 0, P), (1, P, S)):
                    ins = dve.max(top8[:, t, :], score[:, c:c + w])
                link(ins)
                for t, c, w in ((0, 0, P), (1, P, S)):
                    ins = dve.match_replace(score[:, c:c + w], top8[:, t, :], score[:, c:c + w], TAKEN)
                link(ins)
                if n == TOPK // 8 - 1:
                    dve.tensor_scalar(sel_b[:], score[:], TAKEN / 2, NEG, ALU.is_ge, ALU.mult).then_inc(sel_made, 1)

            def step(run, s):
                if 0 <= s < len(run):
                    h = run[s]
                    if isinstance(h, tuple):
                        n = h[1]
                        dve.wait_ge(idx_relu, n + 1)
                        for t, c, w in ((0, 0, P), (1, P, S)):
                            src, w_ = prob[:, n % 2, c:c + w], wis[:, t, n:n + 1]
                            if n == 0:
                                ins = dve.tensor_scalar(score[:, c:c + w], src, w_, None, ALU.mult)
                            else:
                                ins = dve.scalar_tensor_tensor(score[:, c:c + w], src, w_, score[:, c:c + w],
                                                               ALU.mult, ALU.add)
                        ins.then_inc(idx_acc, 1)
                        dve.wait_ge(idx_acc, n + 1)
                    else:
                        w0 = width0(h)
                        dve.wait_ge(s_ready, h + 1)
                        dve.tensor_reduce(mx[:, h, 0:1], b_s[h % 2][:, 0:w0], AX.X, ALU.max)
                        link(dve.tensor_reduce(mx[:, h, 1:2], b_s[h % 2][:, w0:w0 + S], AX.X, ALU.max))
                        dve.tensor_scalar(nmx[:, h, :], mx[:, h, :], -SCALE, None, ALU.mult).then_inc(max_done, 1)
                if LAG_P <= s < len(run) + LAG_P and not isinstance(run[s - LAG_P], tuple):
                    h = run[s - LAG_P]
                    w0 = width0(h)
                    dve.wait_ge(exp_done, h + 1)
                    link(dve.reciprocal(prec[:, h, :], psums[:, h, :]))
                    dve.tensor_scalar(prob[:, h % 2, 0:w0], prob[:, h % 2, 0:w0], prec[:, h, 0:1], None, ALU.mult)
                    dve.tensor_scalar(prob[:, h % 2, w0:w0 + S], prob[:, h % 2, w0:w0 + S], prec[:, h, 1:2], None,
                                      ALU.mult).then_inc(p_ready, 1)
                for what, pr in gate_parts(run, s):
                    dve.wait_ge(part_cp, PART[(what, pr)] + 1)
                    dve.scalar_tensor_tensor(gate_s[:], gated[:], 1.0, b_io[:, 0:S], ALU.add, ALU.mult)\
                       .then_inc(gate_cp, 1)
                if LAG_V <= s and not isinstance(run[s - LAG_V], tuple) and run[s - LAG_V] % 2:
                    h = run[s - LAG_V]
                    pr = h // 2
                    kt = pair_ktile(pr)
                    if HEADS[h][0] in ("fox", "dsa"):
                        dve.wait_ge(pv_done, h + 1)
                        dve.wait_ge(gate_cp, GATES.index(pr) + 1)
                        dve.scalar_tensor_tensor(gated[:], b_v[:, 0:S], 0.5, gate_s[:], ALU.mult, ALU.mult)\
                           .then_inc(pair_tmp, 1)
                        dve.wait_ge(pair_hi, pr + 1)
                        dve.tensor_tensor(b_lo[:, kt, :], gated[:], b_hi[:, kt, :].bitcast(F32), ALU.subtract)\
                           .then_inc(pair_lo, 1)
                    else:
                        dve.wait_ge(pair_hi, pr + 1)
                        dve.tensor_tensor(b_lo[:, kt, :], b_v[:, 0:S], b_hi[:, kt, :].bitcast(F32), ALU.subtract)\
                           .then_inc(pair_lo, 1)
                if 0 <= s < len(run) and not isinstance(run[s], tuple) and run[s] < TOPK // 8:
                    select_round(run[s])

            dve.sem_inc(free_v, 2)
            dve.wait_ge(gains_tr, 1)
            dve.tensor_copy(gain_cols[:, 0:8], b_t[:, 0:8]).then_inc(gains_made, 1)
            dve.wait_ge(gains_made, 1)
            group(G_H, a_hi, a_lo, 0, GAIN_PRE)
            split(0)
            group(G_H + 1, a_hi, a_lo, 2, GAIN_PRE)
            groups(G_H, 2, a_hi, a_lo, GAIN_PRE)
            split(1)
            split(2)
            dve.wait_ge(rstd_done, 1)
            with dve.Fori(0, NBLK_LOOP // 2) as i:
                for j in range(4):
                    c = j + LOOK
                    dve.wait_ge(hi_ready, i * 4 + (c + 1))
                    dve.tensor_tensor(w_lo[:, c % RING, 0:4 * CIN], landing[c % RAW_IN][:, 0:4 * CIN],
                                      w_hi[:, c % RING, 0:4 * CIN].bitcast(F32), ALU.subtract).then_inc(lo_ready, 1)
                    if j % 2:
                        dve.wait_ge(unit_used, i * 4 + (j + 2))
                        dve.tensor_scalar(proj[:, bass.ds((i * 2 + j // 2) * CIN + (DIN + IN_BLOCKS[0][0]), CIN)],
                                          bank[2 * (j // 2) + 1][:, 0:CIN], stat[:, 2, 0, 1:2], None, ALU.mult)\
                           .then_inc(free_v, 1)
            dense(2 * NBLK_LOOP, NBLK_LOOP)

            dve.wait_ge(free_a, freed(NBLK_LOOP, "a"))
            dve.wait_ge(free_v, freed(NBLK_LOOP, "v"))
            link(dve.tensor_scalar(wis[:], pj[:, :, WI:WI + 8], IDX_SCALE, None, ALU.mult))

            for s in run_steps(RUN1):
                step(RUN1, s)
                for u, k, half_ in fill_of(RUN1, s - 1):
                    if half_ and BLOCKS[k] == "merge":
                        evac(k)
                if s == 0:
                    dve.wait_ge(const_landed, 16 * N_SMALL)
                    link(dve.tensor_tensor(fgt[:, 0], pj[:, :, FB:FB + 8], bias_f[:].unsqueeze(1).to_broadcast([P, NT, 8]),
                                           ALU.add))
                    link(dve.tensor_scalar(fgt[:, 4], fgt[:, 0], -1.0, None, ALU.mult))
                    dve.tensor_tensor(fgt[:, 1], fgt[:, 0], fgt[:, 4], ALU.min).then_inc(f_abs, 1)
                    link(dve.tensor_scalar(fgt[:, 5], fgt[:, 0], 0.0, None, ALU.min))
                if s == 3:
                    dve.wait_ge(f_ln, 1)
                    dve.tensor_tensor(fgt[:, 4], fgt[:, 5], fgt[:, 3], ALU.subtract).then_inc(f_log, 1)
                if s == 3:
                    dve.tensor_copy(mask_b[:], mask[:]).then_inc(consts_made, 1)
                fill(RUN1, s)
                if s == 5:
                    dve.wait_ge(c_ready, 1)
                    dve.tensor_scalar(cT[:], b_t[0:8, 0:S], -1.0 / SCALE, None, ALU.mult)
                    dve.tensor_copy(gain_cols[:, 8:56], b_t[:, S:S + 48]).then_inc(c_made, 1)
            for c in range(2):
                cols = slice(c * CB, c * CB + CB)
                unit_ = U_BR + 2 + c
                if c:
                    unit(U_BR + 3)
                    groups(G_MERGED, 0, a_hi, a_lo)
                else:
                    unit(U_BR + 2)
                block_done(unit_)
                for t in range(NT):
                    ins = dve.tensor_tensor(tok[:, t, cols], bank[pair_bank(B_BR + 2 + c) + t][:, :], m_sig[:, t, cols],
                                            ALU.mult)
                ins.then_inc(free_v, 1)
                dve.wait_ge(free_v, freed(B_BR + 2 + c, "v"))
                dve.tensor_tensor(tok[:, :, cols], tok[:, :, cols], m_sig[:, :, D + c * CB:D + c * CB + CB], ALU.add)\
                   .then_inc(merged, 1)
            groups(G_MERGED, 2, a_hi, a_lo)
            unit(U_WO)
            unit(U_WO + 1)
            unit(U_WO + 2)
            groups(G_MEM1, 0, b_hi, b_lo, GAIN_MEM + 8)
            unit(U_WO + 3)
            groups(G_MEM1, 2, b_hi, b_lo, GAIN_MEM + 8)
            unit(U_KV1)
            group(G_P, a_hi, a_lo, 6)
            dve.wait_ge(rstd_done, 3)
            dve.wait_ge(x_again, 16)
            for c in range(2):
                cols = slice(c * CB, c * CB + CB)
                for t in range(NT):
                    ins = dve.scalar_tensor_tensor(m_hi[:, t, cols], bank[pair_bank(B_WO + c) + t][:, :],
                                                   stat[:, 2, 2, t:t + 1], gain_bc[:, cols], ALU.mult, ALU.mult)
                ins.then_inc(free_v, 1)
                dve.wait_ge(free_v, freed(B_WO + c, "v"))
                dve.tensor_tensor(x[:, :, cols], x[:, :, cols], m_hi[:, :, cols], ALU.add).then_inc(x_post, 1)

            def gated_half(c):
                cols = slice(c * CB, c * CB + CB)
                dve.wait_ge(free_a, freed(B_GATE + c, "a"))
                dve.scalar_tensor_tensor(e_tok[:, :, cols], m_hi[:, :, cols], 1.0, e_tok[:, :, cols], ALU.add, ALU.mult)\
                   .then_inc(z_made, 1)

            unit(U_KV1 + 1)
            block_done(U_KV1 + 1)
            evac(B_KV1)
            groups(G_X, 0, a_hi, a_lo)
            head_squares("memk1", B_KV1)
            unit(U_PLE)
            unit(U_GATE)
            groups(G_X, 2, a_hi, a_lo)
            unit(U_GATE + 1)
            groups(G_MEM0, 0, b_hi, b_lo, GAIN_MEM)
            gated_half(0)
            unit(U_GATE + 2)
            unit(U_GATE + 3)
            groups(G_MEM0, 2, b_hi, b_lo, GAIN_MEM)
            gated_half(1)
            dve.wait_ge(z_made, 2)
            dve.wait_ge(bc_landed, 16)
            for t in range(NT):
                ins = dve.tensor_tensor(tok[:, t, :], e_tok[:, t, :], gain_bc[:], ALU.mult)
            link(ins)
            dve.wait_ge(rstd_done, 4)
            for c in range(2):
                cols = slice(c * CB, c * CB + CB)
                for t in range(NT):
                    ins = dve.scalar_tensor_tensor(x[:, t, cols], tok[:, t, cols], stat[:, 2, 3, t:t + 1], x[:, t, cols],
                                                   ALU.mult, ALU.add)
                ins.then_inc(x_half, 1)
            unit(U_KV0)
            groups(G_MIX0, 0, a_hi, a_lo, GAIN_MIX)
            unit(U_KV0 + 1)
            block_done(U_KV0 + 1)
            evac(B_KV0)
            head_squares("memk0", B_KV0)

            def mlp(base, lay, gx, gain):
                def hidden_square(n):
                    dve.wait_ge(ff_relu, n * 4)
                    dve.tensor_tensor(hidden, hidden, hidden, ALU.mult).then_inc(ff_sq, 1)

                def hidden_lo(n, k=0):
                    dve.wait_ge(ff_hi, n)
                    dve.tensor_tensor(b_lo[:, k:k + 4, :], hidden, b_hi[:, k:k + 4, :].bitcast(F32), ALU.subtract)\
                       .then_inc(ff_lo, 1)
                groups(gx, 2, a_hi, a_lo, gain)
                unit(base)
                unit(base + 1)
                hidden_square(lay * FF + 1)

                def chunk(i, peeled):
                    for r in range(4):
                        c = 2 + r + LOOK
                        if peeled:
                            unit(base + 2 + 4 * i + r)
                        else:
                            dve.wait_ge(hi_ready, i * 4 + (base + c + 1))
                            dve.tensor_tensor(w_lo[:, (base + c) % RING, :], raw[:, (base + c) % RAW, :],
                                              w_hi[:, (base + c) % RING, :].bitcast(F32), ALU.subtract).then_inc(lo_ready, 1)
                        if r == 0:
                            hidden_lo(i + (lay * FF + 1))
                        if r == 1:
                            hidden_square(i + (lay * FF + 2))
                with dve.Fori(0, FF - 2) as i:
                    chunk(i, False)
                chunk(FF - 2, True)
                hidden_lo(lay * FF + FF, 4)
                dve.wait_ge(rstd_sq, lay + 1)
                unit(base + 4 * FF - 2)
                block_done(base + 4 * FF - 2)
                add_half(0, 0, 5 + 2 * lay)
                unit(base + 4 * FF - 1)

            def out_projection(u, k, gx, gain, filled=False):
                if not filled:
                    unit(u)
                unit(u + 1)
                block_done(u + 1)
                add_half(0, pair_bank(k))
                unit(u + 2)
                groups(gx, 0, a_hi, a_lo, gain)
                unit(u + 3)
                block_done(u + 3)
                add_half(1, pair_bank(k + 1))

            groups(G_MIX0, 2, a_hi, a_lo, GAIN_MIX)
            unit(U_POOL)
            unit(U_POOL + 1)
            block_done(U_POOL + 1)
            evac(B_POOL)
            head_squares("memq0", B_POOL)
            dense(U_POOL + 2, B_POOL + 1)
            for s in run_steps(RUN2):
                step(RUN2, s)
                fill(RUN2, s)
                if s in POOL_STEPS:
                    g = POOL_STEPS.index(s)
                    dve.wait_ge(d_ready, 2 * g + 2)
                    dve.tensor_copy(dT[:, g, 1, :], bank[1][0:GC, 0:S]).then_inc(d_copied_v, 1)
            dve.wait_ge(pool_landed, 16 * 7)
            for q in range(2):
                cols = slice(q * 2 * GW, q * 2 * GW + 2 * GW)
                dve.wait_ge(y_ready, q + 1)
                for t in range(NT):
                    ins = dve.tensor_tensor(tok[:, t, cols], bank[2 - 2 * q + t][:, 0:2 * GW], gain_bc[:, cols], ALU.mult)
                ins.then_inc(y_made, 1)
                group(G_TOK0 + q, b_hi, b_lo, 2 * q)
            group(G_TOK0 + 2, b_hi, b_lo, 4)
            out_projection(U_OUT0, B_OUT0, G_MLP0, GAIN_MLP)
            mlp(U_FF0, 0, G_MLP0, GAIN_MLP)
            groups(G_MIX1, 0, a_hi, a_lo, GAIN_MIX + 8)
            block_done(U_MOBA0 - 1)
            add_half(1, 2, 5)
            groups(G_MIX1, 2, a_hi, a_lo, GAIN_MIX + 8)
            unit(U_MOBA0)
            unit(U_MOBA0 + 1)
            block_done(U_MOBA0 + 1)
            evac(B_MOBA0)
            head_squares("memq1", B_MOBA0)
            head_squares("q0", B_MOBA0)
            dense(U_MOBA, B_MOBA)
            head_squares("k0", B_MOBA)
            for s in run_steps(RUN3):
                step(RUN3, s)
                if s in SQUARES_AT:
                    head_squares(*SQUARES_AT[s])
                fill(RUN3, s)
            out_projection(U_OUT1, B_OUT1, G_MLP1, GAIN_MLP + 8, filled=True)
            mlp(U_FF1, 1, G_MLP1, GAIN_MLP + 8)
            for t in range(NT):
                dve.wait_ge(tile_done, t + 1)
                xs = x[:, t, CB:D]
                dve.scalar_tensor_tensor(xs, bank[2 + t][:, :], stat[:, 3, 7, t:t + 1], xs, ALU.mult, ALU.add)\
                   .then_inc(x_tile, 1)

        @block.tensor
        def _(pe):
            def product(u, slot, hi, lo, k0, banks, first, last, n=CB, kts=4, col=0, used=True, mid=()):
                pe.wait_ge(lo_ready, u + 1)
                pitch = n if kts == 4 else D
                for k in range(kts):
                    if k in mid:
                        mid[k]()
                    w = slice(k * pitch + col, k * pitch + col + n)
                    for t in range(NT):
                        ts = slice(t * P, t * P + P)
                        for q, (xa, wa) in enumerate(((hi, w_hi), (hi, w_lo), (lo, w_hi))):
                            ins = pe.matmul(banks[t][:, 0:n], xa[:, k0 + k, ts], wa[:, slot, w],
                                            start=first and k == 0 and q == 0, stop=last and k == kts - 1 and q == 2)
                if used:
                    ins.then_inc(unit_used, 1)
                return ins

            def product_by_tiles(u, hi, lo, k0, banks):
                pe.wait_ge(lo_ready, u + 1)
                for t in range(NT):
                    ts = slice(t * P, t * P + P)
                    for k in range(4):
                        w = slice(k * CB, k * CB + CB)
                        for q, (xa, wa) in enumerate(((hi, w_hi), (hi, w_lo), (lo, w_hi))):
                            ins = pe.matmul(banks[t][:, :], xa[:, k0 + k, ts], wa[:, u % RING, w],
                                            start=False, stop=k == 3 and q == 2)
                    ins.then_inc(tile_done, 1)

            def product_by_terms(u, hi, lo, k0, banks, n):
                pe.wait_ge(hi_ready, u + 1)
                for q, (xa, wa, split_of_x) in enumerate(((hi, w_hi, tr_hi), (lo, w_hi, tr_lo), (hi, w_lo, None))):
                    if q == 2:
                        pe.wait_ge(lo_ready, u + 1)
                    for k in range(4):
                        if split_of_x is not None and k % 2 == 0:
                            pe.wait_ge(split_of_x, G_H + (k0 + k) // 2 + 1)
                        for t in range(NT):
                            ins = pe.matmul(banks[t][:, 0:n], xa[:, k0 + k, t * P:t * P + P], wa[:, u, k * n:k * n + n],
                                            start=k0 + k + q == 0, stop=k0 + k == D // P - 1 and q == 2)
                ins.then_inc(unit_used, 1)

            def blocks_read(k):
                pe.wait_ge(free_a, freed(k, "a"))
                pe.wait_ge(free_v, freed(k, "v"))

            def banks_free(k):
                before = [j for j in range(k) if pair_bank(j) == pair_bank(k)]
                blocks_read(before[-1] if before else -1)

            def banks_of(k):
                return bank[pair_bank(k):pair_bank(k) + 2]

            def dense(u0, k, hi, lo, mids=((), ())):
                banks_free(k)
                n = IN_BLOCKS[k][1] if BLOCKS[k] == "in" else CB
                for r in range(2):
                    product(u0 + r, (u0 + r) % RING, hi, lo, 4 * r, banks_of(k), r == 0, r == 1, n, mid=mids[r])

            def group(g, src, k):
                if g >= 4:
                    pe.wait_ge(tr_lo, g - 1)
                ps = group_bank(g)
                for kk in range(2):
                    for t in range(NT):
                        ins = pe.transpose(ps[:, kk * S + t * P:kk * S + t * P + P],
                                           src[:, t, (k + kk) * P:(k + kk) * P + P], ident[:])
                ins.then_inc(tr_ready, 1)

            def groups(g0, src, q, ready, count):
                def work():
                    pe.wait_ge(ready, count)
                    group(g0 + (0 if g0 == G_P else q), src, 2 * q if g0 != G_P else 0)
                return work

            def split_by(g0, q):
                return lambda: pe.wait_ge(tr_lo, g0 + q + 1)

            def both(*works):
                def work():
                    for w in works:
                        w()
                return work

            def lower(g0, src, ready, count):
                return {2: groups(g0, src, 0, ready, count), 3: groups(g0, src, 1, ready, count)}

            def upper(g0, src, ready, count):
                return ({0: split_by(g0, 0), 2: both(split_by(g0, 1), groups(g0, src, 2, ready, count)),
                         3: groups(g0, src, 3, ready, count)},
                        {0: split_by(g0, 2), 2: split_by(g0, 3)})

            def part(what, pr):
                n = PART[(what, pr)]
                if n:
                    pe.wait_ge(part_cp, n)
                before = PARTS[n - 1] if n else None
                if before and before[0] == "gate":
                    pe.wait_ge(gate_cp, GATES.index(before[1]) + 1)
                if what in ("ki", "qi"):
                    pe.wait_ge(rope_idx, 1)
                elif what == "ka":
                    pe.wait_ge(rope_dsa, 1)
                else:
                    kind, j = HEADS[2 * pr]
                    if what == "gate":
                        blocks_read(5 if kind == "fox" else 8)
                    if kind == "dsa" and what == "q":
                        pe.wait_ge(rope_dsa, 1)
                    if kind == "moba":
                        pe.wait_ge(moba_made, 2 * (j // 4) + (1 if what == "q" else 2))
                    if kind[:3] == "mem":
                        pe.wait_ge(memq_made if what == "q" else memk_made, 2 * int(kind[3]) + j // 2 + 1 if what == "q" else 2)
                for t in range(NT):
                    if what in ("ki", "ka"):
                        src = k_twice[:, t].rearrange("p q d -> p (q d)")
                    elif what == "qi":
                        src = pj[:, t, QI + P * pr:QI + P * pr + P]
                    else:
                        src = head_cols(2 * pr)[what][:, t]
                    ins = pe.transpose(b_io[:, t * P:t * P + P], src, ident[:])
                ins.then_inc(part_tr, 1)

            def first_parts(run, k):
                q_part, k_part = parts_at(run, -1)
                return {2: both(lambda: blocks_read(k), lambda: part(*q_part)), 3: lambda: part(*k_part)}

            def logits(ps, q, k, w0, stop):
                pe.matmul(ps[:, 0:w0], q[:, 0:P], k[:, 0:w0], start=True, stop=stop)
                return pe.matmul(ps[:, w0:w0 + S], q[:, P:S], k[:, 0:S], start=True, stop=stop)

            def step(run, s):
                for what in heads_parts(run, s):
                    part(*what)
                if 0 <= s < len(run):
                    h = run[s]
                    if isinstance(h, tuple):
                        n = h[1]
                        rows = slice(HD * (n % 2), HD * (n % 2) + HD)
                        pe.wait_ge(part_cp, PART[("qi", n // 2)] + 1)
                        pe.wait_ge(part_cp, PART[("ki", 0)] + 1)
                        if n >= 2:
                            pe.wait_ge(idx_relu, n - 1)
                        logits(b_s[n % 2], qk[rows, PART_SLOT[("qi", n // 2)], 0], kT[rows], P, True).then_inc(idx_s, 1)
                    else:
                        kind, j = HEADS[h]
                        rows = slice(HD * (h % 2), HD * (h % 2) + HD)
                        slot = PART_SLOT[("q", h // 2)]
                        pe.wait_ge(part_cp, PART[("q", h // 2)] + 1)
                        pe.wait_ge(part_cp, PART[("ka", 0) if kind == "dsa" else ("k", h // 2)] + 1)
                        if h < 2:
                            pe.wait_ge(idx_relu, 7 + h)
                        else:
                            pe.wait_ge(exp_done, h - 1)
                        k = kT[rows] if kind == "dsa" else qk[rows, slot, 1]
                        ps, w0 = b_s[h % 2], width0(h)
                        free = kind[:3] == "mem"
                        for t, c, w in ((0, 0, w0), (1, w0, S)):
                            ins = pe.matmul(ps[:, c:c + w], qk[rows, slot, 0, t * P:t * P + P], k[:, 0:w],
                                            start=True, stop=free)
                            if kind == "fox":
                                pe.wait_ge(c_made, 1)
                                pe.matmul(ps[:, c:c + w], ident[0:8, j:j + 1].to_broadcast([8, P]), cT[:, 0:w],
                                          start=False, stop=False)
                            if kind == "dsa":
                                pe.wait_ge(ident_made, 1)
                                pe.wait_ge(sel_made, 1)
                                pe.matmul(ps[:, c:c + w], ident_b[:], sel_b[:, c:c + w], start=False, stop=False)
                            if not free:
                                pe.wait_ge(ident_made, 1)
                                pe.wait_ge(consts_made, 1)
                                ins = pe.matmul(ps[:, c + w - P:c + w], ident_b[:], mask_b[:], start=False, stop=True)
                        ins.then_inc(s_ready, 1)
                if LAG_T <= s < len(run) + LAG_T and not isinstance(run[s - LAG_T], tuple):
                    h = run[s - LAG_T]
                    w0 = width0(h)
                    pe.wait_ge(p_ready, h + 1)
                    if h:
                        pe.wait_ge(pt_copied, h)
                    pr = prob[:, h % 2]
                    cuts = [0, w0] + ([P, w0 + P] if w0 == S else [w0 + P])
                    for q, c in enumerate(cuts):
                        ins = pe.transpose(b_t[:, q * P:q * P + P], pr[:, c:c + P], ident[:])
                    ins.then_inc(pt_ready, 1)
                for what in gate_parts(run, s):
                    part(*what)
                if LAG_V <= s and not isinstance(run[s - LAG_V], tuple):
                    h = run[s - LAG_V]
                    kind, j = HEADS[h]
                    rows = slice(HD * (h % 2), HD * (h % 2) + HD)
                    v, pT = head_cols(h)["v"], probT[:, h % 2]
                    if kind == "moba":
                        blocks_read(B_MOBA + (0, 2, 3)[j // 4])
                    pe.wait_ge(pt_copied, h + 1)
                    if h % 2 == 0 and h:
                        pe.wait_ge(pair_lo, h // 2)
                    pe.matmul(b_v[rows, 0:S], v[:, 0], pT[:, 0:S], start=True, stop=False)
                    c = S if width0(h) == S else P
                    pe.matmul(b_v[rows, S - c:S], v[:, 1], pT[:, S:S + c], start=False, stop=True)\
                      .then_inc(pv_done, 1)

            def fill(run, s):
                for u, k, half_ in fill_of(run, s):
                    kind = BLOCKS[k]
                    if half_ != 1:
                        banks_free(k)
                    if kind in ("brb", "out"):
                        pe.wait_ge(pair_lo, 4 if kind == "brb" else 16)
                    hi, lo = (b_hi, b_lo) if kind in ("brb", "out") else (a_hi, a_lo)
                    n = IN_BLOCKS[k][1] if kind == "in" else CB
                    product(u, u % RING, hi, lo, 4 if half_ else 0, banks_of(k), half_ != 1, half_ != 0, n)

            pe.sem_inc(unit_used, 1)
            pe.wait_ge(early_landed, 16 * N_EARLY)
            pe.transpose(b_t[:, 0:8], pre_rows, ident[0:8, 0:8]).then_inc(gains_tr, 1)
            pe.wait_ge(x_landed, 16 * NT)
            for g in range(4):
                group(G_H + g, x, 2 * g)
            pe.wait_ge(gains_made, 1)
            def in_pair(i, by_terms):
                for r in range(2):
                    pe.wait_ge(free_a, i * 2 + (r + 1))
                    pe.wait_ge(free_v, i * 2 + (r + 1))
                    for half_ in range(2):
                        j = 2 * r + half_
                        if j < by_terms:
                            product_by_terms(j, a_hi, a_lo, 4 * half_, bank[2 * r:2 * r + 2], CIN)
                        else:
                            product(i * 4 + j, j, a_hi, a_lo, 4 * half_, bank[2 * r:2 * r + 2], half_ == 0, half_ == 1, CIN)

            in_pair(0, 2)
            with pe.Fori(1, NBLK_LOOP // 2) as i:
                in_pair(i, 0)
            pe.wait_ge(const_landed, 16 * N_SMALL)
            dense(2 * NBLK_LOOP, NBLK_LOOP, a_hi, a_lo, ((), first_parts(RUN1, NBLK_LOOP - 1)))

            for s in run_steps(RUN1):
                step(RUN1, s)
                fill(RUN1, s)
                if s == 5:
                    pe.wait_ge(f_log, 1)
                    pe.matmul(b_t[0:8, 0:S], fgt[:, 4, 0], tri[:], start=True, stop=False)
                    pe.matmul(b_t[0:8, P:S], fgt[:, 4, 1], tri[:, 0:P], start=False, stop=True)
                    pe.transpose(b_t[:, S:S + 48], gain_rows, ident[0:48, 0:48]).then_inc(c_ready, 1)
            pe.wait_ge(pair_lo, 8)
            for c in range(2):
                k, u = B_BR + 2 + c, U_BR + 2 + c
                banks_free(k)
                product(u, u % RING, b_hi, b_lo, 0, banks_of(k), True, True, mid=lower(G_MERGED, tok, merged, 1) if c else ())
            dense(U_WO, B_WO, a_hi, a_lo, upper(G_MERGED, tok, merged, 2))
            dense(U_WO + 2, B_WO + 1, a_hi, a_lo, tuple({1: groups(G_MEM1, tok, 2 * r, mem_landed, 16),
                                                         3: groups(G_MEM1, tok, 2 * r + 1, mem_landed, 16)} for r in range(2)))
            dense(U_KV1, B_KV1, b_hi, b_lo, ({0: split_by(G_MEM1, 1), 2: groups(G_P, p_tok, 3, p_landed, 16)},
                                             {0: split_by(G_MEM1, 3)}))
            pe.wait_ge(tr_lo, G_P + 1)
            for c in range(2):
                banks_free(B_PLE + c)
                product(U_PLE, U_PLE % RING, a_hi, a_lo, 6, banks_of(B_PLE + c), True, True, CB, 2, c * CB, used=False,
                        mid={1 - c: groups(G_X, x, c, x_post, 1)})\
                    .then_inc(ple_block, 1)
            pe.wait_ge(ple_block, 2)
            pe.sem_inc(unit_used, 1)
            mids = upper(G_X, x, x_post, 2)
            mids[1][1] = groups(G_MEM0, tok, 0, mem_landed, 16)
            mids[1][3] = groups(G_MEM0, tok, 1, mem_landed, 16)
            dense(U_GATE, B_GATE, a_hi, a_lo, mids)
            dense(U_GATE + 2, B_GATE + 1, a_hi, a_lo, ((), {0: groups(G_MEM0, tok, 2, mem_landed, 16),
                                                            2: groups(G_MEM0, tok, 3, mem_landed, 16)}))
            pe.wait_ge(tr_lo, G_MEM0 + 4)
            dense(U_KV0, B_KV0, b_hi, b_lo, ((), {1: groups(G_MIX0, x, 0, x_half, X_PLE + 1),
                                                  2: groups(G_MIX0, x, 1, x_half, X_PLE + 1)}))

            def mlp(base, lay, gx, x_before, after):
                def up(u, half_, slot, mid=(), read=None):
                    pe.wait_ge(lo_ready, u + 1)
                    for k in range(4):
                        if k in mid:
                            mid[k]()
                        for f in range(4):
                            w = slice(k * CB + f * P, k * CB + f * P + P)
                            if read is not None and k == 0:
                                pe.wait_ge(ff_relu, read + (f + 1))
                            for q, (wa, xa) in enumerate(((w_hi, a_hi), (w_hi, a_lo), (w_lo, a_hi))):
                                ins = pe.matmul(b_hid[f][:, 0:S], wa[:, slot, w], xa[:, 4 * half_ + k, :],
                                                start=half_ + k + q == 0, stop=half_ == 1 and k == 3 and q == 2)
                    ins.then_inc(unit_used, 1)
                mids = upper(gx, x, x_half, x_before + 2)
                mids[0][0] = split_by(gx, 1)
                up(base, 0, base % RING, mids[0])
                up(base + 1, 1, (base + 1) % RING, mids[1])

                def chunk(i, first, last):
                    s = [(base + 2 + r) % RING for r in range(4)]
                    if not last:
                        up(i * 4 + (base + 2), 0, s[0], read=i * 4 + 4 * lay * FF)
                        up(i * 4 + (base + 3), 1, s[1])
                    pe.wait_ge(ff_lo, i + (lay * FF + 1))
                    for c in range(2):
                        if last and c and base == U_FF1:
                            product_by_tiles(N_UNITS - 1, b_hi, b_lo, 4, bank[2:4])
                            continue
                        u, slot = (base + 4 * FF - 2 + c, (base + 4 * FF - 2 + c) % RING) if last else (i * 4 + (base + 4 + c), s[2 + c])
                        product(u, slot, b_hi, b_lo, 4 if last else 0, bank[2 * c:2 * c + 2], first, last,
                                mid=after if last and c else ())
                chunk(0, True, False)
                with pe.Fori(1, FF - 1) as i:
                    chunk(i, False, False)
                chunk(FF - 1, False, True)

            dense(U_POOL, B_POOL, a_hi, a_lo, upper(G_MIX0, x, x_half, X_PLE + 2))
            dense(U_POOL + 2, B_POOL + 1, a_hi, a_lo, ((), first_parts(RUN2, B_POOL)))
            def pooled(g):
                for c in range(2):
                    if g:
                        pe.wait_ge(d_copied_v if c else d_copied_a, g)
                    cols = slice(g * GW + c * GC, g * GW + c * GC + GC)
                    pe.matmul(bank[c][0:GC, 0:S], h_pool[:, 0, cols], band[:, 0, g], start=True, stop=False)
                    pe.matmul(bank[c][0:GC, P:S], h_pool[:, 1, cols], band[:, 1, g, P:S], start=False, stop=True)\
                      .then_inc(d_ready, 1)

            def mixed(g):
                for t in range(NT):
                    for c in range(2):
                        ins = pe.matmul(bank[2 - 2 * (g // 2) + t][:, g % 2 * GW:g % 2 * GW + GW], dT[:, g, c, t * P:t * P + P],
                                        w_group[:, g, c], start=c == 0, stop=c == 1)
                if g % 2:
                    ins.then_inc(y_ready, 1)

            for s in run_steps(RUN2):
                step(RUN2, s)
                fill(RUN2, s)
                if s == POOL_STEPS[0]:
                    blocks_read(B_POOL + 1)
                    pe.wait_ge(pool_landed, 16 * 7)
                if s in POOL_STEPS:
                    pooled(POOL_STEPS.index(s))
            pe.wait_ge(pt_copied, 20)
            pe.wait_ge(part_cp, PART[("k", 9)] + 1)
            for q in range(2):
                pe.wait_ge(d_copied_a, 2 + 2 * q)
                pe.wait_ge(d_copied_v, 2 + 2 * q)
                mixed(2 * q)
                if q:
                    pe.wait_ge(pair_lo, 10)
                    groups(G_TOK0, tok, 0, y_made, 1)()
                mixed(2 * q + 1)
            dense(U_OUT0, B_OUT0, b_hi, b_lo,
                  ({0: split_by(G_TOK0, 0), 1: groups(G_TOK0, tok, 1, y_made, 2),
                    2: both(groups(G_TOK0, tok, 2, y_made, 2), split_by(G_TOK0, 1))},
                   {0: split_by(G_TOK0, 2)}))
            dense(U_OUT0 + 2, B_OUT0 + 1, b_hi, b_lo, (lower(G_MLP0, x, x_half, X_OUT0 + 1), ()))
            mlp(U_FF0, 0, G_MLP0, X_OUT0, lower(G_MIX1, x, x_half, X_FF0 + 1))
            dense(U_MOBA0, B_MOBA0, a_hi, a_lo, upper(G_MIX1, x, x_half, X_FF0 + 2))
            dense(U_MOBA, B_MOBA, a_hi, a_lo, ((), first_parts(RUN3, B_POOL + 1)))
            for s in run_steps(RUN3):
                step(RUN3, s)
                fill(RUN3, s)
            pe.wait_ge(pair_lo, N_HEADS // 2)
            u = U_OUT1 + 1
            product(u, u % RING, b_hi, b_lo, 4, banks_of(B_OUT1), False, True)
            dense(U_OUT1 + 2, B_OUT1 + 1, b_hi, b_lo, (lower(G_MLP1, x, x_half, X_OUT1 + 1), ()))
            mlp(U_FF1, 1, G_MLP1, X_OUT1, ())


_CONSTANTS = ["c_ident", "c_mask", "c_tri", "c_rope_a", "c_rope_m", "c_band"]
_INS = ["x", "p", "w_in", "b_forget", "w_branch_a", "w_branch_b", "w_merge", "w_out", "g_pre", "g_post", "w_ple",
        "w_ple_gate", "g_ple", "mem_2", "g_mix_2", "g_mem_2", "g_mlp_2", "w_in_pool_2", "w_pool_group_2", "pool_scale_2",
        "w_in_moba_2", "moba_q_gain_2", "moba_k_gain_2", "w_mem_kv_2", "mem_q_gain_2", "mem_k_gain_2", "w_out_2",
        "w_ff1_2", "w_ff2_2"]


def constants():
    f = np.float32
    pos = np.arange(S, dtype=f)[:, None]
    ang_a = pos * (f(500000.0) ** (-np.arange(8, dtype=f) / f(8)))[None, :]
    ang_m = pos * (f(10000.0) ** (-np.arange(0, HD, 2, dtype=f) / f(HD)))[None, :]
    q, k = np.arange(P)[:, None], np.arange(P)[None, :]
    tri = np.concatenate([(q <= k), np.ones((P, P), bool)], axis=1)
    t = np.arange(S)[None, :]
    s = np.arange(S)[:, None]
    band = np.stack([((s <= t) & (s > t - w)) / np.minimum(t + 1, w) - (s == t) for w in (2, 4, 8, 16)])
    return {
        "c_ident": np.eye(P, dtype=f),
        "c_mask": np.where(k <= q, 0.0, NEG).astype(f),
        "c_tri": tri.astype(f),
        "c_rope_a": np.stack([np.cos(ang_a), np.sin(ang_a)]).astype(f),
        "c_rope_m": np.stack([np.cos(ang_m), np.sin(ang_m)]).astype(f),
        "c_band": band.astype(f),
    }


def kernel(**inputs):
    from concourse import bacc
    from concourse.bass_utils import run_bass_kernel_spmd

    nc = bacc.Bacc("TRN2", target_bir_lowering=False, num_devices=1)
    arrays, args = {}, {}
    for name, value in [(n, inputs[n]) for n in _INS] + list(constants().items()):
        value = np.ascontiguousarray(value)
        arrays[f"in_{name}"] = value
        args[name] = nc.dram_tensor(f"in_{name}", value.shape, mybir.dt.from_np(value.dtype), kind="ExternalInput").ap()
    out = nc.dram_tensor("out_x", (1, S, D), F32, kind="ExternalOutput").ap()
    build(nc, args, out)
    r = run_bass_kernel_spmd(nc, [arrays], core_ids=[0])
    return r.results[0]["out_x"]
```
